# Optimizing a Trainium2 kernel written in Bass

```python
import math
import jax, jax.numpy as jnp
from jax import lax
import numpy as np

D_MODEL = 1024
BATCH = 1
SEQ = 512
DEPTH = 1

HEAD_DIM = 64
D_ATTN = D_MODEL // 2
D_RWKV = D_MODEL - D_ATTN
D_MIX = D_ATTN + D_RWKV
N_ATTN_HEADS = D_ATTN // HEAD_DIM
N_RWKV_HEADS = D_RWKV // HEAD_DIM
DILATED_BRANCHES = ((128, 1), (512, 4), (2048, 16))
Q_BLOCK = 128
LORA_DECAY = 32
LORA_AAA = 32
LORA_MV = 32
LORA_GATE = 96
D_FF = 4 * D_MODEL
NORM_EPS = 1e-6
GN_EPS = 64e-5
N_SHIFT = 3 * D_RWKV + LORA_DECAY + LORA_AAA + LORA_GATE
N_COLS_FIRST = 3 * D_ATTN + N_SHIFT
N_COLS_REST = N_COLS_FIRST + LORA_MV


def _rms_norm(x, g):
    xf = x.astype(jnp.float32)
    y = xf * lax.rsqrt(jnp.mean(xf * xf, axis=-1, keepdims=True) + NORM_EPS)
    return (y * g.astype(jnp.float32)).astype(x.dtype)

def _token_shift(z, mu):
    prev = jnp.pad(z, ((0, 0), (1, 0), (0, 0)))[:, :-1]
    return z + (prev - z) * mu

def _dilated_branch(q, k, v, window, dilation):
    B, S, H, Dh = q.shape
    L = S // dilation
    K = window // dilation
    qb = math.gcd(L, Q_BLOCK)
    nb = L // qb

    def phase(t):
        return t.reshape(B, L, dilation, H, Dh).transpose(0, 2, 3, 1, 4)

    qs, ks, vs = phase(q), phase(k), phase(v)
    pad = ((0, 0), (0, 0), (0, 0), (K, 0), (0, 0))
    kp, vp = jnp.pad(ks, pad), jnp.pad(vs, pad)
    idx = jnp.arange(nb)[:, None] * qb + jnp.arange(qb + K)[None, :]
    kb = kp[:, :, :, idx, :]
    vb = vp[:, :, :, idx, :]
    qblk = qs.reshape(B, dilation, H, nb, qb, Dh)
    s = jnp.einsum('bdhnqc,bdhnkc->bdhnqk', qblk, kb) * (1.0 / math.sqrt(Dh))
    j = jnp.arange(qb)[:, None]
    m_idx = jnp.arange(qb + K)[None, :]
    dist = j + K - m_idx
    blk = jnp.arange(nb)[:, None, None]
    valid = (dist >= 0) & (dist <= K) & (blk * qb + m_idx - K >= 0)
    s = jnp.where(valid, s, -jnp.inf)
    m = jnp.max(s, axis=-1)
    p = jnp.exp(s - m[..., None])
    l = jnp.sum(p, axis=-1)
    acc = jnp.einsum('bdhnqk,bdhnkc->bdhnqc', p, vb)
    acc = acc.reshape(B, dilation, H, L, Dh).transpose(0, 3, 1, 2, 4).reshape(B, S, H, Dh)
    m = m.reshape(B, dilation, H, L).transpose(0, 3, 1, 2).reshape(B, S, H)
    l = l.reshape(B, dilation, H, L).transpose(0, 3, 1, 2).reshape(B, S, H)
    return m, l, acc

def _dilated_attention(q, k, v):
    B, S, _ = q.shape
    heads = lambda t: t.astype(jnp.float32).reshape(B, S, N_ATTN_HEADS, HEAD_DIM)
    qh, kh, vh = heads(q), heads(k), heads(v)
    outs = [_dilated_branch(qh, kh, vh, w, d) for (w, d) in DILATED_BRANCHES]
    m_all = jnp.maximum(jnp.maximum(outs[0][0], outs[1][0]), outs[2][0])
    num = sum(jnp.exp(m - m_all)[..., None] * acc for (m, l, acc) in outs)
    den = sum(jnp.exp(m - m_all) * l for (m, l, acc) in outs)
    o = num / den[..., None]
    return o.reshape(B, S, D_ATTN).astype(q.dtype)

def _rwkv7_scan(r, w, k, v, kk, b):
    B, S, H, N = r.shape

    def step(state, inp):
        r_t, w_t, k_t, v_t, kk_t, b_t = inp
        sa = jnp.einsum('bhij,bhj->bhi', state, kk_t)
        state = (state * w_t[:, :, None, :]
                 - sa[..., None] * b_t[:, :, None, :]
                 + v_t[..., None] * k_t[:, :, None, :])
        y = jnp.einsum('bhij,bhj->bhi', state, r_t)
        return state, y

    xs = tuple(jnp.moveaxis(t, 1, 0) for t in (r, w, k, v, kk, b))
    state0 = jnp.zeros((B, H, N, N), jnp.float32)
    _, ys = lax.scan(step, state0, xs)
    return jnp.moveaxis(ys, 0, 1)

def _rwkv7(r, k, v, xw, xa, xg, w0, w_up, a0, a_up, g_up, k_k, k_a, r_k, gn_w, gn_b):
    B, S, _ = r.shape
    H, N = N_RWKV_HEADS, HEAD_DIM
    f32 = jnp.float32
    heads = lambda t: t.astype(f32).reshape(B, S, H, N)
    logw = -jax.nn.softplus(-(w0 + jnp.tanh(xw) @ w_up).astype(f32)) - 0.5
    decay = jnp.exp(-jnp.exp(logw))
    a = jax.nn.sigmoid((a0 + xa @ a_up).astype(f32))
    g = (jax.nn.sigmoid(xg) @ g_up).astype(f32)
    kk = heads(k * k_k)
    kk = kk / jnp.maximum(jnp.sqrt(jnp.sum(kk * kk, axis=-1, keepdims=True)), 1e-12)
    k_mod = k.astype(f32) * (1.0 + (a - 1.0) * k_a.astype(f32))
    rh, kh, vh, ah, wh = heads(r), heads(k_mod), heads(v), heads(a), heads(decay)
    y = _rwkv7_scan(rh, wh, kh, vh, kk, kk * ah)
    mean = jnp.mean(y, axis=-1, keepdims=True)
    var = jnp.mean(jnp.square(y - mean), axis=-1, keepdims=True)
    yn = ((y - mean) * lax.rsqrt(var + GN_EPS)).reshape(B, S, D_RWKV)
    yn = yn * gn_w.astype(f32) + gn_b.astype(f32)
    bonus = jnp.sum(rh * kh * r_k.astype(f32), axis=-1, keepdims=True) * vh
    out = (yn + bonus.reshape(B, S, D_RWKV)) * g
    return out.astype(r.dtype)

def first_inputs(seed: int = 0) -> dict:
    key = jax.random.key(seed)
    ks = iter(jax.random.split(key, 40))
    f32 = jnp.float32
    nrm = lambda shape, scale: jax.random.normal(next(ks), shape, f32) * scale
    gain = lambda shape: 1.0 + nrm(shape, 0.05)
    L1 = DEPTH - 1
    return {
        "x": nrm((BATCH, SEQ, D_MODEL), 1.0),
        "norm_mix_pre": gain((DEPTH, D_MODEL)),
        "norm_mix_post": gain((DEPTH, D_MODEL)),
        "norm_ffn_pre": gain((DEPTH, D_MODEL)),
        "norm_ffn_post": gain((DEPTH, D_MODEL)),
        "w_in_first": nrm((D_MODEL, N_COLS_FIRST), D_MODEL ** -0.5),
        "w_in_rest": nrm((L1, D_MODEL, N_COLS_REST), D_MODEL ** -0.5),
        "mu_shift": jax.random.uniform(next(ks), (DEPTH, N_SHIFT), f32),
        "mu_shift_mv": jax.random.uniform(next(ks), (L1, LORA_MV), f32),
        "attn_out_gain": gain((DEPTH, D_ATTN)),
        "decay_w0": jax.random.uniform(next(ks), (DEPTH, D_RWKV), f32, -5.0, 0.0),
        "decay_up": nrm((DEPTH, LORA_DECAY, D_RWKV), 0.5 * LORA_DECAY ** -0.5),
        "aaa_a0": nrm((DEPTH, D_RWKV), 0.1),
        "aaa_up": nrm((DEPTH, LORA_AAA, D_RWKV), 0.5 * LORA_AAA ** -0.5),
        "mv_v0": nrm((L1, D_RWKV), 0.5),
        "mv_up": nrm((L1, LORA_MV, D_RWKV), 0.5 * LORA_MV ** -0.5),
        "gate_up": nrm((DEPTH, LORA_GATE, D_RWKV), LORA_GATE ** -0.5),
        "k_k": 0.85 + nrm((DEPTH, D_RWKV), 0.1),
        "k_a": 1.0 + nrm((DEPTH, D_RWKV), 0.1),
        "r_k": nrm((DEPTH, N_RWKV_HEADS, HEAD_DIM), 0.1),
        "gn_w": gain((DEPTH, D_RWKV)),
        "gn_b": nrm((DEPTH, D_RWKV), 0.02),
        "w_out": nrm((DEPTH, D_MIX, D_MODEL), D_MIX ** -0.5),
        "w_ffn_up": nrm((DEPTH, D_MODEL, D_FF), D_MODEL ** -0.5),
        "w_ffn_down": nrm((DEPTH, D_FF, D_MODEL), D_FF ** -0.5),
    }

def first_block(x, norm_mix_pre, norm_mix_post, norm_ffn_pre, norm_ffn_post,
              w_in_first, w_in_rest, mu_shift, mu_shift_mv, attn_out_gain,
              decay_w0, decay_up, aaa_a0, aaa_up, mv_v0, mv_up, gate_up,
              k_k, k_a, r_k, gn_w, gn_b, w_out, w_ffn_up, w_ffn_down):
    v_first = None
    o0, o1, o2 = 3 * D_RWKV, 3 * D_RWKV + LORA_DECAY, 3 * D_RWKV + LORA_DECAY + LORA_AAA
    for i in range(DEPTH):
        h = _rms_norm(x, norm_mix_pre[i])
        z = h @ (w_in_first if i == 0 else w_in_rest[i - 1])
        q = z[..., 0:D_ATTN]
        k = z[..., D_ATTN:2 * D_ATTN]
        v = z[..., 2 * D_ATTN:3 * D_ATTN]
        zs = _token_shift(z[..., 3 * D_ATTN:3 * D_ATTN + N_SHIFT], mu_shift[i])
        r_r = zs[..., 0:D_RWKV]
        k_r = zs[..., D_RWKV:2 * D_RWKV]
        v_r = zs[..., 2 * D_RWKV:3 * D_RWKV]
        xw = zs[..., o0:o1]
        xa = zs[..., o1:o2]
        xg = zs[..., o2:N_SHIFT]
        if i == 0:
            v_first = v_r
        else:
            xmv = _token_shift(z[..., N_COLS_FIRST:], mu_shift_mv[i - 1])
            vgate = jax.nn.sigmoid(mv_v0[i - 1] + xmv @ mv_up[i - 1])
            v_r = v_r + (v_first - v_r) * vgate
        attn = _rms_norm(_dilated_attention(q, k, v), attn_out_gain[i])
        rw = _rwkv7(r_r, k_r, v_r, xw, xa, xg, decay_w0[i], decay_up[i], aaa_a0[i],
                    aaa_up[i], gate_up[i], k_k[i], k_a[i], r_k[i], gn_w[i], gn_b[i])
        mixed = jnp.concatenate([attn, rw], axis=-1) @ w_out[i]
        x = x + _rms_norm(mixed, norm_mix_post[i])
        h = _rms_norm(x, norm_ffn_pre[i])
        f = jnp.square(jax.nn.relu(h @ w_ffn_up[i])) @ w_ffn_down[i]
        x = x + _rms_norm(f, norm_ffn_post[i])
    return x


MEM_LEN = 256
EPS = 1e-6
CONV_DIM = 512
CONV_WIDTH = 31
FOX_HEADS = 8
FOX_HEAD_DIM = 64
FOX_DIM = FOX_HEADS * FOX_HEAD_DIM
XA_HEADS = 4
XA_HEAD_DIM = 128
XA_DIM = XA_HEADS * XA_HEAD_DIM
N_GROUPS = 4
EXPERTS_PER_GROUP = 4
N_EXPERTS = N_GROUPS * EXPERTS_PER_GROUP
TOP_K = 2
EXPERT_FF = 256
SPLITS = (2 * CONV_DIM, FOX_DIM, FOX_DIM, FOX_DIM, FOX_HEADS, D_MODEL, D_MODEL)
IN_COLS = sum(SPLITS)


def rmsnorm(x, g):
    xf = x.astype(jnp.float32)
    y = xf * lax.rsqrt(jnp.mean(xf * xf, axis=-1, keepdims=True) + EPS)
    return (y * g.astype(jnp.float32)).astype(x.dtype)

def layernorm(x, g, b):
    xf = x.astype(jnp.float32)
    mu = jnp.mean(xf, axis=-1, keepdims=True)
    var = jnp.mean(jnp.square(xf - mu), axis=-1, keepdims=True)
    y = (xf - mu) * lax.rsqrt(var + EPS)
    return (y * g.astype(jnp.float32) + b.astype(jnp.float32)).astype(x.dtype)

def conformer_conv(u_glu, dw_w, dw_b, ln_g, ln_b, pw_w):
    a, gate = jnp.split(u_glu, 2, axis=-1)
    u = a * jax.nn.sigmoid(gate)
    u = lax.conv_general_dilated(
        u, dw_w[:, None, :].astype(u.dtype), window_strides=(1,),
        padding=[(CONV_WIDTH - 1, 0)],
        dimension_numbers=("NWC", "WIO", "NWC"),
        feature_group_count=CONV_DIM) + dw_b
    u = jax.nn.silu(layernorm(u, ln_g, ln_b))
    return u @ pw_w

def fox_attention(q, k, v, logf):
    B, T, H, dh = q.shape
    nb = T // Q_BLOCK
    scale = dh ** -0.5
    c = jnp.cumsum(logf, axis=1).transpose(0, 2, 1)
    qh = q.transpose(0, 2, 1, 3)
    kh = k.transpose(0, 2, 1, 3)
    vh = v.transpose(0, 2, 1, 3)
    qb = qh.reshape(B, H, nb, Q_BLOCK, dh).transpose(2, 0, 1, 3, 4)
    cb = c.reshape(B, H, nb, Q_BLOCK).transpose(2, 0, 1, 3)
    kpos = jnp.arange(T)

    def block(args):
        q_i, c_i, i = args
        s = jnp.einsum("bhqd,bhkd->bhqk", q_i, kh).astype(jnp.float32) * scale
        s = s + c_i[..., :, None] - c[:, :, None, :]
        qpos = i * Q_BLOCK + jnp.arange(Q_BLOCK)
        s = jnp.where(kpos[None, :] <= qpos[:, None], s, -jnp.inf)
        p = jax.nn.softmax(s, axis=-1)
        return jnp.einsum("bhqk,bhkd->bhqd", p.astype(vh.dtype), vh)

    o = lax.map(block, (qb, cb, jnp.arange(nb)))
    return o.transpose(1, 0, 3, 2, 4).reshape(B, T, H * dh)

def cross_attention(h, m, wq, wk, wv, wo):
    B, T, _ = h.shape
    M = m.shape[1]
    q = (h @ wq).reshape(B, T, XA_HEADS, XA_HEAD_DIM)
    k = (m @ wk).reshape(B, M, XA_HEADS, XA_HEAD_DIM)
    v = (m @ wv).reshape(B, M, XA_HEADS, XA_HEAD_DIM)
    s = jnp.einsum("bthd,bmhd->bhtm", q, k).astype(jnp.float32) * XA_HEAD_DIM ** -0.5
    p = jax.nn.softmax(s, axis=-1)
    o = jnp.einsum("bhtm,bmhd->bthd", p.astype(v.dtype), v).reshape(B, T, XA_DIM)
    return o @ wo

def hierarchical_moe(h, wg, bg, we, be, w_gate, w_up, w_down):
    B, T, D = h.shape
    hf = h.reshape(B * T, D)
    g_logits = (hf @ wg).astype(jnp.float32) + bg.astype(jnp.float32)
    p_group = jax.nn.softmax(g_logits, axis=-1)
    g_star = jnp.argmax(p_group, axis=-1)
    p_gsel = jnp.take_along_axis(p_group, g_star[:, None], axis=-1)[:, 0]
    e_logits = ((hf @ we).astype(jnp.float32) + be.astype(jnp.float32)).reshape(-1, N_GROUPS, EXPERTS_PER_GROUP)
    e_sel = jnp.take_along_axis(e_logits, g_star[:, None, None], axis=1)[:, 0]
    p_exp = jax.nn.softmax(e_sel, axis=-1)
    top_v, top_i = lax.top_k(p_exp, TOP_K)
    top_v = top_v / jnp.sum(top_v, axis=-1, keepdims=True)
    weights = p_gsel[:, None] * top_v
    expert_idx = g_star[:, None] * EXPERTS_PER_GROUP + top_i
    combine = jnp.sum(jax.nn.one_hot(expert_idx, N_EXPERTS, dtype=jnp.float32) * weights[..., None], axis=1)
    a = jnp.einsum("nd,edf->nef", hf, w_gate)
    b = jnp.einsum("nd,edf->nef", hf, w_up)
    u = jax.nn.silu(a) * b * combine.astype(hf.dtype)[..., None]
    y = jnp.einsum("nef,efd->nd", u, w_down)
    return y.reshape(B, T, D)

def second_inputs(seed: int = 0) -> dict:
    key = jax.random.key(seed)
    ks = jax.random.split(key, 32)
    f32 = jnp.float32

    def nrm(k, shape, fan_in):
        return jax.random.normal(k, shape, f32) * (fan_in ** -0.5)

    def gain(k, shape):
        return 1.0 + 0.1 * jax.random.normal(k, shape, f32)

    def small(k, shape, s=0.01):
        return s * jax.random.normal(k, shape, f32)

    L = DEPTH
    return {
        "x": jax.random.normal(ks[0], (BATCH, SEQ, D_MODEL), f32),
        "mem": jax.random.normal(ks[1], (BATCH, MEM_LEN, D_MODEL), f32),
        "norm_mix_g": gain(ks[2], (L, D_MODEL)),
        "w_in": nrm(ks[3], (L, D_MODEL, IN_COLS), D_MODEL),
        "fox_bf": jax.random.uniform(ks[4], (L, FOX_HEADS), f32, 1.0, 4.0),
        "conv_dw_w": nrm(ks[5], (L, CONV_WIDTH, CONV_DIM), CONV_WIDTH),
        "conv_dw_b": small(ks[6], (L, CONV_DIM)),
        "conv_ln_g": gain(ks[7], (L, CONV_DIM)),
        "conv_ln_b": small(ks[8], (L, CONV_DIM)),
        "conv_pw_w": nrm(ks[9], (L, CONV_DIM, D_MODEL), CONV_DIM),
        "attn_branch_w": nrm(ks[10], (L, FOX_DIM, D_MODEL), FOX_DIM),
        "w_out": nrm(ks[11], (L, D_MODEL, D_MODEL), D_MODEL),
        "norm_xa_g": gain(ks[12], (L, D_MODEL)),
        "norm_mem_g": gain(ks[13], (L, D_MODEL)),
        "xa_wq": nrm(ks[14], (L, D_MODEL, XA_DIM), D_MODEL),
        "xa_wk": nrm(ks[15], (L, D_MODEL, XA_DIM), D_MODEL),
        "xa_wv": nrm(ks[16], (L, D_MODEL, XA_DIM), D_MODEL),
        "xa_wo": nrm(ks[17], (L, XA_DIM, D_MODEL), XA_DIM),
        "norm_moe_g": gain(ks[18], (L, D_MODEL)),
        "router_group_w": nrm(ks[19], (L, D_MODEL, N_GROUPS), D_MODEL),
        "router_group_b": small(ks[20], (L, N_GROUPS)),
        "router_expert_w": nrm(ks[21], (L, D_MODEL, N_EXPERTS), D_MODEL),
        "router_expert_b": small(ks[22], (L, N_EXPERTS)),
        "expert_w_gate": nrm(ks[23], (L, N_EXPERTS, D_MODEL, EXPERT_FF), D_MODEL),
        "expert_w_up": nrm(ks[24], (L, N_EXPERTS, D_MODEL, EXPERT_FF), D_MODEL),
        "expert_w_down": nrm(ks[25], (L, N_EXPERTS, EXPERT_FF, D_MODEL), EXPERT_FF),
        "norm_final_g": gain(ks[26], (D_MODEL,)),
    }

def second_block(x, mem, norm_mix_g, w_in, fox_bf, conv_dw_w, conv_dw_b, conv_ln_g, conv_ln_b,
              conv_pw_w, attn_branch_w, w_out, norm_xa_g, norm_mem_g, xa_wq, xa_wk, xa_wv, xa_wo,
              norm_moe_g, router_group_w, router_group_b, router_expert_w, router_expert_b,
              expert_w_gate, expert_w_up, expert_w_down, norm_final_g):
    B, T, _ = x.shape
    cuts = np.cumsum(SPLITS)[:-1].tolist()
    for l in range(DEPTH):
        h = rmsnorm(x, norm_mix_g[l])
        proj = h @ w_in[l]
        u_glu, q, k, v, f_logit, gate_c, gate_a = jnp.split(proj, cuts, axis=-1)
        conv_out = conformer_conv(u_glu, conv_dw_w[l], conv_dw_b[l], conv_ln_g[l],
                                  conv_ln_b[l], conv_pw_w[l])
        logf = jax.nn.log_sigmoid(f_logit.astype(jnp.float32) + fox_bf[l].astype(jnp.float32))
        attn = fox_attention(q.reshape(B, T, FOX_HEADS, FOX_HEAD_DIM),
                             k.reshape(B, T, FOX_HEADS, FOX_HEAD_DIM),
                             v.reshape(B, T, FOX_HEADS, FOX_HEAD_DIM), logf)
        attn_out = attn @ attn_branch_w[l]
        merged = jax.nn.sigmoid(gate_c) * conv_out + jax.nn.sigmoid(gate_a) * attn_out
        x = x + merged @ w_out[l]
        x = x + cross_attention(rmsnorm(x, norm_xa_g[l]), rmsnorm(mem, norm_mem_g[l]),
                                xa_wq[l], xa_wk[l], xa_wv[l], xa_wo[l])
        x = x + hierarchical_moe(rmsnorm(x, norm_moe_g[l]), router_group_w[l], router_group_b[l],
                                 router_expert_w[l], router_expert_b[l], expert_w_gate[l],
                                 expert_w_up[l], expert_w_down[l])
    return rmsnorm(x, norm_final_g)


def setup_inputs(seed=0):
    out = dict(first_inputs(seed))
    for name, value in second_inputs(seed + 1).items():
        if name != "x":
            out[name + "_2"] = value
    return out


def reference(
    x, norm_mix_pre, norm_mix_post, norm_ffn_pre, norm_ffn_post, w_in_first, w_in_rest,
    mu_shift, mu_shift_mv, attn_out_gain, decay_w0, decay_up, aaa_a0, aaa_up, mv_v0, mv_up,
    gate_up, k_k, k_a, r_k, gn_w, gn_b, w_out, w_ffn_up, w_ffn_down, mem_2, norm_mix_g_2,
    w_in_2, fox_bf_2, conv_dw_w_2, conv_dw_b_2, conv_ln_g_2, conv_ln_b_2, conv_pw_w_2,
    attn_branch_w_2, w_out_2, norm_xa_g_2, norm_mem_g_2, xa_wq_2, xa_wk_2, xa_wv_2, xa_wo_2,
    norm_moe_g_2, router_group_w_2, router_group_b_2, router_expert_w_2, router_expert_b_2,
    expert_w_gate_2, expert_w_up_2, expert_w_down_2, norm_final_g_2,
):
    x = first_block(
        x, norm_mix_pre, norm_mix_post, norm_ffn_pre, norm_ffn_post, w_in_first, w_in_rest,
        mu_shift, mu_shift_mv, attn_out_gain, decay_w0, decay_up, aaa_a0, aaa_up, mv_v0, mv_up,
        gate_up, k_k, k_a, r_k, gn_w, gn_b, w_out, w_ffn_up, w_ffn_down,
    )
    return second_block(
        x, mem_2, norm_mix_g_2, w_in_2, fox_bf_2, conv_dw_w_2, conv_dw_b_2, conv_ln_g_2,
        conv_ln_b_2, conv_pw_w_2, attn_branch_w_2, w_out_2, norm_xa_g_2, norm_mem_g_2, xa_wq_2,
        xa_wk_2, xa_wv_2, xa_wo_2, norm_moe_g_2, router_group_w_2, router_group_b_2,
        router_expert_w_2, router_expert_b_2, expert_w_gate_2, expert_w_up_2, expert_w_down_2,
        norm_final_g_2,
    )


_drawn_inputs = setup_inputs


def setup_inputs(seed=0):
    import zlib

    import numpy as np

    out = dict(_drawn_inputs(seed))
    spreads = {}
    factors = {'decay_up': 3.332,
     'aaa_a0': 2.869,
     'gn_b': 4.142,
     'conv_dw_b_2': 5.905,
     'conv_ln_b_2': 8.0,
     'norm_xa_g_2': 5.546,
     'norm_mem_g_2': 3.729,
     'router_group_b_2': 39.302,
     'router_expert_b_2': 64.0,
     'norm_moe_g_2': 3.152}
    for name, (base, spread) in spreads.items():
        noise = np.random.default_rng([zlib.crc32(name.encode()), seed]).standard_normal(out[name].shape)
        drawn = base * np.exp(spread * noise) if base else spread * noise
        out[name] = __import__('jax').numpy.asarray(drawn.astype(out[name].dtype))
    for name, factor in factors.items():
        out[name] = (out[name] * factor).astype(out[name].dtype)
    return out
```

```python
from contextlib import ExitStack

import concourse.bass as bass
from concourse import mybir
import numpy as np

F32 = mybir.dt.float32
F32R = mybir.dt.float32r
I32 = mybir.dt.int32
U32 = mybir.dt.uint32
ALU = mybir.AluOpType
ACT = mybir.ActivationFunctionType
AX_X = mybir.AxisListType.X

P = 128
T = 512
NT = T // P
D = 1024
KD = D // P
H = 512
KH = H // P
HD = 64
NHEAD = H // HD
FF = 4 * D
MEM = 256
NMT = MEM // P
XH = 4
XHD = 128
NSHIFT = 3 * H + 32 + 32 + 96
W_LORA = 32
R_GATE = 96
IN1 = 3 * H + NSHIFT
EPS = 1e-6
GN_EPS = 64e-5
NEG = -1e30
TAPS = 31
PAD = TAPS - 1
NG = 4
EPG = 4
NE = NG * EPG
EF = 256
TOPK = 2
MOE_TILES = T * TOPK // P + NE - 1
SLOTS = MOE_TILES * P
EXTRA = MOE_TILES - NE
PAIRS = MOE_TILES // 2
CHUNK = 128
NCH = T // CHUNK
DECAY = float(np.exp(-0.5))
LEVELS = 7

COLS = [
    ("norm_mix_pre", 8), ("norm_ffn_pre", 8), ("attn_out_gain", 4), ("mu_r", 4), ("mu_k", 4), ("mu_v", 4),
    ("mu_wa", 1), ("mu_g", 1), ("decay_w0", 4), ("aaa_a0", 4), ("k_k", 4), ("k_a", 4), ("r_k", 4),
    ("gn_w", 4), ("gn_b", 4), ("norm_mix_g_2", 8), ("norm_xa_g_2", 8), ("norm_mem_g_2", 8),
    ("norm_moe_g_2", 8), ("conv_dw_w_2", 4 * TAPS), ("conv_dw_b_2", 4), ("conv_ln_g_2", 4),
    ("conv_ln_b_2", 4), ("fox_bf_2", 1),
]
COL_AT = {}
_at = 0
for _name, _n in COLS:
    COL_AT[_name] = (_at, _n)
    _at += _n
NCOLS = _at

CONSTS = [
    ("ident", 128), ("head_sum", 128), ("head_mean", 128), ("chan_mean", 128), ("ones", 128), ("before", 128),
    ("band_causal", T), ("band_dilated", T), ("tri", 256), ("restart", T), ("levels", LEVELS * 64),
    ("ident64", 64), ("eps", 2), ("first4", 4), ("tile_edges", 4), ("tile_no", 24),
]
CONST_AT = {}
_at = 0
for _name, _n in CONSTS:
    CONST_AT[_name] = (_at, _n)
    _at += _n
NCONSTS = _at


def shape_constants():
    c = np.zeros((P, NCONSTS), np.float32)

    def put(name, a):
        at, n = CONST_AT[name]
        c[:, at:at + n] = a

    i = np.arange(P)
    same_head = (i[:, None] // HD == i[None, :] // HD).astype(np.float32)
    put("ident", np.eye(P))
    put("head_sum", same_head)
    put("head_mean", same_head / HD)
    put("chan_mean", np.full((P, P), 1.0 / H))
    put("ones", np.ones((P, P)))
    put("before", i[:, None] < i[None, :])
    dist = i[:, None] + (T - P) - np.arange(T)[None, :]
    put("band_causal", np.where(dist >= 0, 0.0, NEG))
    count = ((dist >= 0) & (dist <= 128)).astype(int)
    count += (dist >= 0) & (dist % 4 == 0)
    count += (dist >= 0) & (dist % 16 == 0)
    put("band_dilated", np.where(count > 0, np.log(np.maximum(count, 1)), NEG))
    put("tri", np.concatenate([i[:, None] < i[None, :], i[:, None] <= i[None, :]], 1))
    put("restart", np.broadcast_to(np.arange(T) % CHUNK != 0, (P, T)))
    lv = []
    for n in range(LEVELS):
        b = 1 << n
        col = np.arange(64)
        lv.append(i[:, None] // b == 2 * (col[None, :] // b) + 1)
    put("levels", np.concatenate(lv, 1))
    put("ident64", np.concatenate([np.eye(64), np.eye(64)], 0))
    put("eps", np.broadcast_to(np.array([EPS, GN_EPS]), (P, 2)))
    put("first4", np.broadcast_to(np.array([4.0, 3.0, 2.0, 1.0]), (P, 4)))
    put("tile_edges", np.broadcast_to(np.arange(4) * 128.0, (P, 4)))
    put("tile_no", np.broadcast_to(np.arange(24), (P, 24)))
    return c


FFN_ORDER = [(0, None), (1, None), (None, 0), (2, None), (None, 1), (3, None), (None, 2), (None, 3)]


def weight_slabs(w):
    slabs = []

    def wide(name, a, c0, cols):
        for n in range(0, cols, 256):
            m = min(256, cols - n)
            slabs.append((f"{name}{n // 256}", a[:, c0 + n:c0 + n + m].rearrange("(k p) n -> p k n", p=P)))

    def deep(name, a, r0, rows, c0):
        for n in range(0, rows, 512):
            slabs.append((f"{name}{n // 512}", a[r0 + n:r0 + n + 512, c0:c0 + 512].rearrange("(k p) n -> p k n", p=P)))

    w1, w2 = w["w_in_first"], w["w_in_2"][0]
    wide("q", w1, 0, H)
    wide("k", w1, H, H)
    deep("v", w1, 0, D, 2 * H)
    wide("rr", w1, 3 * H, H)
    wide("rk", w1, 4 * H, H)
    wide("rv", w1, 5 * H, H)
    wide("lora", w1, 6 * H, 160)
    for hf in range(2):
        deep(f"out.{hf}.", w["w_out"][0], 0, D, 512 * hf)
    for up, down in FFN_ORDER:
        if up is not None:
            wide(f"up.{up}.", w["w_ffn_up"][0], up * D, D)
        else:
            for hf in range(2):
                deep(f"down.{down}.{hf}.", w["w_ffn_down"][0], down * D, D, 512 * hf)
    wide("glu_gate", w2, H, H)
    wide("glu_a", w2, 0, H)
    wide("fq", w2, 2 * H, H)
    wide("fk", w2, 3 * H, H)
    deep("fv", w2, 0, D, 4 * H)
    wide("ff", w2, 5 * H, 128)
    for hf in range(2):
        wide(f"gc.{hf}.", w2, 5 * H + 8 + 512 * hf, 512)
        deep(f"pw.{hf}.", w["conv_pw_w_2"][0], 0, H, 512 * hf)
    for hf in range(2):
        wide(f"ga.{hf}.", w2, 5 * H + 8 + D + 512 * hf, 512)
        deep(f"ab.{hf}.", w["attn_branch_w_2"][0], 0, H, 512 * hf)
    for hf in range(2):
        deep(f"out2.{hf}.", w["w_out_2"][0], 0, D, 512 * hf)
    wide("xk", w["xa_wk_2"][0], 0, H)
    deep("xv", w["xa_wv_2"][0], 0, D, 0)
    wide("xq", w["xa_wq_2"][0], 0, H)
    for hf in range(2):
        deep(f"xo.{hf}.", w["xa_wo_2"][0], 0, H, 512 * hf)
    return slabs


RAW = 2
SPLIT = 2
WIDE_STEPS = 3


class Banks:

    def __init__(self, banks, full, free):
        self.banks, self.full, self.free = banks, full, free
        self.uses = [0] * len(banks)
        self.frees = [0] * len(banks)
        self.next = 0
        self.at = {}
        self.last = [None] * len(banks)

    def plan(self, name, read=None, full=True):
        b = self.next % len(self.banks)
        self.next += 1
        assert name not in self.at, name
        if read is None:
            self.frees[b] += 1
            read = (self.free[b], self.frees[b])
        self.uses[b] += full
        self.at[name] = (b, self.uses[b], read, self.last[b])
        self.last[b] = name

    def open(self, pe, name):
        b, _, _, before = self.at[name]
        if before:
            pe.wait_ge(*self.at[before][2])
        return self.banks[b]

    def filled(self, product, name):
        product.then_inc(self.full[self.at[name][0]], 1)

    def full_at(self, name):
        b, n, _, _ = self.at[name]
        return self.full[b], n

    def take(self, eng, name):
        eng.wait_ge(*self.full_at(name))
        return self.banks[self.at[name][0]]

    def done(self, read, name):
        assert self.at[name][2][0] is self.free[self.at[name][0]], name
        read.then_inc(self.free[self.at[name][0]], 1)


class Steps:

    def __init__(self, eng, sem):
        self.eng, self.sem, self.n = eng, sem, 0

    def mark(self, ins):
        ins.then_inc(self.sem, 1)
        self.n += 1
        return self.n

    def after(self, n):
        self.eng.wait_ge(self.sem, n)

    def link(self, ins):
        self.after(self.mark(ins))


def in_turn(*programs):
    programs = list(programs)
    while programs:
        for program in list(programs):
            if next(program, END) is END:
                programs.remove(program)


END = object()


def two_blocks(nc, w, cols_in, consts_in, out):
    slabs = weight_slabs(w)
    slab_no = {name: n for n, (name, _) in enumerate(slabs)}

    with ExitStack() as ctx:
        def sem(name):
            return ctx.enter_context(nc.semaphore(name))

        place = [16512]

        def sb(name, shape, dt=F32, at=None):
            size = int(np.prod(shape[1:])) * 4
            offset = place[0] if at is None else at
            if at is None:
                place[0] += (size + 31) // 32 * 32
            assert offset + size <= nc.sbuf_usable_end, (name, offset + size)
            return nc.alloc_sbuf_tensor_at(name, list(shape), dt, offset=offset)

        def phase(start):
            at = [start]

            def put(name, shape, dt=F32):
                size = (int(np.prod(shape[1:])) * 4 + 31) // 32 * 32
                t = sb(name, shape, dt, at=at[0])
                at[0] += size
                return t

            put.at = at
            return put

        consts = sb("consts", [P, NCONSTS])
        cols = sb("cols", [P, NCOLS])
        less = sb("less", [P, 20])
        gain_row = sb("gain_row", [P, D])
        ring_at = place[0]
        raw = sb("raw", [P, RAW, 2048])
        whi = sb("whi", [P, SPLIT, 2048], F32R)
        wlo = sb("wlo", [P, SPLIT, 2048], F32R)
        act_at = place[0]
        ahi = sb("ahi", [P, KD, T], F32R)
        alo = sb("alo", [P, KD, T], F32R)
        region = place[0]

        def const(name):
            at, n = CONST_AT[name]
            return consts[:, at:at + n]

        def col(name, j=0, n=1):
            at, _ = COL_AT[name]
            return cols[:, at + j:at + j + n]

        ident = const("ident")
        LESS = {"mu_r": 0, "mu_k": 4, "mu_v": 8, "mu_wa": 12, "mu_g": 13, "k_a": 14}

        def one_less(name, j=0):
            return less[:, LESS[name] + j:LESS[name] + j + 1]

        banks = Banks([ctx.enter_context(nc.psum_tensor(f"bank{b}", [P, 512], F32)) for b in range(8)],
                      [sem(f"bank_full{b}") for b in range(8)], [sem(f"bank_free{b}") for b in range(8)])

        raw_in = [sem(f"raw_in{n}") for n in range(RAW)]
        hi_made = sem("hi_made")
        lo_made = sem("lo_made")
        slab_used = sem("slab_used")
        consts_in_sem = sem("consts_loaded")
        dve_steps = sem("dve_steps")
        act_steps = sem("act_steps")
        pool_steps = sem("pool_steps")

        def view(t, n, k, cols_):
            return t[:, n, 0:k * cols_].rearrange("p (k n) -> p k n", k=k)

        def slab_shape(n):
            return slabs[n][1].shape[1], slabs[n][1].shape[2]

        def load_slabs(sp, state, upto):
            while state[0] < min(upto, len(slabs)):
                n = state[0]
                k, c = slab_shape(n)
                if n >= RAW:
                    sp.wait_ge(lo_made, n - RAW + 1)
                sp.dma_start(view(raw, n % RAW, k, c), slabs[n][1]).then_inc(raw_in[n % RAW], 16)
                state[0] += 1

        def make_hi(act, state, upto):
            while state[0] < min(upto, len(slabs)):
                n = state[0]
                k, c = slab_shape(n)
                act.wait_ge(raw_in[n % RAW], 16 * (n // RAW + 1))
                if n >= SPLIT:
                    act.wait_ge(*slab_end[n - SPLIT])
                nc.scalar.activation(whi[:, n % SPLIT, 0:k * c], raw[:, n % RAW, 0:k * c], ACT.Copy).then_inc(hi_made, 1)
                state[0] += 1

        def make_lo(pool, state, upto):
            while state[0] < min(upto, len(slabs)):
                n = state[0]
                k, c = slab_shape(n)
                pool.wait_ge(hi_made, n + 1)
                nc.gpsimd.tensor_tensor(wlo[:, n % SPLIT, 0:k * c], raw[:, n % RAW, 0:k * c],
                                        whi[:, n % SPLIT, 0:k * c].bitcast(F32), ALU.subtract).then_inc(lo_made, 1)
                state[0] += 1

        sp_slab, act_slab, pool_slab = [0], [0], [0]

        slab_end = {}
        inner_slabs = [0]

        def wide_units(name, units, read=None):
            for j in range(units):
                banks.plan(f"{name}/{j}", read(j) if read else None)
                if j == units - 1:
                    slab_end[slab_no[name]] = banks.full_at(f"{name}/{j}")
                yield from range(WIDE_STEPS)

        def plan_wide(name, units, read=None):
            in_turn(wide_units(name, units, read))

        def plan_deep(names, unit, tiles=NT, read=None):
            for t in range(tiles):
                banks.plan(f"{unit}/{t}", read(t) if read else None)
            for name in names[:-1]:
                inner_slabs[0] += 1
                slab_end[slab_no[name]] = (slab_used, inner_slabs[0])
            slab_end[slab_no[names[-1]]] = banks.full_at(f"{unit}/{tiles - 1}")

        def three_passes(acc, pairs, first, last):
            ins = None
            for i, ((sh, sl), (mh, ml)) in enumerate(pairs):
                end = i == len(pairs) - 1
                nc.tensor.matmul(acc, sh, ml, start=first and i == 0, stop=False)
                nc.tensor.matmul(acc, sh, mh, start=False, stop=False)
                ins = nc.tensor.matmul(acc, sl, mh, start=False, stop=last and end)
            return ins

        def pe_wide(pe, name, **how):
            in_turn(pe_wide_steps(pe, name, **how))

        def pe_wide_steps(pe, name, k0=0, tokens=T, acts=None, parts=None):
            n = slab_no[name]
            k, c = slab_shape(n)
            xh, xl = acts or (ahi, alo)
            pe.wait_ge(lo_made, n + 1)
            wh, wl = view(whi, n % SPLIT, k, c), view(wlo, n % SPLIT, k, c)
            parts = parts or [(i, i + P) for i in range(0, c, P)]
            for j, (c0, c1) in enumerate(parts):
                unit = f"{name}/{j}"
                acc = banks.open(pe, unit)
                for step in range(WIDE_STEPS):
                    ks = range(step * k // WIDE_STEPS, (step + 1) * k // WIDE_STEPS)
                    ins = three_passes(acc[0:c1 - c0, 0:tokens],
                                       [((wh[:, i, c0:c1], wl[:, i, c0:c1]), (xh[:, k0 + i, 0:tokens], xl[:, k0 + i, 0:tokens]))
                                        for i in ks], step == 0, step == WIDE_STEPS - 1)
                    if step == WIDE_STEPS - 1:
                        banks.filled(ins, unit)
                    yield

        def pe_deep(pe, names, unit, k0=0, tiles=NT, acts=None):
            xh, xl = acts or (ahi, alo)
            accs = [banks.open(pe, f"{unit}/{t}") for t in range(tiles)]
            at = k0
            for s, name in enumerate(names):
                n = slab_no[name]
                k, c = slab_shape(n)
                pe.wait_ge(lo_made, n + 1)
                wh, wl = view(whi, n % SPLIT, k, c), view(wlo, n % SPLIT, k, c)
                for t in range(tiles):
                    ts = slice(t * P, (t + 1) * P)
                    ins = three_passes(accs[t][:, :], [((xh[:, at + i, ts], xl[:, at + i, ts]), (wh[:, i, :], wl[:, i, :]))
                                                       for i in range(k)], s == 0, s == len(names) - 1)
                    if s == len(names) - 1:
                        banks.filled(ins, f"{unit}/{t}")
                if s < len(names) - 1:
                    ins.then_inc(slab_used, 1)
                at += k


        squares_made = sem("squares_made")
        var_made = sem("var_made")
        root_made = sem("root_made")
        rows_normed = sem("rows_normed")
        cols_scaled = sem("cols_scaled")
        cols_hi = sem("cols_hi")
        cols_lo = sem("cols_lo")
        turns = {}
        turn_count = {"tile": 0, "stage": 0, "unit": 0, "split": 0}

        def plan_turn(name, tiles, depth, normalise=True, split=True):
            halves = (depth + 3) // 4
            st = dict(tiles=tiles, depth=depth, halves=halves, normalise=normalise, **turn_count)
            turns[name] = st
            if normalise:
                turn_count["tile"] += tiles
                turn_count["stage"] += 1
            turn_count["unit"] += tiles * halves
            if split:
                turn_count["split"] += tiles * halves
            for t in range(tiles):
                for h in range(halves):
                    banks.plan(f"{name}/{t}.{h}", (cols_scaled, st["unit"] + t * halves + h + 1))

        def act_squares(act, name, rows, ready, scratch, sums):
            st = turns[name]
            n = st["tiles"]
            for t in range(n):
                ready(act, t)
                if t >= 2:
                    act.wait_ge(squares_made, st["tile"] + t - 1)
                nc.scalar.activation(scratch[:, t % 2, 0:st["depth"] * P], rows(t), ACT.Square,
                                     accum_out=sums[:, t:t + 1]).then_inc(squares_made, 1)
            act.wait_ge(var_made, st["stage"] + 1)
            nc.scalar.activation(sums[:, 8:8 + n], sums[:, 4:4 + n], ACT.Sqrt).then_inc(root_made, 1)

        def dve_rows(dve, steps, name, rows, ready, sums, normal, gain=None, scaled=None, plain=None):
            st = turns[name]
            n = st["tiles"]
            dve.wait_ge(squares_made, st["tile"] + n)
            nc.vector.tensor_scalar(sums[:, 4:4 + n], sums[:, 0:n], 1.0 / (st["depth"] * P), EPS,
                                    ALU.mult, ALU.add).then_inc(var_made, 1)
            dve.wait_ge(root_made, st["stage"] + 1)
            steps.link(nc.vector.reciprocal(sums[:, 12:12 + n], sums[:, 8:8 + n]))
            for t in range(n + 1):
                if t < n:
                    ready(dve, t)
                    if t >= 2:
                        banks.take(dve, f"{name}/{t - 2}.{st['halves'] - 1}")
                    nc.vector.tensor_scalar(normal(t), rows(t), sums[:, 12 + t:13 + t], None, ALU.mult).then_inc(rows_normed, 1)
                if t >= 1:
                    dve_columns(dve, name, t - 1, gain, scaled, plain)

        def dve_columns(dve, name, t, gain, scaled, plain=None):
            st = turns[name]
            for h in range(st["halves"]):
                n = st["split"] + t * st["halves"] + h
                acc = banks.take(dve, f"{name}/{t}.{h}")
                blocks = acc[:, :].rearrange("p (j n) -> p j n", j=4)
                if plain is None:
                    if n >= 2:
                        dve.wait_ge(cols_lo, n - 1)
                    to = scaled[:, n % 2, :].rearrange("p (j n) -> p j n", j=4)
                else:
                    to = plain[:, 4 * h:4 * h + 4, t * P:(t + 1) * P]
                if gain is None:
                    ins = nc.vector.tensor_copy(to, blocks)
                else:
                    ins = nc.vector.tensor_tensor(to, blocks, col(gain, 4 * h, 4).unsqueeze(2).broadcast_to([P, 4, P]), ALU.mult)
                ins.then_inc(cols_scaled, 1)

        def pe_turn(pe, name, normal, ready=None):
            st = turns[name]
            for t in range(st["tiles"]):
                if st["normalise"]:
                    pe.wait_ge(rows_normed, st["tile"] + t + 1)
                else:
                    ready(pe, t)
                for h in range(st["halves"]):
                    acc = banks.open(pe, f"{name}/{t}.{h}")
                    for j in range(4):
                        c = (4 * h + j) * P
                        ins = nc.tensor.transpose(acc[:, j * P:(j + 1) * P], normal(t)[:, c:c + P], ident)
                    banks.filled(ins, f"{name}/{t}.{h}")

        def each_split(name):
            st = turns[name]
            for t in range(st["tiles"]):
                for h in range(st["halves"]):
                    j = t * st["halves"] + h
                    yield st["unit"] + j, st["split"] + j, slice(4 * h, 4 * h + 4), slice(t * P, (t + 1) * P)

        def act_columns(act, name, scaled, hi):
            for unit, n, ks, ts in each_split(name):
                act.wait_ge(cols_scaled, unit + 1)
                nc.scalar.activation(hi[:, ks, ts], scaled[:, n % 2, :].rearrange("p (j n) -> p j n", j=4),
                                     ACT.Copy).then_inc(cols_hi, 1)

        def pool_columns(pool, name, scaled, hi, lo):
            for unit, n, ks, ts in each_split(name):
                pool.wait_ge(cols_hi, n + 1)
                nc.gpsimd.tensor_tensor(lo[:, ks, ts], scaled[:, n % 2, :].rearrange("p (j n) -> p j n", j=4),
                                        hi[:, ks, ts].bitcast(F32), ALU.subtract).then_inc(cols_lo, 1)

        def columns_ready(pe, name):
            st = turns[name]
            pe.wait_ge(cols_lo, st["split"] + st["tiles"] * st["halves"])

        scores_in = sem("scores_in_sbuf")
        peak_made = sem("score_peaks")
        probs_made = sem("probs_made")
        probs_turned = sem("probs_turned")
        heads_out = sem("heads_out")
        attns = {}
        attn_count = [0]

        def attn_units(name, heads, keys):
            items = [(h, t, keys(t)) for h in range(heads) for t in range(NT)]
            base = attn_count[0]
            attns[name] = dict(items=items, base=base)
            attn_count[0] += len(items)
            for i in range(len(items) + 2):
                n = base + i
                if i < len(items):
                    banks.plan(f"{name}/s{i}", (scores_in, n + 1))
                if 1 <= i <= len(items):
                    banks.plan(f"{name}/t{i - 1}", (probs_turned, n))
                if i >= 2:
                    banks.plan(f"{name}/o{i - 2}", (heads_out, n - 1))
                yield

        def pe_attn(pe, name, q, k, v, probs, probs_t, bias=None):
            items, base = attns[name]["items"], attns[name]["base"]
            for i in range(len(items) + 2):
                if i < len(items):
                    h, t, keys = items[i]
                    acc = banks.open(pe, f"{name}/s{i}")
                    ins = nc.tensor.matmul(acc[:, 0:keys], q(h, t), k(h, keys), start=True, stop=bias is None)
                    if bias is not None:
                        ins = nc.tensor.matmul(acc[:, 0:keys], bias[0](h), bias[1](keys), start=False, stop=True)
                    banks.filled(ins, f"{name}/s{i}")
                if 1 <= i <= len(items):
                    h, t, keys = items[i - 1]
                    pe.wait_ge(probs_made, base + i)
                    acc = banks.open(pe, f"{name}/t{i - 1}")
                    for b in range(0, keys, P):
                        ins = nc.tensor.transpose(acc[:, b:b + P], probs[:, (i - 1) % 2, b:b + P], ident)
                    banks.filled(ins, f"{name}/t{i - 1}")
                if i >= 2:
                    h, t, keys = items[i - 2]
                    pe.wait_ge(probs_turned, base + i - 1)
                    acc = banks.open(pe, f"{name}/o{i - 2}")
                    n = v(h, 0).shape[1]
                    for b in range(keys // P):
                        ins = nc.tensor.matmul(acc[:, 0:n], probs_t[:, (i - 2) % 2, b * P:(b + 1) * P], v(h, b),
                                               start=b == 0, stop=b == keys // P - 1)
                    banks.filled(ins, f"{name}/o{i - 2}")
                yield

        def dve_attn(dve, steps, name, scale, band, masked, peaks, sums, heads):
            items, base = attns[name]["items"], attns[name]["base"]
            for i in range(len(items) + 2):
                if i < len(items):
                    h, t, keys = items[i]
                    n = base + i
                    acc = banks.take(dve, f"{name}/s{i}")
                    if i >= 2:
                        dve.wait_ge(probs_made, n - 1)
                    if band is None:
                        ins = nc.vector.tensor_scalar(masked[:, i % 2, 0:keys], acc[:, 0:keys], scale, None, ALU.mult)
                    else:
                        off = (NT - 1 - t) * P
                        ins = nc.vector.scalar_tensor_tensor(out=masked[:, i % 2, 0:keys], in0=acc[:, 0:keys], scalar=scale,
                                                             in1=band[:, off:off + keys], op0=ALU.mult, op1=ALU.add)
                    ins.then_inc(scores_in, 1)
                    dve.wait_ge(scores_in, n + 1)
                    nc.vector.tensor_reduce(peaks[:, i:i + 1], masked[:, i % 2, 0:keys], AX_X, ALU.max, negate=True).then_inc(peak_made, 1)
                if i >= 2:
                    h, t, keys = items[i - 2]
                    acc = banks.take(dve, f"{name}/o{i - 2}")
                    steps.link(nc.vector.reciprocal(peaks[:, 32 + i - 2:33 + i - 2], sums[:, i - 2:i - 1]))
                    to = heads(h, t)
                    nc.vector.tensor_scalar(to, acc[:, 0:to.shape[1]], peaks[:, 32 + i - 2:33 + i - 2], None,
                                            ALU.mult).then_inc(heads_out, 1)
                yield

        def act_attn(act, name, masked, peaks, sums, probs, probs_t):
            items, base = attns[name]["items"], attns[name]["base"]
            for i in range(len(items) + 2):
                if i < len(items):
                    h, t, keys = items[i]
                    act.wait_ge(peak_made, base + i + 1)
                    if i >= 2:
                        banks.take(act, f"{name}/t{i - 2}")
                    nc.scalar.activation(probs[:, i % 2, 0:keys], masked[:, i % 2, 0:keys], ACT.Exp, bias=peaks[:, i:i + 1],
                                         accum_out=sums[:, i:i + 1]).then_inc(probs_made, 1)
                if 1 <= i <= len(items):
                    h, t, keys = items[i - 1]
                    acc = banks.take(act, f"{name}/t{i - 1}")
                    if i >= 3:
                        banks.take(act, f"{name}/o{i - 3}")
                    nc.scalar.activation(probs_t[:, (i - 1) % 2, 0:keys], acc[:, 0:keys], ACT.Copy).then_inc(probs_turned, 1)
                yield

        put = phase(region)
        x_rows = put("x_rows", [P, NT, D])
        normal1 = put("normal1", [P, 2, D])
        scratch1 = put("scratch1", [P, 2, D])
        p1_scaled = sb("p1_scaled", [P, 2, 512], at=put.at[0])
        sums1 = sb("sums1", [P, 16], at=put.at[0] + 4096)
        put = phase(region)
        zr, zk, zv = (put(n, [P, KH, T]) for n in ("zr", "zk", "zv"))
        lora_wa = put("lora_wa", [P, T])
        lora_g = put("lora_g", [P, T])
        lora_w = put("lora_w", [2 * W_LORA, H])
        gate_w = put("gate_w", [R_GATE, H])
        rw_region = put.at[0]
        qt, kt = (put(n, [P, KH, T]) for n in ("qt", "kt"))
        vt = put("vt", [P, NT, H])
        masked1 = put("masked1", [P, 2, T])
        probs1 = put("probs1", [P, 2, T])
        probst1 = put("probst1", [P, 2, T])
        heads1 = put("heads1", [P, NT, H])
        peaks1 = put("peaks1", [P, 64])
        esum1 = put("esum1", [P, 32])
        ascaled = put("attn_scaled", [P, 2, 512])
        ascratch = put("attn_scratch", [P, 2, 512])
        anormal = put("attn_normal", [P, 2, 512])
        asums = put("attn_sums", [P, 16])
        put = phase(rw_region)

        class Pair:
            pass

        def pair_buffers(s):
            b = Pair()
            work = put(f"rw_work{s}", [P, 12, T])

            def wk(n, m=1):
                return work[:, n:n + m, :].rearrange("p a n -> p (a n)")

            def units(n):
                return wk(n, 4).rearrange("p (u n) -> p u n", u=8)

            b.cum, b.cumx, b.e_in, b.e_inv, b.e_ex, b.aaa, b.knorm, b.kk, b.kmod, b.ka, b.rk, b.sig = (wk(n) for n in range(12))
            b.kr = put(f"rw_kr{s}", [P, NCH, 2, CHUNK])
            b.beta = put(f"rw_beta{s}", [P, T])
            b.khat = put(f"rw_khat{s}", [P, T])
            b.mids, b.fin, b.fout = (put(f"rw_{n}{s}", [P, 4]) for n in ("mids", "fin", "fout"))
            b.ab, b.bd = units(0), units(4)
            b.xinv = wk(8, 2).rearrange("p (u n) -> p u n", u=8)
            b.xinv_t = b.bd[:, :, 0:CHUNK]
            b.ktok, b.btok = (wk(n).rearrange("p (c n) -> p c n", c=NCH) for n in (10, 11))
            b.vtok = put(f"rw_vtok{s}", [P, NCH, P])
            b.kb = put(f"rw_kb{s}", [P, 2, NCH, P])
            b.tm = b.beta[:, :].rearrange("p (u n) -> p u n", u=8)
            b.neg_w = b.xinv
            b.qq = b.khat[:, :]
            kb_flat = b.kb[:, :, :, :].rearrange("p h c n -> p (h c n)")
            b.gt = kb_flat[:, 0:256].rearrange("p (c n) -> p c n", c=4)
            b.state = kb_flat[:, 256:384].rearrange("p (b n) -> p b n", b=2)
            b.ysb, b.dev, b.dev2, b.rstd, b.norm_y, b.with_bonus, b.rw = (wk(n) for n in (0, 1, 2, 3, 0, 2, 1))
            return b

        pairs = [pair_buffers(0), pair_buffers(1)]

        x_in = sem("x_in")
        qkv_out = sem("qkv_out")
        z_less = sem("z_less")
        z_shifted = sem("z_shifted")
        lora_acts = sem("lora_acts")
        less_made = sem("less_made")
        small_in = sem("small_in")
        LEVEL_NAMES = [str(n) for n in range(LEVELS)]
        PAIR_STEPS = {
            "act": ["sig", "aaa", "sq", "norm", "e_in", "e_inv", "e_ex", "fout", "ktok", "vtok", "btok", "kktok", "bv"]
                   + [f"xt{n}.{i}" for n in LEVEL_NAMES for i in range(2)] + ["w0", "w1", "y", "dev2", "sd", "hi"],
            "dve": ["scan", "mids", "cum", "cumx", "fin", "kmod_a", "kmod", "rk", "nmax", "nrec", "kk", "khat", "beta", "kappa", "bonus"]
                   + [f"mask{i}" for i in range(8)] + [f"{x}{n}" for n in LEVEL_NAMES for x in ("tm", "x")]
                   + ["qq", "gt", "state0", "state1", "state2", "dev", "rstd", "norm_y", "with_bonus", "rw"],
            "pool": ["ka", "r", "init_x", "init_xt", "lo"],
        }
        pair_done = {e: [sem(f"pair_{e}_steps{s}") for s in range(2)] for e in PAIR_STEPS}
        states_summed = [sem(f"states_summed{s}") for s in range(2)]

        def step_of(engine, p, name):
            names = PAIR_STEPS[engine]
            return pair_done[engine][p % 2], len(names) * (p // 2) + names.index(name) + 1

        class PairSteps:

            def __init__(self, eng, engine, p):
                self.eng, self.engine, self.p, self.names = eng, engine, p, list(PAIR_STEPS.get(engine, []))

            def done(self, ins, name):
                assert name == self.names.pop(0), name
                ins.then_inc(pair_done[self.engine][self.p % 2], 1)

            def after(self, engine, name):
                self.eng.wait_ge(*step_of(engine, self.p, name))

        QKV = ["q0", "q1", "k0", "k1"]
        SHIFT = ["rr0", "rr1", "rk0", "rk1", "rv0", "rv1"]
        shift_units = [(f"{n}/{j}", z, 2 * (s % 2) + j, mu) for s, n in enumerate(SHIFT) for j in range(2)
                       for z, mu in [((zr, "mu_r"), (zk, "mu_k"), (zv, "mu_v"))[s // 2]]]

        plan_turn("mix1", NT, KD)
        for s, n in enumerate(QKV):
            plan_wide(n, 2, lambda j, s=s: (qkv_out, 2 * s + j + 1))
        plan_deep(["v0", "v1"], "v", read=lambda t: (qkv_out, 9 + t))
        def shift_plan():
            for s, n in enumerate(SHIFT):
                yield from wide_units(n, 2, lambda j, s=s: (z_shifted, 2 * s + j + 1))
            yield from wide_units("lora0", 2, lambda j: (z_shifted, 13 + j))

        in_turn(attn_units("dil", NHEAD, lambda t: (t + 1) * P), shift_plan())
        plan_turn("attn1", NT, KH)
        def rwkv_units(p):
            u = f"rw{p}/"

            def plan(name, engine, step):
                banks.plan(u + name, step_of(engine, p, step))

            plan("decay", "act", "sig")
            plan("aaa", "act", "aaa")
            yield
            plan("ss", "act", "norm")
            yield
            plan("bonus", "dve", "bonus")
            yield
            for name in ("ktok", "vtok", "btok", "kktok"):
                plan(name, "act", name)
                yield
            for i in range(8):
                plan(f"mask{i}", "dve", f"mask{i}")
                yield
            plan("bv", "act", "bv")
            yield
            for n in range(LEVELS):
                plan(f"t{n}", "dve", f"tm{n}")
                yield
                if n:
                    plan(f"x{n}", "dve", f"x{n}")
                    yield
                for i in range(2):
                    plan(f"xt{n}.{i}", "act", f"xt{n}.{i}")
                    yield
            for i in range(2):
                plan(f"w{i}", "act", f"w{i}")
            yield
            plan("q", "dve", "qq")
            plan("g", "dve", "gt")
            yield
            banks.plan(u + "h", step_of("dve", p, "state2"), full=False)
            yield
            plan("y", "act", "y")
            yield
            for c in range(1, NCH):
                yield
            plan("mean", "dve", "dev")
            yield
            plan("var", "act", "sd")
            yield
            plan("gate", "dve", "rw")
            yield

        for p in range(0, 4, 2):
            in_turn(rwkv_units(p), rwkv_units(p + 1))

        def x_ready(eng, t):
            eng.wait_ge(x_in, 16 * NT)

        def heads1_ready(eng, t):
            eng.wait_ge(heads_out, attns["dil"]["base"] + len(attns["dil"]["items"]))

        def normal1_of(t):
            return normal1[:, t % 2, :]

        def anormal_of(t):
            return anormal[:, t % 2, :]

        def half(h):
            return slice(h * HD, (h + 1) * HD)

        def pe_phase1(pe):
            pe.wait_ge(consts_in_sem, 32)
            pe_turn(pe, "mix1", normal1_of)
            columns_ready(pe, "mix1")
            for n in QKV:
                pe_wide(pe, n)
            pe_deep(pe, ["v0", "v1"], "v")
            pe.wait_ge(qkv_out, 12)
            in_turn(pe_attn(pe, "dil",
                            lambda h, t: qt[half(h % 2), h // 2, t * P:(t + 1) * P], lambda h, n: kt[half(h % 2), h // 2, 0:n],
                            lambda h, b: vt[:, b, half(h)], probs1, probst1),
                    pe_shift(pe))
            pe_turn(pe, "attn1", anormal_of)
            pe.wait_ge(small_in, 48)
            pe.wait_ge(lora_acts, 2)
            for p in range(0, 4, 2):
                in_turn(pe_rwkv(pe, p), pe_rwkv(pe, p + 1))

        def pe_shift(pe):
            for n in SHIFT:
                yield from pe_wide_steps(pe, n)
            yield from pe_wide_steps(pe, "lora0", parts=[(0, P), (2 * W_LORA, 2 * W_LORA + R_GATE)])

        def pe_rwkv(pe, p):
            u = f"rw{p}/"
            b = pairs[p % 2]
            st = PairSteps(pe, "pe", p)
            fc = slice(p * P, (p + 1) * P)
            units = [(h, c) for h in range(2) for c in range(NCH)]

            def single(name, lhs, rhs):
                acc = banks.open(pe, u + name)
                banks.filled(nc.tensor.matmul(acc[:, :], lhs, rhs, start=True, stop=True), u + name)

            single("decay", lora_w[0:W_LORA, fc], lora_wa[0:W_LORA, :])
            single("aaa", lora_w[W_LORA:2 * W_LORA, fc], lora_wa[W_LORA:2 * W_LORA, :])
            yield
            st.after("act", "sq")
            single("ss", const("head_sum"), b.knorm)
            yield
            st.after("dve", "rk")
            single("bonus", const("head_sum"), b.rk)
            yield
            for name, src, made in (("ktok", b.khat[:, :], "khat"), ("vtok", zv[:, p, :], None), ("btok", b.beta[:, :], "beta"),
                                    ("kktok", b.kr[:, :, 0, :], "kappa")):
                if made:
                    st.after("dve", made)
                acc = banks.open(pe, u + name)
                for c in range(NCH):
                    tokens = src[:, c, :] if name == "kktok" else src[:, c * CHUNK:(c + 1) * CHUNK]
                    ins = nc.tensor.transpose(acc[:, c * P:(c + 1) * P], tokens, ident)
                banks.filled(ins, u + name)
                yield
            st.after("pool", "r")
            for i, (src, h, c) in enumerate((src, h, c) for src in (b.beta, b.khat) for h in range(2) for c in (0, 2)):
                acc = banks.open(pe, f"{u}mask{i}")
                for j in range(2):
                    ins = nc.tensor.matmul(acc[:, j * 256:(j + 1) * 256], src[half(h), (c + j) * CHUNK:(c + j + 1) * CHUNK],
                                           b.kr[half(h), c + j, :, :].rearrange("p a n -> p (a n)"), start=True, stop=True)
                banks.filled(ins, f"{u}mask{i}")
                yield
            st.after("act", "vtok")
            st.after("dve", "mask7")
            acc = banks.open(pe, u + "bv")
            for n, (h, c) in enumerate(units):
                ins = nc.tensor.matmul(acc[:, n * HD:(n + 1) * HD], b.bd[:, n, 0:CHUNK], b.vtok[:, c, half(h)], start=True, stop=True)
            banks.filled(ins, u + "bv")
            yield
            for lv in range(LEVELS):
                size = 1 << lv
                if lv:
                    st.after("dve", f"x{lv - 1}")
                else:
                    st.after("pool", "init_x")
                acc = banks.open(pe, f"{u}t{lv}")
                left = b.xinv.rearrange("p u (n s b) -> p u n s b", s=2, b=size)
                for n in range(8):
                    ins = nc.tensor.matmul(acc[:, n * 64:(n + 1) * 64], b.ab[:, n, 0:CHUNK], left[:, n, :, 0, :], start=True, stop=True)
                banks.filled(ins, f"{u}t{lv}")
                yield
                if lv:
                    st.after("dve", f"tm{lv}")
                    st.after("act", f"xt{lv - 1}.1")
                    acc = banks.open(pe, f"{u}x{lv}")
                    for n in range(8):
                        ins = nc.tensor.matmul(acc[:, n * 64:(n + 1) * 64], b.xinv_t[:, n, :], b.tm[:, n, :], start=True, stop=True)
                    banks.filled(ins, f"{u}x{lv}")
                    yield
                st.after("dve", f"x{lv}")
                for i in range(2):
                    acc = banks.open(pe, f"{u}xt{lv}.{i}")
                    for j in range(4):
                        ins = nc.tensor.transpose(acc[:, j * P:(j + 1) * P], b.xinv[:, 4 * i + j, :], ident)
                    banks.filled(ins, f"{u}xt{lv}.{i}")
                    yield
            st.after("act", f"xt{LEVELS - 1}.1")
            for i in range(2):
                acc = banks.open(pe, f"{u}w{i}")
                for c in range(NCH):
                    ins = nc.tensor.matmul(acc[:, c * P:(c + 1) * P], b.xinv_t[:, 4 * i + c, :], b.kb[:, i, c, :], start=True, stop=True)
                banks.filled(ins, f"{u}w{i}")
            yield
            st.after("act", "w1")
            acc = banks.open(pe, u + "q")
            for n, (h, c) in enumerate(units):
                ins = nc.tensor.matmul(acc[half(h), c * CHUNK:(c + 1) * CHUNK], b.neg_w[:, n, HD:2 * HD], b.ab[:, n, CHUNK:2 * CHUNK],
                                       start=c == 0, stop=c == NCH - 1, skip_group_check=True)
            banks.filled(ins, u + "q")
            acc = banks.open(pe, u + "g")
            for n, (h, c) in enumerate(units):
                if 1 <= c < NCH - 1:
                    ins = nc.tensor.matmul(acc[half(h), c * HD:(c + 1) * HD], b.neg_w[:, n, HD:2 * HD], b.btok[:, c, half(h)],
                                           start=c == 1, stop=c == NCH - 2, skip_group_check=True)
            banks.filled(ins, u + "g")
            yield
            hacc = banks.open(pe, u + "h")
            for n, (h, c) in enumerate(units):
                if c < NCH - 1:
                    to = hacc[half(h), c * HD:(c + 1) * HD]
                    nc.tensor.matmul(to, b.ktok[:, c, half(h)], b.vtok[:, c, half(h)], start=c == 0, stop=False, skip_group_check=True)
                    ins = nc.tensor.matmul(to, b.btok[:, c, half(h)], b.neg_w[:, n, 0:HD], start=False, stop=True, skip_group_check=True)
            ins.then_inc(states_summed[p % 2], 1)
            yield
            yacc = banks.open(pe, u + "y")
            for n, (h, c) in enumerate(units):
                to = yacc[half(h), c * CHUNK:(c + 1) * CHUNK]
                nc.tensor.matmul(to, b.neg_w[:, n, 0:HD], b.ab[:, n, CHUNK:2 * CHUNK], start=c == 0, stop=False, skip_group_check=True)
                nc.tensor.matmul(to, b.vtok[:, c, half(h)], b.bd[:, n, CHUNK:2 * CHUNK], start=False, stop=True, skip_group_check=True)
            yield
            st.after("dve", "gt")
            for c in range(1, NCH):
                st.after("dve", f"state{c - 1}")
                state = b.state[:, (c - 1) % 2, :]
                if c < NCH - 1:
                    for h in range(2):
                        ins = nc.tensor.matmul(hacc[half(h), c * HD:(c + 1) * HD], b.gt[half(h), c, :], state[half(h), :],
                                               start=False, stop=True, skip_group_check=True)
                    ins.then_inc(states_summed[p % 2], 1)
                for h in range(2):
                    ins = nc.tensor.matmul(yacc[half(h), c * CHUNK:(c + 1) * CHUNK], state[half(h), :],
                                           b.qq[half(h), c * CHUNK:(c + 1) * CHUNK], start=False, stop=True, skip_group_check=True)
                if c == NCH - 1:
                    banks.filled(ins, u + "y")
                yield
            st.after("act", "y")
            single("mean", const("head_mean"), b.ysb)
            yield
            st.after("act", "dev2")
            single("var", const("head_mean"), b.dev2)
            yield
            single("gate", gate_w[:, fc], lora_g[0:R_GATE, :])
            yield

        def act_phase1(act):
            make_hi(act, act_slab, SPLIT)
            act.wait_ge(consts_in_sem, 32)
            act_squares(act, "mix1", lambda t: x_rows[:, t, :], x_ready, scratch1, sums1)
            act_columns(act, "mix1", p1_scaled, ahi)
            act.wait_ge(less_made, 2)
            for n in QKV + ["v0", "v1"]:
                make_hi(act, act_slab, slab_no[n] + 1 + SPLIT)
            in_turn(act_attn(act, "dil", masked1, peaks1, esum1, probs1, probst1), act_shift(act))
            act.wait_ge(z_shifted, 14)
            nc.scalar.activation(lora_wa[0:W_LORA, :], lora_wa[0:W_LORA, :], ACT.Tanh).then_inc(lora_acts, 1)
            nc.scalar.activation(lora_g[0:R_GATE, :], lora_g[0:R_GATE, :], ACT.Sigmoid).then_inc(lora_acts, 1)
            act_squares(act, "attn1", lambda t: heads1[:, t, :], heads1_ready, ascratch, asums)
            act_columns(act, "attn1", ascaled, ahi)
            act.wait_ge(cols_lo, turns["attn1"]["split"] + NT)
            for p in range(0, 4, 2):
                in_turn(act_rwkv(act, p), act_rwkv(act, p + 1))

        def act_shift(act):
            for i, (unit, z, m, mu) in enumerate(shift_units):
                yield from range(WIDE_STEPS - 1)
                acc = banks.take(act, unit)
                nc.scalar.activation(z[:, m, :], acc[:, :], ACT.Copy, scale=one_less(mu, m)).then_inc(z_less, 1)
                if i % 2:
                    make_hi(act, act_slab, slab_no[unit.split("/")[0]] + 1 + SPLIT)
                yield
            for i, (to, mu) in enumerate(((lora_wa, "mu_wa"), (lora_g, "mu_g"))):
                yield from range(WIDE_STEPS - 1)
                acc = banks.take(act, f"lora0/{i}")
                r = slice(0, (2 * W_LORA, R_GATE)[i])
                nc.scalar.activation(to[r, :], acc[r, :], ACT.Copy, scale=one_less(mu)[r, :]).then_inc(z_less, 1)
                yield
            make_hi(act, act_slab, slab_no["lora0"] + 1 + SPLIT)

        def act_rwkv(act, p):
            u = f"rw{p}/"
            b = pairs[p % 2]
            st = PairSteps(act, "act", p)
            activate = nc.scalar.activation
            if p >= 2:
                act.wait_ge(*step_of("pool", p - 2, "lo"))
            acc = banks.take(act, u + "decay")
            st.done(activate(b.sig, acc[:, :], ACT.Sigmoid, bias=col("decay_w0", p)), "sig")
            acc = banks.take(act, u + "aaa")
            st.done(activate(b.aaa, acc[:, :], ACT.Sigmoid, bias=col("aaa_a0", p)), "aaa")
            st.done(activate(b.knorm, zk[:, p, :], ACT.Square, scale=col("k_k", p)), "sq")
            yield
            acc = banks.take(act, u + "ss")
            st.done(activate(b.knorm, acc[:, :], ACT.Sqrt), "norm")
            yield
            st.after("dve", "fin")
            st.done(activate(b.e_in, b.cum, ACT.Exp, scale=-DECAY), "e_in")
            st.done(activate(b.e_inv, b.cum, ACT.Exp, scale=DECAY), "e_inv")
            st.done(activate(b.e_ex, b.cumx, ACT.Exp, scale=-DECAY), "e_ex")
            st.done(activate(b.fout[:, 0:3], b.fin[:, 0:3], ACT.Exp, scale=-DECAY), "fout")
            yield
            for name, to in (("ktok", b.ktok), ("vtok", b.vtok), ("btok", b.btok)):
                acc = banks.take(act, u + name)
                st.done(activate(to[:, :, :], acc[:, :].rearrange("p (c n) -> p c n", c=NCH), ACT.Copy), name)
                yield
            acc = banks.take(act, u + "kktok")
            st.done(activate(b.kb[:, :, :, HD:2 * HD].rearrange("p h c n -> p c h n"),
                             acc[:, :].rearrange("p (c h n) -> p c h n", c=NCH, h=2), ACT.Copy), "kktok")
            yield
            acc = banks.take(act, u + "bv")
            st.done(activate(b.kb[:, :, :, 0:HD].rearrange("p h c n -> p (h c) n"),
                             acc[:, :].rearrange("p (u n) -> p u n", u=8), ACT.Copy), "bv")
            yield
            for lv in range(LEVELS):
                for i in range(2):
                    acc = banks.take(act, f"{u}xt{lv}.{i}")
                    st.after("pool", "init_xt")
                    st.done(activate(b.xinv_t[:, 4 * i:4 * i + 4, :], acc[:, :].rearrange("p (u n) -> p u n", u=4),
                                     ACT.Copy), f"xt{lv}.{i}")
                    yield
            for i in range(2):
                acc = banks.take(act, f"{u}w{i}")
                st.done(activate(b.neg_w[:, 4 * i:4 * i + 4, :], acc[:, :].rearrange("p (u n) -> p u n", u=4),
                                 ACT.Copy, scale=-1.0), f"w{i}")
            yield
            acc = banks.take(act, u + "y")
            st.done(activate(b.ysb, acc[:, :], ACT.Copy), "y")
            yield
            st.after("dve", "dev")
            st.done(activate(b.dev2, b.dev, ACT.Square), "dev2")
            yield
            acc = banks.take(act, u + "var")
            st.done(activate(b.rstd, acc[:, :], ACT.Sqrt, bias=const("eps")[:, 1:2]), "sd")
            yield
            st.after("dve", "rw")
            st.done(activate(ahi[:, KH + p, :], b.rw, ACT.Copy), "hi")
            yield

        def dve_phase1(dve, steps):
            dve.wait_ge(consts_in_sem, 32)
            at, _ = COL_AT["mu_r"]
            nc.vector.tensor_scalar(less[:, 0:14], cols[:, at:at + 14], -1.0, 1.0, ALU.mult, ALU.add).then_inc(less_made, 1)
            nc.vector.tensor_scalar(less[:, 14:18], col("k_a", 0, 4), -1.0, 1.0, ALU.mult, ALU.add).then_inc(less_made, 1)
            dve_rows(dve, steps, "mix1", lambda t: x_rows[:, t, :], x_ready, sums1, normal1_of, "norm_mix_pre", p1_scaled)
            for s, n in enumerate(QKV):
                for j in range(2):
                    acc = banks.take(dve, f"{n}/{j}")
                    nc.vector.tensor_copy((qt, kt)[s // 2][:, 2 * (s % 2) + j, :], acc[:, :]).then_inc(qkv_out, 1)
            for t in range(NT):
                acc = banks.take(dve, f"v/{t}")
                nc.vector.tensor_copy(vt[:, t, :], acc[:, :]).then_inc(qkv_out, 1)
            in_turn(dve_attn(dve, steps, "dil", HD ** -0.5, const("band_dilated"), masked1, peaks1, esum1,
                             lambda h, t: heads1[:, t, half(h)]),
                    dve_shift(dve))
            dve_rows(dve, steps, "attn1", lambda t: heads1[:, t, :], heads1_ready, asums, anormal_of, "attn_out_gain", ascaled)
            for p in range(0, 4, 2):
                in_turn(dve_rwkv(dve, p), dve_rwkv(dve, p + 1))

        def dve_shift(dve):
            for i, (unit, z, m, mu) in enumerate(shift_units):
                yield from range(WIDE_STEPS - 1)
                acc = banks.take(dve, unit)
                dve.wait_ge(z_less, i + 1)
                nc.vector.scalar_tensor_tensor(out=z[:, m, 1:T], in0=acc[:, 0:T - 1], scalar=col(mu, m), in1=z[:, m, 1:T],
                                               op0=ALU.mult, op1=ALU.add).then_inc(z_shifted, 1)
                yield
            for i, (to, mu) in enumerate(((lora_wa, "mu_wa"), (lora_g, "mu_g"))):
                yield from range(WIDE_STEPS - 1)
                r = slice(0, (2 * W_LORA, R_GATE)[i])
                acc = banks.take(dve, f"lora0/{i}")
                dve.wait_ge(z_less, 13 + i)
                nc.vector.scalar_tensor_tensor(out=to[r, 1:T], in0=acc[r, 0:T - 1], scalar=col(mu)[r, :], in1=to[r, 1:T],
                                               op0=ALU.mult, op1=ALU.add).then_inc(z_shifted, 1)
                yield

        def dve_rwkv(dve, p):
            u = f"rw{p}/"
            b = pairs[p % 2]
            st = PairSteps(dve, "dve", p)
            chunks = lambda a: a.rearrange("p (c n) -> p c n", c=NCH)
            tt, stt, tsc = nc.vector.tensor_tensor, nc.vector.scalar_tensor_tensor, nc.vector.tensor_scalar

            def link(ins, name):
                st.done(ins, name)
                st.after("dve", name)

            st.after("act", "sig")
            link(nc.vector.tensor_tensor_scan(b.cum, const("restart"), b.sig, 0.0, ALU.mult, ALU.add), "scan")
            link(nc.vector.tensor_copy(b.mids[:, :], chunks(b.cum)[:, :, CHUNK // 2 - 1]), "mids")
            link(tt(chunks(b.cum), chunks(b.cum), b.mids[:, :].unsqueeze(2).broadcast_to([P, NCH, CHUNK]), ALU.subtract), "cum")
            st.done(tt(b.cumx, b.cum, b.sig, ALU.subtract), "cumx")
            st.done(tt(b.fin[:, 0:3], chunks(b.cum)[:, 0:3, CHUNK - 1], b.mids[:, 1:4], ALU.add), "fin")
            yield
            st.after("act", "aaa")
            link(tsc(b.kmod, b.aaa, col("k_a", p), one_less("k_a", p), ALU.mult, ALU.add), "kmod_a")
            link(tt(b.kmod, b.kmod, zk[:, p, :], ALU.mult), "kmod")
            st.done(stt(out=b.rk, in0=zr[:, p, :], scalar=col("r_k", p), in1=b.kmod, op0=ALU.mult, op1=ALU.mult), "rk")
            yield
            st.after("act", "norm")
            link(tsc(b.knorm, b.knorm, 1e-12, None, ALU.max), "nmax")
            link(nc.vector.reciprocal(b.knorm, b.knorm), "nrec")
            st.done(stt(out=b.kk, in0=zk[:, p, :], scalar=col("k_k", p), in1=b.knorm, op0=ALU.mult, op1=ALU.mult), "kk")
            yield
            st.after("act", "e_inv")
            st.done(tt(b.khat[:, :], b.kmod, b.e_inv, ALU.mult), "khat")
            yield
            st.after("pool", "ka")
            st.done(tt(b.beta[:, :], b.ka, b.e_inv, ALU.mult), "beta")
            st.after("dve", "kk")
            st.after("act", "e_ex")
            st.done(tt(b.kr[:, :, 0, :], chunks(b.kk), chunks(b.e_ex), ALU.mult), "kappa")
            yield
            acc = banks.take(dve, u + "bonus")
            banks.take(dve, u + "vtok")
            st.done(tt(zv[:, p, :], acc[:, :], zv[:, p, :], ALU.mult), "bonus")
            yield
            tri = const("tri").unsqueeze(1).broadcast_to([P, 2, 256])
            for i in range(8):
                acc = banks.take(dve, f"{u}mask{i}")
                to = (b.ab, b.bd)[i // 4][:, 2 * (i % 4):2 * (i % 4) + 2, :]
                st.done(tt(to, acc[:, :].rearrange("p (c n) -> p c n", c=2), tri, ALU.mult), f"mask{i}")
                yield
            for lv in range(LEVELS):
                size = 1 << lv
                between = const("levels")[:, lv * 64:(lv + 1) * 64].unsqueeze(1).broadcast_to([P, 8, 64])
                acc = banks.take(dve, f"{u}t{lv}")
                st.done(tt(b.tm, acc[:, :].rearrange("p (u n) -> p u n", u=8), between, ALU.mult), f"tm{lv}")
                yield
                left = b.xinv.rearrange("p u (n s b) -> p (u n) s b", s=2, b=size)[:, :, 0, :]
                if lv:
                    minus = banks.take(dve, f"{u}x{lv}")[:, :]
                else:
                    st.after("dve", "tm0")
                    minus = b.tm.rearrange("p u n -> p (u n)")
                st.done(tt(left, left, minus.rearrange("p (n b) -> p n b", b=size), ALU.subtract), f"x{lv}")
                yield
            acc = banks.take(dve, u + "q")
            st.done(tt(chunks(b.qq), chunks(acc[:, :]), b.kr[:, :, 1, :], ALU.add), "qq")
            acc = banks.take(dve, u + "g")
            st.done(tt(b.gt[:, 1:3, :], acc[:, HD:3 * HD].rearrange("p (c n) -> p c n", c=2),
                       const("ident64").unsqueeze(1).broadcast_to([P, 2, HD]), ALU.add), "gt")
            yield
            acc = banks.banks[banks.at[u + "h"][0]]
            for c in range(NCH - 1):
                dve.wait_ge(states_summed[p % 2], (NCH - 1) * (p // 2) + c + 1)
                st.done(tsc(b.state[:, c % 2, :], acc[:, c * HD:(c + 1) * HD], b.fout[:, c:c + 1], None, ALU.mult), f"state{c}")
                yield
            acc = banks.take(dve, u + "mean")
            st.done(tt(b.dev, b.ysb, acc[:, :], ALU.subtract), "dev")
            yield
            st.after("act", "sd")
            link(nc.vector.reciprocal(b.rstd, b.rstd), "rstd")
            link(stt(out=b.norm_y, in0=b.dev, scalar=col("gn_w", p), in1=b.rstd, op0=ALU.mult, op1=ALU.mult), "norm_y")
            link(stt(out=b.with_bonus, in0=zv[:, p, :], scalar=col("gn_b", p), in1=b.norm_y, op0=ALU.add, op1=ALU.add), "with_bonus")
            acc = banks.take(dve, u + "gate")
            st.done(tt(b.rw, b.with_bonus, acc[:, :], ALU.mult), "rw")
            yield

        def pool_phase1(pool, steps):
            nc.gpsimd.memset(gain_row[:, :], 0.0).then_inc(zeros_made, 1)
            make_lo(pool, pool_slab, SPLIT)
            pool_columns(pool, "mix1", p1_scaled, ahi, alo)
            make_lo(pool, pool_slab, slab_no["lora0"] + 1 + SPLIT)
            pool_columns(pool, "attn1", ascaled, ahi, alo)
            for p in range(0, 4, 2):
                in_turn(pool_rwkv(pool, p), pool_rwkv(pool, p + 1))

        def pool_rwkv(pool, p):
            b = pairs[p % 2]
            st = PairSteps(pool, "pool", p)
            tt, copy = nc.gpsimd.tensor_tensor, nc.gpsimd.tensor_copy
            st.after("dve", "kk")
            st.done(tt(b.ka, b.kk, b.aaa, ALU.mult), "ka")
            st.after("act", "e_in")
            st.done(tt(b.kr[:, :, 1, :], zr[:, p, :].rearrange("p (c n) -> p c n", c=NCH),
                       b.e_in.rearrange("p (c n) -> p c n", c=NCH), ALU.mult), "r")
            yield
            st.after("dve", "beta")
            st.after("pool", "ka")
            st.done(copy(b.xinv, ident.unsqueeze(1).broadcast_to([P, 8, P])), "init_x")
            yield
            banks.take(pool, f"rw{p}/bv")
            st.done(copy(b.xinv_t, ident.unsqueeze(1).broadcast_to([P, 8, P])), "init_xt")
            yield
            st.after("act", "hi")
            st.done(tt(alo[:, KH + p, :], b.rw, ahi[:, KH + p, :].bitcast(F32), ALU.subtract), "lo")
            yield

        def sp_phase1(sp):
            sp.dma_start(consts[:, :], consts_in).then_inc(consts_in_sem, 16)
            sp.dma_start(cols[:, :], cols_in).then_inc(consts_in_sem, 16)
            x_view = w["x"][0].rearrange("(t p) d -> p t d", p=P)
            for t in range(NT):
                sp.dma_start(x_rows[:, t, :], x_view[:, t, :]).then_inc(x_in, 16)
            load_slabs(sp, sp_slab, RAW)
            sp.wait_ge(cols_lo, turns["mix1"]["split"] + 2 * NT)
            sp.dma_start(lora_w[0:W_LORA, :], w["decay_up"][0]).then_inc(small_in, 16)
            sp.dma_start(lora_w[W_LORA:2 * W_LORA, :], w["aaa_up"][0]).then_inc(small_in, 16)
            sp.dma_start(gate_w[:, :], w["gate_up"][0]).then_inc(small_in, 16)
            load_slabs(sp, sp_slab, slab_no["lora0"] + 1 + RAW)
            sp.wait_ge(zeros_made, 1)
            sp.dma_start(slots_dram.rearrange("(t p) d -> p t d", p=P),
                         gain_row[:, :].unsqueeze(1).broadcast_to([P, MOE_TILES, D])).then_inc(slots_zeroed, 16)

        put = phase(region)
        x = put("x_res", [P, NT, D])
        after_x = put.at[0]
        fsb = put("f_rows", [P, NT, D])
        normal2 = put("normal2", [P, 2, D])
        scratch2 = put("scratch2", [P, 2, D])
        scaled2 = put("scaled2", [P, 2, T])
        put.at[0] -= 5 * 4096
        fhi = put("ffn_hi", [P, 2, KD, T], F32R)
        flo = put("ffn_lo", [P, 2, KD, T], F32R)
        relu = put("ffn_relu", [P, 2, T])
        relu2 = put("ffn_relu2", [P, 2, T])
        sums2 = put("sums2", [P, 16])
        psums = put("post_sums", [P, 16])

        mix_out = sem("mix_out")
        post_sq = sem("post_sq")
        post_var = sem("post_var")
        post_root = sem("post_root")
        x_added = sem("x_added")
        gain_in = sem("gain_in")
        up_relu = sem("up_relu")
        up_sq = sem("up_sq")
        up_hi = sem("up_hi")
        up_lo = sem("up_lo")

        for hf in range(2):
            plan_deep([f"out.{hf}.0", f"out.{hf}.1"], f"mix.{hf}", read=lambda t, hf=hf: (mix_out, 4 * hf + t + 1))
        plan_turn("ffn", NT, KD)
        for up, down in FFN_ORDER:
            if up is not None:
                for s in range(4):
                    plan_wide(f"up.{up}.{s}", 2, lambda j, up=up, s=s: (up_relu, 8 * up + 2 * s + j + 1))
            else:
                for hf in range(2):
                    plan_deep([f"down.{down}.{hf}.0", f"down.{down}.{hf}.1"], f"down.{down}.{hf}",
                              read=lambda t, hf=hf, down=down: (mix_out, 8 + 8 * down + 4 * hf + t + 1))

        def normal2_of(t):
            return normal2[:, t % 2, :]

        def x_ready_after(n):
            return lambda eng, t: eng.wait_ge(x_added, 4 * n)

        def sp_phase2(sp):
            wait_pairs(sp)
            x_view = w["x"][0].rearrange("(t p) d -> p t d", p=P)
            for t in range(NT):
                sp.dma_start(x[:, t, :], x_view[:, t, :]).then_inc(x_in, 16)
            load_slabs(sp, sp_slab, slab_no["up.0.0"])
            for i, name in enumerate(("norm_mix_post", "norm_ffn_post")):
                if i:
                    sp.wait_ge(x_added, 4)
                else:
                    sp.wait_ge(slots_zeroed, 16)
                sp.dma_start(gain_row[:, :], w[name][0:1, :].broadcast_to([P, D])).then_inc(gain_in, 16)
                load_slabs(sp, sp_slab, slab_no[("down.0.0.0", "glu_gate0")[i]] + RAW)

        def wait_pairs(eng):
            for p in (2, 3):
                eng.wait_ge(*step_of("pool", p, "lo"))

        def pe_phase2(pe):
            columns_ready(pe, "attn1")
            wait_pairs(pe)
            for hf in range(2):
                pe_deep(pe, [f"out.{hf}.0", f"out.{hf}.1"], f"mix.{hf}")
            pe_turn(pe, "ffn", normal2_of)
            columns_ready(pe, "ffn")
            for up, down in FFN_ORDER:
                if up is not None:
                    for s in range(4):
                        pe_wide(pe, f"up.{up}.{s}")
                else:
                    pe.wait_ge(up_lo, 8 * down + 8)
                    b = down % 2
                    for hf in range(2):
                        pe_deep(pe, [f"down.{down}.{hf}.0", f"down.{down}.{hf}.1"], f"down.{down}.{hf}",
                                acts=(fhi[:, b, :, :], flo[:, b, :, :]))

        def act_post(act, stage, rows_after):
            for t in range(NT):
                act.wait_ge(mix_out, rows_after + t + 1)
                n = 4 * stage + t
                if t >= 2:
                    act.wait_ge(post_sq, n - 1)
                nc.scalar.activation(scratch2[:, t % 2, :], fsb[:, t, :], ACT.Square, accum_out=psums[:, t:t + 1]).then_inc(post_sq, 1)
            act.wait_ge(post_var, stage + 1)
            nc.scalar.activation(psums[:, 8:12], psums[:, 4:8], ACT.Sqrt).then_inc(post_root, 1)

        def dve_post(dve, steps, stage):
            dve.wait_ge(post_sq, 4 * stage + 4)
            nc.vector.tensor_scalar(psums[:, 4:8], psums[:, 0:4], 1.0 / D, EPS, ALU.mult, ALU.add).then_inc(post_var, 1)
            dve.wait_ge(post_root, stage + 1)
            steps.link(nc.vector.reciprocal(psums[:, 12:16], psums[:, 8:12]))
            dve.wait_ge(gain_in, 16 * (stage + 1))
            dve.wait_ge(x_in, 2 * 16 * NT)
            for t in range(NT):
                steps.link(nc.vector.scalar_tensor_tensor(out=fsb[:, t, :], in0=fsb[:, t, :], scalar=psums[:, 12 + t:13 + t],
                                                          in1=gain_row[:, :], op0=ALU.mult, op1=ALU.mult))
                nc.vector.tensor_tensor(x[:, t, :], x[:, t, :], fsb[:, t, :], ALU.add).then_inc(x_added, 1)

        def act_phase2(act):
            make_hi(act, act_slab, slab_no["up.0.0"] + SPLIT)
            act_post(act, 0, 4)
            act_squares(act, "ffn", lambda t: x[:, t, :], x_ready_after(1), scratch2, sums2)
            act_columns(act, "ffn", scaled2, ahi)
            for up, down in FFN_ORDER:
                if up is not None:
                    for s in range(4):
                        name = f"up.{up}.{s}"
                        make_hi(act, act_slab, slab_no[name] + 1 + SPLIT)
                        for j in range(2):
                            m = 2 * s + j
                            n = 8 * up + m
                            acc = banks.take(act, f"{name}/{j}")
                            if n >= 2:
                                act.wait_ge(up_sq, n - 1)
                            nc.scalar.activation(relu[:, n % 2, :], acc[:, :], ACT.Relu).then_inc(up_relu, 1)
                            act.wait_ge(up_sq, n + 1)
                            nc.scalar.activation(fhi[:, up % 2, m, :], relu2[:, n % 2, :], ACT.Copy).then_inc(up_hi, 1)
                else:
                    make_hi(act, act_slab, slab_no[f"down.{down}.1.1"] + 1 + SPLIT)
            act_post(act, 1, 8 + 24 + 4)

        def dve_phase2(dve, steps):
            for hf in range(2):
                for t in range(NT):
                    acc = banks.take(dve, f"mix.{hf}/{t}")
                    nc.vector.tensor_copy(fsb[:, t, hf * 512:(hf + 1) * 512], acc[:, :]).then_inc(mix_out, 1)
            dve_post(dve, steps, 0)
            dve_rows(dve, steps, "ffn", lambda t: x[:, t, :], x_ready_after(1), sums2, normal2_of, "norm_ffn_pre", scaled2)
            for up, down in FFN_ORDER:
                if up is not None:
                    for m in range(8):
                        n = 8 * up + m
                        dve.wait_ge(up_relu, n + 1)
                        if n >= 2:
                            dve.wait_ge(up_lo, n - 1)
                        nc.vector.tensor_tensor(relu2[:, n % 2, :], relu[:, n % 2, :], relu[:, n % 2, :], ALU.mult).then_inc(up_sq, 1)
                else:
                    for hf in range(2):
                        for t in range(NT):
                            acc = banks.take(dve, f"down.{down}.{hf}/{t}")
                            to = fsb[:, t, hf * 512:(hf + 1) * 512]
                            if down == 0:
                                ins = nc.vector.tensor_copy(to, acc[:, :])
                            else:
                                dve.wait_ge(mix_out, 8 + 8 * (down - 1) + 4 * hf + t + 1)
                                ins = nc.vector.tensor_tensor(to, to, acc[:, :], ALU.add)
                            ins.then_inc(mix_out, 1)
            dve_post(dve, steps, 1)

        def pool_phase2(pool, steps):
            make_lo(pool, pool_slab, slab_no["up.0.0"] + SPLIT)
            pool_columns(pool, "ffn", scaled2, ahi, alo)
            for up, down in FFN_ORDER:
                if up is not None:
                    for s in range(4):
                        make_lo(pool, pool_slab, slab_no[f"up.{up}.{s}"] + 1 + SPLIT)
                        for j in range(2):
                            m = 2 * s + j
                            n = 8 * up + m
                            pool.wait_ge(up_hi, n + 1)
                            nc.gpsimd.tensor_tensor(flo[:, up % 2, m, :], relu2[:, n % 2, :],
                                                    fhi[:, up % 2, m, :].bitcast(F32), ALU.subtract).then_inc(up_lo, 1)
                else:
                    make_lo(pool, pool_slab, slab_no[f"down.{down}.1.1"] + 1 + SPLIT)

        put = phase(after_x)
        r1 = put.at[0]
        sig_glu = put("sig_glu", [P, KH, T])
        u_glu = put("u_glu", [P, KH, PAD + T])
        r2 = put.at[0]
        conv = put("conv", [P, KH, T])
        conv_sq = put("conv_sq", [P, KH, T])
        r3 = put.at[0]
        uhi = put("u_hi", [P, KH, T], F32R)
        ulo = put("u_lo", [P, KH, T], F32R)
        r4 = put.at[0]
        fq, fk = (put(n, [P, KH, T]) for n in ("fq_t", "fk_t"))
        r4b = put.at[0]
        fv = put("fv_rows", [P, NT, H])
        crstd = put("conv_rstd", [P, T])
        silu = put("conv_silu", [P, 2, T])
        forget = put("forget", [NHEAD, 4, T])
        ones8 = put("ones8", [NHEAD, T])
        minus8 = put("minus8", [NHEAD, NHEAD, P])
        sums3 = put("sums3", [P, 16])
        put = phase(r1)
        masked3 = put("masked3", [P, 2, T])
        probs3 = put("probs3", [P, 2, T])
        probst3 = put("probst3", [P, 2, T])
        peaks3 = put("peaks3", [P, 64])
        esum3 = put("esum3", [P, 32])
        gated = put("gated", [P, 2, T])
        assert put.at[0] <= r2
        heads3 = sb("heads3", [P, NT, H], at=r2 + KH * T * 4)
        merged = sb("merged", [P, KD, T], at=r2)
        normal3 = sb("normal3", [P, 2, D], at=r3)
        scratch3 = sb("scratch3", [P, 2, D], at=r3 + 8192)
        scaled3 = sb("scaled3", [P, 2, T], at=r4)
        ohi = sb("o_hi", [P, KH, T], F32R, at=r4)
        olo = sb("o_lo", [P, KH, T], F32R, at=r4 + 8192)
        scaled3o = sb("scaled3o", [P, 2, T], at=r1)
        sig_gate = sb("sig_gate", [P, KH, T], at=r4b)

        glu_gate = sem("glu_gate")
        glu_u = sem("glu_u")
        pads = sem("glu_pads")
        fox_in = sem("fox_in")
        forget_in = sem("forget_in")
        forget_dve = sem("forget_dve")
        forget_act = sem("forget_act")
        conv_made = sem("conv_made")
        conv_dev = sem("conv_dev")
        conv_dev2 = sem("conv_dev2")
        conv_sd = sem("conv_sd")
        conv_norm = sem("conv_norm")
        conv_silu = sem("conv_silu_made")
        conv_hi = sem("conv_hi")
        conv_lo = sem("conv_lo")
        gate_sig = sem("gate_sig")
        merged_made = sem("merged_made")
        gated_made = sem("gated_made")
        merged_hi = sem("merged_hi")
        merged_lo = sem("merged_lo")

        plan_turn("mix2", NT, KD)
        for s in range(2):
            plan_wide(f"glu_gate{s}", 2, lambda j, s=s: (glu_gate, 2 * s + j + 1))
        for s in range(2):
            plan_wide(f"glu_a{s}", 2, lambda j, s=s: (glu_u, 2 * s + j + 1))
        for s in range(4):
            plan_wide(("fq0", "fq1", "fk0", "fk1")[s], 2, lambda j, s=s: (fox_in, 2 * s + j + 1))
        plan_deep(["fv0", "fv1"], "fv", read=lambda t: (fox_in, 9 + t))
        plan_wide("ff0", 1, lambda j: (forget_in, 1))
        banks.plan("conv_mean", (conv_dev, KH))
        banks.plan("conv_var", (conv_sd, 1))
        in_turn(attn_units("fox", NHEAD, lambda t: (t + 1) * P))
        plan_turn("foxo", NT, KH, normalise=False)
        for g, (gate_name, val_name) in enumerate((("gc", "pw"), ("ga", "ab"))):
            for hf in range(2):
                for s in range(2):
                    plan_wide(f"{gate_name}.{hf}.{s}", 2, lambda j, g=g, hf=hf, s=s: (gate_sig, 8 * g + 4 * hf + 2 * s + j + 1))
                plan_wide(f"{val_name}.{hf}.0", 4, lambda j, g=g, hf=hf: ((merged_made, gated_made)[g], 4 * hf + j + 1))
        plan_deep(["out2.0.0", "out2.0.1"], "mix2.0", read=lambda t: (x_added, 8 + t + 1))
        plan_turn("mem", NMT, KD)
        plan_deep(["out2.1.0", "out2.1.1"], "mix2.1", read=lambda t: (x_added, 12 + t + 1))

        def normal3_of(t):
            return normal3[:, t % 2, :]

        def sp_phase3(sp):
            load_slabs(sp, sp_slab, slab_no["out2.1.1"] + 1)

        def pe_phase3(pe):
            pe_turn(pe, "mix2", normal3_of)
            columns_ready(pe, "mix2")
            for n in ("glu_gate0", "glu_gate1", "glu_a0", "glu_a1", "fq0", "fq1", "fk0", "fk1"):
                pe_wide(pe, n)
            pe_deep(pe, ["fv0", "fv1"], "fv")
            pe_wide(pe, "ff0")
            pe.wait_ge(conv_made, KH)
            acc = banks.open(pe, "conv_mean")
            for m in range(KH):
                ins = nc.tensor.matmul(acc[:, :], const("chan_mean"), conv[:, m, :], start=m == 0, stop=m == KH - 1)
            banks.filled(ins, "conv_mean")
            pe.wait_ge(conv_dev2, KH)
            acc = banks.open(pe, "conv_var")
            for m in range(KH):
                ins = nc.tensor.matmul(acc[:, :], const("chan_mean"), conv_sq[:, m, :], start=m == 0, stop=m == KH - 1)
            banks.filled(ins, "conv_var")
            pe.wait_ge(fox_in, 12)
            pe.wait_ge(forget_dve, 6)
            in_turn(pe_attn(pe, "fox",
                            lambda h, t: fq[half(h % 2), h // 2, t * P:(t + 1) * P], lambda h, n: fk[half(h % 2), h // 2, 0:n],
                            lambda h, b: fv[:, b, half(h)], probs3, probst3,
                            bias=(lambda h: minus8[:, h, :], lambda n: forget[:, 3, 0:n])))
            pe_turn(pe, "foxo", lambda t: heads3[:, t, :], fox_heads_ready)
            pe.wait_ge(conv_lo, KH)
            for hf in range(2):
                for s in range(2):
                    pe_wide(pe, f"gc.{hf}.{s}")
                pe_wide(pe, f"pw.{hf}.0", acts=(uhi, ulo))
            columns_ready(pe, "foxo")
            for hf in range(2):
                for s in range(2):
                    pe_wide(pe, f"ga.{hf}.{s}")
                pe_wide(pe, f"ab.{hf}.0", acts=(ohi, olo))
            pe.wait_ge(merged_lo, KD)
            pe_deep(pe, ["out2.0.0", "out2.0.1"], "mix2.0")
            pe_turn(pe, "mem", lambda t: normal4m[:, t, :])
            pe_deep(pe, ["out2.1.0", "out2.1.1"], "mix2.1")

        def fox_heads_ready(eng, t):
            eng.wait_ge(heads_out, attns["fox"]["base"] + len(attns["fox"]["items"]))

        def act_phase3(act):
            act_squares(act, "mix2", lambda t: x[:, t, :], x_ready_after(2), scratch3, sums3)
            act_columns(act, "mix2", scaled3, ahi)
            for s in range(2):
                make_hi(act, act_slab, slab_no[f"glu_gate{s}"] + 1 + SPLIT)
                for j in range(2):
                    acc = banks.take(act, f"glu_gate{s}/{j}")
                    nc.scalar.activation(sig_glu[:, 2 * s + j, :], acc[:, :], ACT.Sigmoid).then_inc(glu_gate, 1)
            for s in range(2):
                make_hi(act, act_slab, slab_no[f"glu_a{s}"] + 1 + SPLIT)
            for s, n in enumerate(("fq0", "fq1", "fk0", "fk1")):
                make_hi(act, act_slab, slab_no[n] + 1 + SPLIT)
                for j in range(2):
                    acc = banks.take(act, f"{n}/{j}")
                    nc.scalar.activation((fq, fk)[s // 2][:, 2 * (s % 2) + j, :], acc[:, :], ACT.Copy).then_inc(fox_in, 1)
            make_hi(act, act_slab, slab_no["fv1"] + 1 + SPLIT)
            for t in range(NT):
                acc = banks.take(act, f"fv/{t}")
                nc.scalar.activation(fv[:, t, :], acc[:, :], ACT.Copy).then_inc(fox_in, 1)
            make_hi(act, act_slab, slab_no["ff0"] + 1 + SPLIT)
            act.wait_ge(forget_dve, 3)
            nc.scalar.activation(forget[:, 1, :], forget[:, 1, :], ACT.Exp, scale=-1.0).then_inc(forget_act, 1)
            act.wait_ge(forget_act, 1)
            nc.scalar.activation(forget[:, 1, :], forget[:, 1, :], ACT.Ln, bias=const("ones")[0:NHEAD, 0:1]).then_inc(forget_act, 1)
            for m in range(KH):
                act.wait_ge(conv_dev, m + 1)
                nc.scalar.activation(conv_sq[:, m, :], conv[:, m, :], ACT.Square).then_inc(conv_dev2, 1)
            acc = banks.take(act, "conv_var")
            nc.scalar.activation(crstd[:, :], acc[:, :], ACT.Sqrt, bias=const("eps")[:, 0:1]).then_inc(conv_sd, 1)
            for m in range(KH):
                act.wait_ge(conv_norm, m + 1)
                if m >= 2:
                    act.wait_ge(conv_lo, m - 1)
                nc.scalar.activation(silu[:, m % 2, :], conv[:, m, :], ACT.Silu, bias=col("conv_ln_b_2", m)).then_inc(conv_silu, 1)
                act.wait_ge(conv_silu, m + 1)
                nc.scalar.activation(uhi[:, m, :], silu[:, m % 2, :], ACT.Copy).then_inc(conv_hi, 1)
            in_turn(act_attn(act, "fox", masked3, peaks3, esum3, probs3, probst3))
            act_columns(act, "foxo", scaled3o, ohi)
            for g, (gate_name, val_name) in enumerate((("gc", "pw"), ("ga", "ab"))):
                for hf in range(2):
                    for s in range(2):
                        make_hi(act, act_slab, slab_no[f"{gate_name}.{hf}.{s}"] + 1 + SPLIT)
                        for j in range(2):
                            n = 8 * g + 4 * hf + 2 * s + j
                            acc = banks.take(act, f"{gate_name}.{hf}.{s}/{j}")
                            if n >= 4:
                                act.wait_ge(merged_made, n - 3)
                            nc.scalar.activation(sig_gate[:, 2 * s + j, :], acc[:, :], ACT.Sigmoid).then_inc(gate_sig, 1)
                    make_hi(act, act_slab, slab_no[f"{val_name}.{hf}.0"] + 1 + SPLIT)
            for m in range(KD):
                act.wait_ge(merged_made, 9 + m)
                if m == 0:
                    banks.take(act, "ab.1.0/0")
                nc.scalar.activation(ahi[:, m, :], merged[:, m, :], ACT.Copy).then_inc(merged_hi, 1)

        def dve_phase3(dve, steps):
            dve_rows(dve, steps, "mix2", lambda t: x[:, t, :], x_ready_after(2), sums3, normal3_of, "norm_mix_g_2", scaled3)
            for m in range(KH):
                acc = banks.take(dve, f"glu_a{m // 2}/{m % 2}")
                dve.wait_ge(glu_gate, m + 1)
                nc.vector.tensor_tensor(u_glu[:, m, PAD:PAD + T], acc[:, :], sig_glu[:, m, :], ALU.mult).then_inc(glu_u, 1)
            dve.wait_ge(pads, 1)
            dve.wait_ge(glu_u, KH)
            before = [0] * KH
            for m in range(KH):
                before[m] = steps.mark(nc.vector.tensor_scalar(conv[:, m, :], u_glu[:, m, 0:T], col("conv_dw_w_2", m),
                                                               col("conv_dw_b_2", m), ALU.mult, ALU.add))
            for j in range(1, TAPS):
                for m in range(KH):
                    steps.after(before[m])
                    ins = nc.vector.scalar_tensor_tensor(out=conv[:, m, :], in0=u_glu[:, m, j:j + T],
                                                         scalar=col("conv_dw_w_2", KH * j + m), in1=conv[:, m, :],
                                                         op0=ALU.mult, op1=ALU.add)
                    if j < TAPS - 1:
                        before[m] = steps.mark(ins)
                    else:
                        ins.then_inc(conv_made, 1)
            acc = banks.take(dve, "ff0/0")
            nc.vector.tensor_scalar(forget[:, 0, :], acc[0:NHEAD, :], col("fox_bf_2")[0:NHEAD, :], None, ALU.add).then_inc(forget_in, 1)
            nc.vector.tensor_scalar(minus8[:, :, :], ident[0:NHEAD, 0:NHEAD].unsqueeze(2).broadcast_to([NHEAD, NHEAD, P]),
                                    -float(HD) ** 0.5, None, ALU.mult).then_inc(forget_dve, 1)
            dve.wait_ge(forget_in, 1)
            nc.vector.tensor_scalar(forget[:, 2, :], forget[:, 0, :], 0.0, None, ALU.min).then_inc(forget_dve, 1)
            dve.wait_ge(forget_dve, 2)
            nc.vector.scalar_tensor_tensor(out=forget[:, 1, :], in0=forget[:, 2, :], scalar=-2.0, in1=forget[:, 0, :],
                                           op0=ALU.mult, op1=ALU.add).then_inc(forget_dve, 1)
            acc = banks.take(dve, "conv_mean")
            for m in range(KH):
                nc.vector.tensor_tensor(conv[:, m, :], conv[:, m, :], acc[:, :], ALU.subtract).then_inc(conv_dev, 1)
            dve.wait_ge(forget_act, 2)
            nc.vector.memset(ones8[:, :], 1.0).then_inc(forget_dve, 1)
            nc.vector.tensor_tensor(forget[:, 0, :], forget[:, 2, :], forget[:, 1, :], ALU.subtract).then_inc(forget_dve, 1)
            dve.wait_ge(forget_dve, 5)
            nc.vector.tensor_tensor_scan(forget[:, 3, :], ones8[:, :], forget[:, 0, :], 0.0, ALU.mult, ALU.add).then_inc(forget_dve, 1)
            dve.wait_ge(conv_sd, 1)
            steps.link(nc.vector.reciprocal(crstd[:, :], crstd[:, :]))
            dve.wait_ge(conv_dev, KH)
            for m in range(KH):
                nc.vector.scalar_tensor_tensor(out=conv[:, m, :], in0=conv[:, m, :], scalar=col("conv_ln_g_2", m), in1=crstd[:, :],
                                               op0=ALU.mult, op1=ALU.mult).then_inc(conv_norm, 1)
            in_turn(dve_attn(dve, steps, "fox", HD ** -0.5, const("band_causal"), masked3, peaks3, esum3,
                             lambda h, t: heads3[:, t, half(h)]))
            for t in range(NT):
                dve_columns(dve, "foxo", t, None, scaled3o)
            for g, val_name in enumerate(("pw", "ab")):
                for m in range(KD):
                    n = 8 * g + m
                    unit = f"{val_name}.{m // 4}.0/{m % 4}"
                    acc = banks.take(dve, unit)
                    dve.wait_ge(gate_sig, n + 1)
                    if g == 0:
                        ins = nc.vector.tensor_tensor(merged[:, m, :], acc[:, :], sig_gate[:, m % 4, :], ALU.mult)
                        ins.then_inc(merged_made, 1)
                    else:
                        if m >= 2:
                            dve.wait_ge(merged_made, KD + m - 1)
                        nc.vector.tensor_tensor(gated[:, m % 2, :], acc[:, :], sig_gate[:, m % 4, :], ALU.mult).then_inc(gated_made, 1)
                        dve.wait_ge(gated_made, m + 1)
                        dve.wait_ge(merged_made, m + 1)
                        nc.vector.tensor_tensor(merged[:, m, :], merged[:, m, :], gated[:, m % 2, :], ALU.add).then_inc(merged_made, 1)
            dve_rows(dve, steps, "mem", lambda t: mem_rows[:, t, :], mem_ready, sums4m, lambda t: normal4m[:, t, :], "norm_mem_g_2", scaled4)
            for hf in range(2):
                for t in range(NT):
                    acc = banks.take(dve, f"mix2.{hf}/{t}")
                    to = x[:, t, hf * 512:(hf + 1) * 512]
                    nc.vector.tensor_tensor(to, to, acc[:, :], ALU.add).then_inc(x_added, 1)

        def pool_phase3(pool, steps):
            pool_columns(pool, "mix2", scaled3, ahi, alo)
            pool.wait_ge(cols_lo, turns["mix2"]["split"] + 2 * NT)
            nc.gpsimd.memset(u_glu[:, :, 0:PAD], 0.0).then_inc(pads, 1)
            make_lo(pool, pool_slab, slab_no["ff0"] + 1 + SPLIT)
            for m in range(KH):
                pool.wait_ge(conv_hi, m + 1)
                nc.gpsimd.tensor_tensor(ulo[:, m, :], silu[:, m % 2, :], uhi[:, m, :].bitcast(F32), ALU.subtract).then_inc(conv_lo, 1)
            pool_columns(pool, "foxo", scaled3o, ohi, olo)
            make_lo(pool, pool_slab, slab_no["ab.1.0"] + 1 + SPLIT)
            for m in range(KD):
                pool.wait_ge(merged_hi, m + 1)
                nc.gpsimd.tensor_tensor(alo[:, m, :], merged[:, m, :], ahi[:, m, :].bitcast(F32), ALU.subtract).then_inc(merged_lo, 1)

        put = phase(after_x)
        scaled4 = put("scaled4", [P, 2, T])
        mem_rows = put("mem_rows", [P, NMT, D])
        scratch4 = put("scratch4", [P, 2, D])
        normal4 = put("normal4", [P, 2, D])
        normal4m = put("normal4m", [P, NMT, D])
        mhi = put("mem_hi", [P, KD, MEM], F32R)
        mlo = put("mem_lo", [P, KD, MEM], F32R)
        kx = put("kx_t", [P, XH, MEM])
        vx = put("vx_rows", [P, NMT, H])
        qx = put("qx_t", [P, XH, T])
        masked4 = put("masked4", [P, 2, MEM])
        probs4 = put("probs4", [P, 2, MEM])
        probst4 = put("probst4", [P, 2, MEM])
        sums4m = put("sums4m", [P, 16])
        sums4 = put("sums4", [P, 16])
        peaks4 = put("peaks4", [P, 64])
        esum4 = put("esum4", [P, 32])
        heads4 = sb("heads4", [P, NT, H], at=act_at)
        xohi = sb("xo_hi", [P, KH, T], F32R, at=act_at + 8192)
        xolo = sb("xo_lo", [P, KH, T], F32R, at=act_at + 16384)

        mem_in = sem("mem_in")
        cross_in = sem("cross_in")

        for s in range(2):
            plan_wide(f"xk{s}", 2, lambda j, s=s: (cross_in, 2 * s + j + 1))
        plan_deep(["xv0", "xv1"], "xv", NMT, lambda t: (cross_in, 5 + t))
        plan_turn("xa", NT, KD)
        for s in range(2):
            plan_wide(f"xq{s}", 2, lambda j, s=s: (cross_in, 7 + 2 * s + j))
        in_turn(attn_units("xa", XH, lambda t: MEM))
        plan_turn("xao", NT, KH, normalise=False)
        for hf in range(2):
            plan_deep([f"xo.{hf}.0"], f"xo.{hf}", read=lambda t, hf=hf: (x_added, 16 + 4 * hf + t + 1))

        def mem_ready(eng, t):
            eng.wait_ge(mem_in, 16 * NMT)

        def normal4_of(t):
            return normal4[:, t % 2, :]

        def cross_heads_ready(eng, t):
            eng.wait_ge(heads_out, attns["xa"]["base"] + len(attns["xa"]["items"]))

        def sp_phase4(sp):
            sp.wait_ge(merged_lo, KD)
            mem_view = w["mem_2"][0].rearrange("(t p) d -> p t d", p=P)
            for t in range(NMT):
                sp.dma_start(mem_rows[:, t, :], mem_view[:, t, :]).then_inc(mem_in, 16)
            load_slabs(sp, sp_slab, len(slabs))

        def pe_phase4(pe):
            columns_ready(pe, "mem")
            for s in range(2):
                pe_wide(pe, f"xk{s}", tokens=MEM, acts=(mhi, mlo))
            pe_deep(pe, ["xv0", "xv1"], "xv", tiles=NMT, acts=(mhi, mlo))
            pe_turn(pe, "xa", normal4_of)
            columns_ready(pe, "xa")
            for s in range(2):
                pe_wide(pe, f"xq{s}")
            pe.wait_ge(cross_in, 10)
            in_turn(pe_attn(pe, "xa", lambda h, t: qx[:, h, t * P:(t + 1) * P], lambda h, n: kx[:, h, 0:n],
                            lambda h, b: vx[:, b, h * XHD:(h + 1) * XHD], probs4, probst4))
            pe_turn(pe, "xao", lambda t: heads4[:, t, :], cross_heads_ready)
            columns_ready(pe, "xao")
            for hf in range(2):
                pe_deep(pe, [f"xo.{hf}.0"], f"xo.{hf}", acts=(xohi, xolo))

        def act_phase4(act):
            act_squares(act, "mem", lambda t: mem_rows[:, t, :], mem_ready, scratch4, sums4m)
            make_hi(act, act_slab, slab_no["out2.1.1"] + 1)
            act_columns(act, "mem", scaled4, mhi)
            make_hi(act, act_slab, slab_no["xk1"] + 1)
            act_squares(act, "xa", lambda t: x[:, t, :], x_ready_after(4), scratch4, sums4)
            for s in range(2):
                make_hi(act, act_slab, slab_no[f"xk{s}"] + 1 + SPLIT)
                for j in range(2):
                    acc = banks.take(act, f"xk{s}/{j}")
                    nc.scalar.activation(kx[:, 2 * s + j, :], acc[:, 0:MEM], ACT.Copy).then_inc(cross_in, 1)
            make_hi(act, act_slab, slab_no["xv1"] + 1 + SPLIT)
            for t in range(NMT):
                acc = banks.take(act, f"xv/{t}")
                nc.scalar.activation(vx[:, t, :], acc[:, :], ACT.Copy).then_inc(cross_in, 1)
            act_columns(act, "xa", scaled4, ahi)
            for s in range(2):
                make_hi(act, act_slab, slab_no[f"xq{s}"] + 1 + SPLIT)
                for j in range(2):
                    acc = banks.take(act, f"xq{s}/{j}")
                    nc.scalar.activation(qx[:, 2 * s + j, :], acc[:, :], ACT.Copy).then_inc(cross_in, 1)
            in_turn(act_attn(act, "xa", masked4, peaks4, esum4, probs4, probst4))
            act_columns(act, "xao", scaled4, xohi)

        def dve_phase4(dve, steps):
            dve_rows(dve, steps, "xa", lambda t: x[:, t, :], x_ready_after(4), sums4, normal4_of, "norm_xa_g_2", scaled4)
            in_turn(dve_attn(dve, steps, "xa", XHD ** -0.5, None, masked4, peaks4, esum4,
                             lambda h, t: heads4[:, t, h * XHD:(h + 1) * XHD]))
            for t in range(NT):
                dve_columns(dve, "xao", t, None, scaled4)
            for hf in range(2):
                for t in range(NT):
                    acc = banks.take(dve, f"xo.{hf}/{t}")
                    to = x[:, t, hf * 512:(hf + 1) * 512]
                    nc.vector.tensor_tensor(to, to, acc[:, :], ALU.add).then_inc(x_added, 1)

        def pool_phase4(pool, steps):
            make_lo(pool, pool_slab, slab_no["out2.1.1"] + 1)
            pool_columns(pool, "mem", scaled4, mhi, mlo)
            make_lo(pool, pool_slab, slab_no["xv1"] + 1 + SPLIT)
            pool_columns(pool, "xa", scaled4, ahi, alo)
            make_lo(pool, pool_slab, len(slabs))
            pool_columns(pool, "xao", scaled4, xohi, xolo)

        put = phase(after_x)
        hn = put("hn_rows", [P, NT, D])
        scratch5 = put("scratch5", [P, 2, D])
        h_t = put("h_cols", [P, KD, T])
        sums5 = put("sums5", [P, 16])
        router_w = put("router_w", [P, KD, NG + NE])
        router_b = put("router_b", [P, NG + NE])
        logits = put("logits", [P, NT, NG + NE])
        small4 = put("small4", [P, 12, NT])
        group16 = put("group16", [P, 8, NT, EPG])
        by_expert = put("by_expert", [P, 4, NT, NG, EPG])
        edges = put("edges", [P, NE, 3])
        expert16 = put("expert16", [P, 5, NE])
        later = put("later_tiles", [P, EXTRA, NE])
        later_sum = put("later_sum", [P, 8])
        later_expert = put("later_expert", [P, 8], I32)
        slot_f = put("slot_f", [P, TOPK, NT])
        slot = put("slot", [P, TOPK, NT], I32)
        weight = put("weight", [P, TOPK, NT])
        rows = put("expert_rows", [P, 2, D])
        silu5 = put("expert_silu", [P, 2, EF])
        hidden = put("expert_hidden", [P, 2, EF])
        hidden_t = put("expert_hidden_t", [P, 2, EF])
        down_w = sb("expert_down", [P, 2, EF // P, D], at=ring_at)
        x_t = sb("expert_x_t", [P, 2, KD, P], at=ring_at + 16384)
        y_rows = sb("expert_y", [P, 2, D], at=ring_at + 24576)
        gate_up = sb("expert_gate_up", [P, 2, KD, 2 * EF], at=act_at)
        y_pair = sb("y_pair", [P, NT, TOPK, D], at=after_x)
        final_sq = sb("final_sq", [P, 2, D], at=act_at)
        out_rows = sb("out_rows", [P, NT, D], at=act_at + 8192)

        slots_dram = nc.dram_tensor("expert_rows_dram", (SLOTS, D), F32, kind="Internal").ap()
        y_dram = nc.dram_tensor("expert_y_dram", (SLOTS, D), F32, kind="Internal").ap()

        router_in = sem("router_in")
        slots_zeroed = sem("slots_zeroed")
        zeros_made = sem("zeros_made")
        logits_made = sem("logits_made")
        route_exp_in = sem("route_exp_in")
        route_exps = sem("route_exps")
        picks_made = sem("picks_made")
        slots_made = sem("slots_made")
        weights_made = sem("weights_made")
        rows_placed = sem("rows_placed")
        y_gathered = sem("y_gathered")
        y_sums = sem("y_sums")
        final_squares = sem("final_squares")
        final_var = sem("final_var")
        final_root = sem("final_root")
        final_rows = sem("final_rows")
        out_stored = sem("out_stored")

        def two(name):
            return [sem(f"{name}{s}") for s in range(2)]

        gate_up_in, down_in, rows_in = two("gate_up_in"), two("down_in"), two("rows_in")
        rows_turned = two("rows_turned")
        x_t_made = two("x_t_made")
        gate_up_made = two("gate_up_made")
        silu_made = two("silu_made")
        hidden_made = two("hidden_made")
        hidden_turned = two("hidden_turned")
        hidden_t_made = two("hidden_t_made")
        y_made = two("y_made")
        y_left = two("y_left")
        y_right = two("y_right")
        y_stored = two("y_stored")

        plan_turn("moe", NT, KD, split=False)
        banks.plan("logits", (logits_made, 1))
        banks.plan("ranks", (slots_made, 1))
        TURN_BANKS, GATE_UP_BANKS, HIDDEN_BANKS, Y_BANKS = ([banks.banks[2 * i], banks.banks[2 * i + 1]] for i in range(4))

        def hn_of(t):
            return hn[:, t, :]

        def unless_first(eng, sem_, n):
            if not isinstance(n, int) or n > 0:
                eng.wait_ge(sem_, n)

        def turn_rows(pe, r, s):
            pe.wait_ge(rows_in[s], 16 * (r + 1))
            unless_first(pe, x_t_made[1 - s], 2 * (r + s))
            for h in range(2):
                for j in range(4):
                    c = (4 * h + j) * P
                    ins = nc.tensor.transpose(TURN_BANKS[h][:, j * P:(j + 1) * P], rows[:, s, c:c + P], ident)
            ins.then_inc(rows_turned[s], 1)

        def pe_gate_up(pe, r, s):
            pe.wait_ge(x_t_made[s], 2 * (r + 1))
            pe.wait_ge(gate_up_in[s], 32 * (r + 1))
            unless_first(pe, hidden_made[s], r)
            for k in range(KD):
                ins = nc.tensor.matmul(GATE_UP_BANKS[s][:, :], x_t[:, s, k, :], gate_up[:, s, k, :], start=k == 0, stop=k == KD - 1)
            ins.then_inc(gate_up_made[s], 1)

        def turn_hidden(pe, r, s):
            pe.wait_ge(hidden_made[s], r + 1)
            unless_first(pe, hidden_t_made[s], r)
            for j in range(EF // P):
                ins = nc.tensor.transpose(HIDDEN_BANKS[s][:, j * P:(j + 1) * P], hidden[:, s, j * P:(j + 1) * P], ident)
            ins.then_inc(hidden_turned[s], 1)

        def pe_down(pe, r, s):
            pe.wait_ge(hidden_t_made[s], r + 1)
            pe.wait_ge(down_in[s], 16 * (r + 1))
            unless_first(pe, y_left[1 - s], r + s)
            unless_first(pe, y_right[1 - s], r + s)
            for k in range(EF // P):
                for h in range(2):
                    ins = nc.tensor.matmul(Y_BANKS[h][:, :], hidden_t[:, s, k * P:(k + 1) * P], down_w[:, s, k, h * 512:(h + 1) * 512],
                                           start=k == 0, stop=k == EF // P - 1)
            ins.then_inc(y_made[s], 1)

        def pe_step(pe, r, s, last=False):
            before, after = (r - 1 + s, 1 - s), (r + s, 1 - s)
            pe_gate_up(pe, r, s)
            turn_hidden(pe, *before)
            if not last:
                turn_rows(pe, *after)
            pe_down(pe, *before)

        def pe_phase5(pe):
            pe_turn(pe, "moe", hn_of)
            pe.wait_ge(cols_scaled, turns["moe"]["unit"] + 2 * NT)
            pe.wait_ge(router_in, 64)
            acc = banks.open(pe, "logits")
            for t in range(NT):
                for k in range(KD):
                    ins = nc.tensor.matmul(acc[:, t * (NG + NE):(t + 1) * (NG + NE)], h_t[:, k, t * P:(t + 1) * P], router_w[:, k, :],
                                           start=k == 0, stop=k == KD - 1)
            banks.filled(ins, "logits")
            pe.wait_ge(picks_made, 3)
            acc = banks.open(pe, "ranks")
            picks = by_expert[:, 2, :, :, :].rearrange("p t g e -> p t (g e)")
            for t in range(NT + 1):
                to = acc[:, t * NE:(t + 1) * NE]
                for b in range(t):
                    ins = nc.tensor.matmul(to, const("ones"), picks[:, b, :], start=b == 0, stop=t == NT and b == t - 1)
                if t < NT:
                    ins = nc.tensor.matmul(to, const("before"), picks[:, t, :], start=t == 0, stop=True)
            banks.filled(ins, "ranks")
            turn_rows(pe, 0, 0)
            pe_gate_up(pe, 0, 0)
            turn_rows(pe, 0, 1)
            pe_step(pe, 0, 1)
            pe_step(pe, 1, 0)
            with pe.Fori(1, PAIRS - 1) as r:
                pe_step(pe, r, 1)
                pe_step(pe, r + 1, 0)
            pe_step(pe, PAIRS - 1, 1)
            pe_step(pe, PAIRS, 0, last=True)
            turn_hidden(pe, PAIRS, 0)
            pe_down(pe, PAIRS, 0)

        def act_tile(act, r, s):
            act.wait_ge(gate_up_made[s], r + 1)
            unless_first(act, hidden_made[s], r)
            nc.scalar.activation(silu5[:, s, :], GATE_UP_BANKS[s][:, 0:EF], ACT.Silu).then_inc(silu_made[s], 1)
            act.wait_ge(hidden_turned[s], r + 1)
            unless_first(act, y_made[s], r)
            nc.scalar.activation(hidden_t[:, s, :], HIDDEN_BANKS[s][:, 0:EF], ACT.Copy).then_inc(hidden_t_made[s], 1)
            act.wait_ge(y_made[s], r + 1)
            unless_first(act, y_stored[s], 16 * r)
            nc.scalar.activation(y_rows[:, s, 512:1024], Y_BANKS[1][:, :], ACT.Copy).then_inc(y_right[s], 1)

        def act_phase5(act):
            act_squares(act, "moe", lambda t: x[:, t, :], x_ready_after(6), scratch5, sums5)
            act.wait_ge(route_exp_in, 1)
            nc.scalar.activation(group16[:, 1, :, :], group16[:, 0, :, :], ACT.Exp).then_inc(route_exps, 1)
            act.wait_ge(route_exp_in, 2)
            nc.scalar.activation(small4[:, 4, :], small4[:, 3, :], ACT.Exp).then_inc(route_exps, 1)
            act_tile(act, 0, 0)
            act_tile(act, 0, 1)
            with act.Fori(1, PAIRS) as r:
                act_tile(act, r, 0)
                act_tile(act, r, 1)
            act_tile(act, PAIRS, 0)
            for t in range(NT):
                act.wait_ge(y_sums, 2 * t + 2)
                if t >= 2:
                    act.wait_ge(final_squares, t - 1)
                nc.scalar.activation(final_sq[:, t % 2, :], x[:, t, :], ACT.Square, accum_out=sums5[:, t:t + 1]).then_inc(final_squares, 1)
            act.wait_ge(final_var, 1)
            nc.scalar.activation(sums5[:, 8:12], sums5[:, 4:8], ACT.Sqrt).then_inc(final_root, 1)

        def dve_first_max(steps, values, peak, one):
            tt = nc.vector.tensor_tensor
            steps.link(nc.vector.tensor_reduce(peak, values, AX_X, ALU.max))
            steps.link(tt(one, values, peak.unsqueeze(2).broadcast_to([P, NT, 4]), ALU.is_equal))
            steps.link(tt(one, one, const("first4").unsqueeze(1).broadcast_to([P, NT, 4]), ALU.mult))
            top = small4[:, 11, :]
            steps.link(nc.vector.tensor_reduce(top, one, AX_X, ALU.max))
            steps.link(tt(one, one, top.unsqueeze(2).broadcast_to([P, NT, 4]), ALU.is_equal))

        def dve_route(dve, steps):
            tt, stt, tsc, reduce = (nc.vector.tensor_tensor, nc.vector.scalar_tensor_tensor, nc.vector.tensor_scalar,
                                    nc.vector.tensor_reduce)
            acc = banks.take(dve, "logits")
            tt(logits[:, :, :], acc[:, 0:NT * (NG + NE)].rearrange("p (t n) -> p t n", t=NT),
               router_b[:, :].unsqueeze(1).broadcast_to([P, NT, NG + NE]), ALU.add).then_inc(logits_made, 1)
            dve.wait_ge(logits_made, 1)
            g = logits[:, :, 0:NG]
            e = logits[:, :, NG:NG + NE].rearrange("p t (g e) -> p t g e", g=NG)
            g_peak, peak1, peak2, gap, gap_exp, g_sum, den, pw = (small4[:, i, :] for i in range(8))
            g_gap, g_exp, g_one, one1, one2, e_of, e_rest = (group16[:, i, :, :] for i in range(7))
            dve_first_max(steps, g, g_peak, g_one)
            tt(g_gap, g, g_peak.unsqueeze(2).broadcast_to([P, NT, NG]), ALU.subtract).then_inc(route_exp_in, 1)
            over = g_one.unsqueeze(3).broadcast_to([P, NT, NG, EPG])
            steps.link(tt(by_expert[:, 3], e, over, ALU.mult))
            steps.link(reduce(e_of, by_expert[:, 3].rearrange("p t g e -> p t e g"), AX_X, ALU.add))
            dve_first_max(steps, e_of, peak1, one1)
            steps.link(stt(out=e_rest, in0=one1, scalar=NEG, in1=e_of, op0=ALU.mult, op1=ALU.add))
            dve_first_max(steps, e_rest, peak2, one2)
            tt(gap, peak2, peak1, ALU.subtract).then_inc(route_exp_in, 1)
            for k, one in enumerate((one1, one2)):
                tt(by_expert[:, k], over, one.unsqueeze(2).broadcast_to([P, NT, NG, EPG]), ALU.mult).then_inc(picks_made, 1)
            dve.wait_ge(picks_made, 2)
            tt(by_expert[:, 2], by_expert[:, 0], by_expert[:, 1], ALU.add).then_inc(picks_made, 1)
            dve.wait_ge(route_exps, 2)
            steps.link(reduce(g_sum, g_exp, AX_X, ALU.add))
            steps.link(tsc(den, gap_exp, 1.0, None, ALU.add))
            steps.link(tt(den, den, g_sum, ALU.mult))
            steps.link(nc.vector.reciprocal(weight[:, 0, :], den))
            tt(weight[:, 1, :], weight[:, 0, :], gap_exp, ALU.mult).then_inc(weights_made, 1)
            extra, to, start, shift = (expert16[:, i, :] for i in range(4))
            numbers = const("tile_no")
            acc = banks.take(dve, "ranks")
            count = acc[:, NT * NE:(NT + 1) * NE]
            rank = acc[:, 0:NT * NE].rearrange("p (t n) -> p t n", t=NT)
            steps.link(tt(edges[:, :, :], count.unsqueeze(2).broadcast_to([P, NE, 3]),
                          const("tile_edges")[:, 1:4].unsqueeze(1).broadcast_to([P, NE, 3]), ALU.is_gt))
            steps.link(reduce(extra, edges[:, :, :], AX_X, ALU.add))
            steps.link(nc.vector.tensor_tensor_scan(to, const("ones")[:, 0:NE], extra, 0.0, ALU.mult, ALU.add))
            steps.link(tt(start, to, extra, ALU.subtract))
            steps.link(tt(start, start, numbers[:, 0:NE], ALU.subtract))
            steps.link(tsc(shift, start, float(NE - 1), float(P), ALU.add, ALU.mult))
            by = [by_expert[:, i].rearrange("p t g e -> p t (g e)") for i in range(4)]
            steps.link(tsc(by[3], rank, float(P), None, ALU.is_ge))
            steps.link(tt(by[3], by[3], shift.unsqueeze(1).broadcast_to([P, NT, NE]), ALU.mult))
            steps.link(tt(by[3], by[3], rank, ALU.add))
            steps.link(stt(out=by[3], in0=numbers[:, 0:NE].unsqueeze(1).broadcast_to([P, NT, NE]), scalar=float(P), in1=by[3],
                           op0=ALU.mult, op1=ALU.add))
            for k in range(TOPK):
                steps.link(tt(by[k], by[k], by[3], ALU.mult))
                steps.link(reduce(slot_f[:, k, :], by[k], AX_X, ALU.add))
            nc.vector.tensor_copy(slot[:, :, :], slot_f[:, :, :]).then_inc(slots_made, 1)
            steps.link(tt(later[:, :, :], to.unsqueeze(1).broadcast_to([P, EXTRA, NE]),
                          numbers[:, 0:EXTRA].unsqueeze(2).broadcast_to([P, EXTRA, NE]), ALU.is_le))
            steps.link(reduce(later_sum[:, 0:EXTRA], later[:, :, :], AX_X, ALU.add))
            steps.link(tsc(later_sum[:, 0:EXTRA], later_sum[:, 0:EXTRA], float(NE - 1), None, ALU.min))
            nc.vector.tensor_copy(later_expert[:, 0:EXTRA], later_sum[:, 0:EXTRA]).then_inc(slots_made, 1)

        def dve_x_t(dve, r, s):
            dve.wait_ge(rows_turned[s], r + 1)
            unless_first(dve, gate_up_made[s], r)
            for h in range(2):
                nc.vector.tensor_tensor(x_t[:, s, 4 * h:4 * h + 4, :], TURN_BANKS[h][:, :].rearrange("p (j n) -> p j n", j=4),
                                        col("norm_moe_g_2", 4 * h, 4).unsqueeze(2).broadcast_to([P, 4, P]),
                                        ALU.mult).then_inc(x_t_made[s], 1)

        def dve_hidden(dve, r, s):
            dve.wait_ge(silu_made[s], r + 1)
            unless_first(dve, hidden_turned[s], r)
            nc.vector.tensor_tensor(hidden[:, s, :], silu5[:, s, :], GATE_UP_BANKS[s][:, EF:2 * EF], ALU.mult).then_inc(hidden_made[s], 1)

        def dve_y(dve, r, s):
            dve.wait_ge(y_made[s], r + 1)
            unless_first(dve, y_stored[s], 16 * r)
            nc.vector.tensor_copy(y_rows[:, s, 0:512], Y_BANKS[0][:, :]).then_inc(y_left[s], 1)

        def dve_step(dve, r, s, last=False):
            dve_hidden(dve, r, s)
            if not last:
                dve_x_t(dve, r + 1, s)
            dve_y(dve, r, s)

        def dve_phase5(dve, steps):
            dve_rows(dve, steps, "moe", lambda t: x[:, t, :], x_ready_after(6), sums5, hn_of, "norm_moe_g_2", plain=h_t)
            dve_route(dve, steps)
            dve_x_t(dve, 0, 0)
            dve_x_t(dve, 0, 1)
            dve_step(dve, 0, 0)
            dve_step(dve, 0, 1)
            with dve.Fori(1, PAIRS - 1) as r:
                dve_step(dve, r, 0)
                dve_step(dve, r, 1)
            dve_step(dve, PAIRS - 1, 0)
            dve_step(dve, PAIRS - 1, 1, last=True)
            dve_step(dve, PAIRS, 0, last=True)
            for t in range(NT):
                for k in range(TOPK):
                    dve.wait_ge(y_gathered, 16 * TOPK * NT)
                    if k:
                        dve.wait_ge(y_sums, 2 * t + 1)
                    nc.vector.scalar_tensor_tensor(out=x[:, t, :], in0=y_pair[:, t, k, :], scalar=weight[:, k, t:t + 1], in1=x[:, t, :],
                                                   op0=ALU.mult, op1=ALU.add).then_inc(y_sums, 1)
            dve.wait_ge(final_squares, NT)
            nc.vector.tensor_scalar(sums5[:, 4:8], sums5[:, 0:4], 1.0 / D, EPS, ALU.mult, ALU.add).then_inc(final_var, 1)
            dve.wait_ge(final_root, 1)
            steps.link(nc.vector.reciprocal(sums5[:, 12:16], sums5[:, 8:12]))
            dve.wait_ge(gain_in, 16 * 3)
            for t in range(NT):
                nc.vector.scalar_tensor_tensor(out=out_rows[:, t, :], in0=x[:, t, :], scalar=sums5[:, 12 + t:13 + t], in1=gain_row[:, :],
                                               op0=ALU.mult, op1=ALU.mult).then_inc(final_rows, 1)

        def pool_tile_in(pool, r, s):
            unless_first(pool, rows_turned[s], r)
            i = 2 * r + s
            pool.dma_start(rows[:, s, :], slots_dram[bass.ds(i * P, P), :]).then_inc(rows_in[s], 16)

        def pool_tile_out(pool, r, s):
            pool.wait_ge(y_left[s], r + 1)
            pool.wait_ge(y_right[s], r + 1)
            i = 2 * r + s
            pool.dma_start(y_dram[bass.ds(i * P, P), :], y_rows[:, s, :]).then_inc(y_stored[s], 16)

        def pool_phase5(pool, steps):
            pool.wait_ge(slots_zeroed, 16)
            pool.wait_ge(slots_made, 1)
            for t in range(NT):
                for k in range(TOPK):
                    pool.indirect_dma_start(slots_dram, bass.IndirectOffsetOnAxis(ap=slot[:, k, t:t + 1], axis=0),
                                            hn[:, t, :], None).then_inc(rows_placed, 16)
            pool.wait_ge(rows_placed, 16 * NT * TOPK)
            for r in range(2):
                pool_tile_in(pool, r, 0)
                pool_tile_in(pool, r, 1)
            with pool.Fori(2, PAIRS) as r:
                for s in range(2):
                    pool_tile_in(pool, r, s)
                    pool_tile_out(pool, r - 2, s)
            pool_tile_in(pool, PAIRS, 0)
            for r in (PAIRS - 2, PAIRS - 1):
                pool_tile_out(pool, r, 0)
                pool_tile_out(pool, r, 1)
            pool_tile_out(pool, PAIRS, 0)
            pool.wait_ge(y_stored[0], 16 * (PAIRS + 1))
            pool.wait_ge(y_stored[1], 16 * PAIRS)
            for t in range(NT):
                for k in range(TOPK):
                    pool.indirect_dma_start(y_pair[:, t, k, :], None, y_dram,
                                            bass.IndirectOffsetOnAxis(ap=slot[:, k, t:t + 1], axis=0)).then_inc(y_gathered, 16)

        def sp_expert(sp, r, s, e):
            view3 = lambda a: a[0, bass.ds(e, 1), :, :].rearrange("o (k p) n -> p (o k) n", p=P)
            unless_first(sp, gate_up_made[s], r)
            sp.dma_start(gate_up[:, s, :, 0:EF], view3(w["expert_w_gate_2"])).then_inc(gate_up_in[s], 16)
            sp.dma_start(gate_up[:, s, :, EF:2 * EF], view3(w["expert_w_up_2"])).then_inc(gate_up_in[s], 16)
            unless_first(sp, y_made[s], r)
            sp.dma_start(down_w[:, s, :, :], view3(w["expert_w_down_2"])).then_inc(down_in[s], 16)

        def sp_phase5(sp):
            sp.wait_ge(cross_in, 10)
            k3 = lambda a: a[0].rearrange("(k p) n -> p k n", p=P)
            sp.wait_ge(x_added, 24)
            sp.dma_start(router_w[:, :, 0:NG], k3(w["router_group_w_2"])).then_inc(router_in, 16)
            sp.dma_start(router_w[:, :, NG:NG + NE], k3(w["router_expert_w_2"])).then_inc(router_in, 16)
            sp.dma_start(router_b[:, 0:NG], w["router_group_b_2"][0:1, :].broadcast_to([P, NG])).then_inc(router_in, 16)
            sp.dma_start(router_b[:, NG:NG + NE], w["router_expert_b_2"][0:1, :].broadcast_to([P, NE])).then_inc(router_in, 16)
            sp.dma_start(gain_row[:, :], w["norm_final_g_2"].rearrange("(o d) -> o d", o=1).broadcast_to([P, D])).then_inc(gain_in, 16)
            for s in range(2):
                sp_expert(sp, 0, s, s)
            with sp.Fori(1, NE // 2) as r:
                for s in range(2):
                    sp_expert(sp, r, s, 2 * r + s)
            sp.wait_ge(slots_made, 2)
            with sp.Fori(NE // 2, PAIRS) as r:
                for s in range(2):
                    at = 2 * r + (s - NE)
                    sp_expert(sp, r, s, sp.value_load(later_expert[0:1, bass.ds(at, 1)], min_val=0, max_val=NE - 1))
            sp_expert(sp, PAIRS, 0, sp.value_load(later_expert[0:1, EXTRA - 1:EXTRA], min_val=0, max_val=NE - 1))
            out_view = out[0].rearrange("(t p) d -> p t d", p=P)
            for t in range(NT):
                sp.wait_ge(final_rows, t + 1)
                sp.dma_start(out_view[:, t, :], out_rows[:, t, :]).then_inc(out_stored, 16)
            sp.wait_ge(out_stored, 16 * NT)

        block = ctx.enter_context(nc.Block())

        @block.sync
        def _(sp):
            sp_phase1(sp)
            sp_phase2(sp)
            sp_phase3(sp)
            sp_phase4(sp)
            sp_phase5(sp)

        @block.tensor
        def _(pe):
            pe_phase1(pe)
            pe_phase2(pe)
            pe_phase3(pe)
            pe_phase4(pe)
            pe_phase5(pe)

        @block.scalar
        def _(act):
            act_phase1(act)
            act_phase2(act)
            act_phase3(act)
            act_phase4(act)
            act_phase5(act)

        @block.vector
        def _(dve):
            steps = Steps(dve, dve_steps)
            dve_phase1(dve, steps)
            dve_phase2(dve, steps)
            dve_phase3(dve, steps)
            dve_phase4(dve, steps)
            dve_phase5(dve, steps)

        @block.gpsimd
        def _(pool):
            steps = Steps(pool, pool_steps)
            pool_phase1(pool, steps)
            pool_phase2(pool, steps)
            pool_phase3(pool, steps)
            pool_phase4(pool, steps)
            pool_phase5(pool, steps)


_BIG = ["x", "w_in_first", "decay_up", "aaa_up", "gate_up", "w_out", "w_ffn_up", "w_ffn_down", "norm_mix_post",
        "norm_ffn_post", "mem_2", "w_in_2", "conv_pw_w_2", "attn_branch_w_2", "w_out_2", "xa_wq_2", "xa_wk_2",
        "xa_wv_2", "xa_wo_2", "router_group_w_2", "router_group_b_2", "router_expert_w_2", "router_expert_b_2",
        "expert_w_gate_2", "expert_w_up_2", "expert_w_down_2", "norm_final_g_2"]


def _packed_cols(inputs):
    v = {name: np.asarray(inputs[name]).reshape(-1) for name in
         ("norm_mix_pre", "norm_ffn_pre", "attn_out_gain", "decay_w0", "aaa_a0", "k_k", "k_a", "r_k", "gn_w", "gn_b",
          "norm_mix_g_2", "norm_xa_g_2", "norm_mem_g_2", "norm_moe_g_2", "conv_dw_b_2", "conv_ln_g_2", "conv_ln_b_2",
          "fox_bf_2", "conv_dw_w_2")}
    mu = np.asarray(inputs["mu_shift"]).reshape(-1)
    v["mu_r"], v["mu_k"], v["mu_v"] = mu[0:H], mu[H:2 * H], mu[2 * H:3 * H]
    v["mu_wa"], v["mu_g"] = mu[3 * H:3 * H + 2 * W_LORA], mu[3 * H + 2 * W_LORA:NSHIFT]
    packed = np.zeros((P, NCOLS), np.float32)
    for name, (at, n) in COL_AT.items():
        a = v[name]
        if a.size == n * P:
            packed[:, at:at + n] = a.reshape(n, P).T
        else:
            packed[0:a.size, at] = a
    return packed


def kernel(**inputs):
    import concourse.bacc as _bacc
    from concourse.bass_utils import run_bass_kernel_spmd as _run

    nc = _bacc.Bacc("TRN2", target_bir_lowering=False, num_devices=1)
    arrays = {f"in_{n}_dram": np.ascontiguousarray(inputs[n]) for n in _BIG}
    arrays["in_cols_dram"] = _packed_cols(inputs)
    arrays["in_consts_dram"] = shape_constants()
    aps = {n: nc.dram_tensor(n, a.shape, mybir.dt.from_np(a.dtype), kind="ExternalInput").ap() for n, a in arrays.items()}
    out = nc.dram_tensor("out_0_dram", (1, T, D), F32, kind="ExternalOutput").ap()
    two_blocks(nc, {n: aps[f"in_{n}_dram"] for n in _BIG}, aps["in_cols_dram"], aps["in_consts_dram"], out)
    r = _run(nc, [arrays], core_ids=[0])
    return r.results[0]["out_0_dram"]
```

```python
from contextlib import ExitStack

import concourse.bass as bass
from concourse import mybir
import numpy as np

F32 = mybir.dt.float32
F32R = mybir.dt.float32r
I32 = mybir.dt.int32
ALU = mybir.AluOpType
ACT = mybir.ActivationFunctionType
AX_X = mybir.AxisListType.X

P = 128
T = 512
NT = T // P
D = 1024
KD = D // P
H = 512
KH = H // P
HD = 64
NHEAD = H // HD
MEM = 256
NMT = MEM // P
XH = 4
XHD = 128
NSHIFT = 3 * H + 32 + 32 + 96
W_LORA = 32
R_GATE = 96
EPS = 1e-6
GN_EPS = 64e-5
NEG = -1e30
TAPS = 31
PAD = TAPS - 1
NG = 4
EPG = 4
NE = NG * EPG
EF = 256
TOPK = 2
MOE_TILES = T * TOPK // P + NE - 1
SLOTS = MOE_TILES * P
EXTRA = MOE_TILES - NE
PAIRS = MOE_TILES // 2
FIRST_PAIRS = NE // 2
CHUNK = 128
NCH = T // CHUNK
DECAY = float(np.exp(-0.5))
LEVELS = 7

COLS = [
    ("mu_r", 4), ("mu_k", 4), ("mu_v", 4), ("mu_wa", 1), ("mu_g", 1), ("decay_w0", 4), ("aaa_a0", 4), ("k_k", 4), ("k_a", 4),
    ("r_k", 4), ("gn_w", 4), ("gn_b", 4), ("conv_dw_w_2", 4 * TAPS), ("conv_dw_b_2", 4), ("conv_ln_g_2", 4),
    ("conv_ln_b_2", 4), ("fox_bf_2", 1),
]
COL_AT = {}
_at = 0
for _name, _n in COLS:
    COL_AT[_name] = (_at, _n)
    _at += _n
NCOLS = _at

CONSTS = [
    ("ident", 128), ("eps", 2), ("head_sum", 128), ("head_mean", 128), ("chan_mean", 128), ("ones", 128), ("before", 128),
    ("first4", 4), ("tile_edges", 4), ("tile_no", 30), ("band_causal", T),
    ("band_dilated", T), ("tri", 256), ("restart", T), ("levels", LEVELS * 64), ("ident64", 64),
]
CONST_AT = {}
_at = 0
for _name, _n in CONSTS:
    CONST_AT[_name] = (_at, _n)
    _at += _n
NCONSTS = _at


def shape_constants():
    c = np.zeros((P, NCONSTS), np.float32)

    def put(name, a):
        at, n = CONST_AT[name]
        c[:, at:at + n] = a

    i = np.arange(P)
    same_head = (i[:, None] // HD == i[None, :] // HD).astype(np.float32)
    put("ident", np.eye(P))
    put("head_sum", same_head)
    put("head_mean", same_head / HD)
    put("chan_mean", np.full((P, P), 1.0 / H))
    put("ones", np.ones((P, P)))
    put("before", i[:, None] < i[None, :])
    dist = i[:, None] + (T - P) - np.arange(T)[None, :]
    put("band_causal", np.where(dist >= 0, 0.0, NEG))
    count = ((dist >= 0) & (dist <= 128)).astype(int)
    count += (dist >= 0) & (dist % 4 == 0)
    count += (dist >= 0) & (dist % 16 == 0)
    put("band_dilated", np.where(count > 0, np.log(np.maximum(count, 1)), NEG))
    put("tri", np.concatenate([i[:, None] < i[None, :], i[:, None] <= i[None, :]], 1))
    put("restart", np.broadcast_to(np.arange(T) % CHUNK != 0, (P, T)))
    lv = []
    for n in range(LEVELS):
        b = 1 << n
        col = np.arange(64)
        lv.append(i[:, None] // b == 2 * (col[None, :] // b) + 1)
    put("levels", np.concatenate(lv, 1))
    put("ident64", np.concatenate([np.eye(64), np.eye(64)], 0))
    put("eps", np.broadcast_to(np.array([EPS, GN_EPS]), (P, 2)))
    put("first4", np.broadcast_to(np.array([4.0, 3.0, 2.0, 1.0]), (P, 4)))
    put("tile_edges", np.broadcast_to(np.arange(4) * 128.0, (P, 4)))
    put("tile_no", np.broadcast_to(np.arange(30), (P, 30)))
    return c


FFN_ORDER = [(0, None), (1, None), (None, 0), (2, None), (None, 1), (3, None), (None, 2), (None, 3)]


def weight_slabs(w):
    slabs = []

    def wide(name, a, c0, cols):
        for n in range(0, cols, 256):
            m = min(256, cols - n)
            slabs.append((f"{name}{n // 256}", a[:, c0 + n:c0 + n + m].rearrange("(k p) n -> p k n", p=P)))

    def deep(name, a, r0, rows, c0):
        for n in range(0, rows, 512):
            slabs.append((f"{name}{n // 512}", a[r0 + n:r0 + n + 512, c0:c0 + 512].rearrange("(k p) n -> p k n", p=P)))

    w1, w2 = w["w_in_first"], w["w_in_2"][0]
    wide("q", w1, 0, H)
    wide("k", w1, H, H)
    deep("v", w1, 0, D, 2 * H)
    wide("rr", w1, 3 * H, H)
    wide("rk", w1, 4 * H, H)
    wide("rv", w1, 5 * H, H)
    wide("lora", w1, 6 * H, 160)
    for hf in range(2):
        deep(f"out.{hf}.", w["w_out"][0], 0, D, 512 * hf)
    for up, down in FFN_ORDER:
        if up is not None:
            wide(f"up.{up}.", w["w_ffn_up"][0], up * D, D)
        else:
            for hf in range(2):
                deep(f"down.{down}.{hf}.", w["w_ffn_down"][0], down * D, D, 512 * hf)
    wide("glu_gate", w2, H, H)
    wide("glu_a", w2, 0, H)
    wide("fq", w2, 2 * H, H)
    wide("fk", w2, 3 * H, H)
    deep("fv", w2, 0, D, 4 * H)
    wide("ff", w2, 5 * H, 128)
    for hf in range(2):
        wide(f"gc.{hf}.", w2, 5 * H + 8 + 512 * hf, 512)
    for hf in range(2):
        deep(f"pw.{hf}.", w["conv_pw_w_2"][0], 0, H, 512 * hf)
    for hf in range(2):
        wide(f"ga.{hf}.", w2, 5 * H + 8 + D + 512 * hf, 512)
    for hf in range(2):
        deep(f"ab.{hf}.", w["attn_branch_w_2"][0], 0, H, 512 * hf)
    for hf in range(2):
        deep(f"out2.{hf}.", w["w_out_2"][0], 0, D, 512 * hf)
    wide("xk", w["xa_wk_2"][0], 0, H)
    deep("xv", w["xa_wv_2"][0], 0, D, 0)
    wide("xq", w["xa_wq_2"][0], 0, H)
    for hf in range(2):
        deep(f"xo.{hf}.", w["xa_wo_2"][0], 0, H, 512 * hf)
    return slabs


RAW = 2
SPLIT = 2
WIDE_STEPS = 3


class Banks:

    def __init__(self, banks, full, free):
        self.banks, self.full, self.free = banks, full, free
        self.uses = [0] * len(banks)
        self.frees = [0] * len(banks)
        self.next = 0
        self.at = {}
        self.last = [None] * len(banks)

    def plan(self, name, read=None, full=True):
        b = self.next % len(self.banks)
        self.next += 1
        assert name not in self.at, name
        if read is None:
            self.frees[b] += 1
            read = (self.free[b], self.frees[b])
        self.uses[b] += full
        self.at[name] = (b, self.uses[b], read, self.last[b])
        self.last[b] = name

    def open(self, pe, name):
        b, _, _, before = self.at[name]
        if before:
            pe.wait_ge(*self.at[before][2])
        return self.banks[b]

    def filled(self, product, name):
        product.then_inc(self.full[self.at[name][0]], 1)

    def full_at(self, name):
        b, n, _, _ = self.at[name]
        return self.full[b], n

    def take(self, eng, name):
        eng.wait_ge(*self.full_at(name))
        return self.banks[self.at[name][0]]

    def done(self, read, name):
        assert self.at[name][2][0] is self.free[self.at[name][0]], name
        read.then_inc(self.free[self.at[name][0]], 1)


class Steps:

    def __init__(self, eng, sem):
        self.eng, self.sem, self.n = eng, sem, 0

    def mark(self, ins):
        ins.then_inc(self.sem, 1)
        self.n += 1
        return self.n

    def after(self, n):
        self.eng.wait_ge(self.sem, n)

    def link(self, ins):
        self.after(self.mark(ins))


def in_turn(*programs):
    programs = list(programs)
    while programs:
        for program in list(programs):
            if next(program, END) is END:
                programs.remove(program)


END = object()


def later(n, program):
    yield from range(n)
    yield from program


def two_blocks(nc, w, cols_in, consts_in, out):
    slabs = weight_slabs(w)
    slab_no = {name: n for n, (name, _) in enumerate(slabs)}

    with ExitStack() as ctx:
        def sem(name):
            return ctx.enter_context(nc.semaphore(name))

        place = [16512]

        def sb(name, shape, dt=F32, at=None):
            size = int(np.prod(shape[1:])) * 4
            offset = place[0] if at is None else at
            if at is None:
                place[0] += (size + 31) // 32 * 32
            assert offset + size <= nc.sbuf_usable_end, (name, offset + size)
            return nc.alloc_sbuf_tensor_at(name, list(shape), dt, offset=offset)

        def phase(start):
            at = [start]

            def put(name, shape, dt=F32):
                size = (int(np.prod(shape[1:])) * 4 + 31) // 32 * 32
                t = sb(name, shape, dt, at=at[0])
                at[0] += size
                return t

            put.at = at
            return put

        consts_at = place[0]
        consts = sb("consts", [P, NCONSTS])
        cols = sb("cols", [P, NCOLS])
        less = sb("less", [P, 20])
        gain_row = sb("gain_row", [P, D])
        gain_row_b = sb("gain_row_b", [P, D], at=consts_at + 4 * CONST_AT["band_dilated"][0])
        ring_at = place[0]
        raw = sb("raw", [P, RAW, 2048])
        whi = sb("whi", [P, SPLIT, 2048], F32R)
        wlo = sb("wlo", [P, SPLIT, 2048], F32R)
        act_at = place[0]
        ahi = sb("ahi", [P, KD, T], F32R)
        alo = sb("alo", [P, KD, T], F32R)
        region = place[0]

        def const(name):
            at, n = CONST_AT[name]
            return consts[:, at:at + n]

        def col(name, j=0, n=1):
            at, _ = COL_AT[name]
            return cols[:, at + j:at + j + n]

        ident = const("ident")
        LESS = {"mu_r": 0, "mu_k": 4, "mu_v": 8, "mu_wa": 12, "mu_g": 13, "k_a": 14}

        def one_less(name, j=0):
            return less[:, LESS[name] + j:LESS[name] + j + 1]

        banks = Banks([ctx.enter_context(nc.psum_tensor(f"bank{b}", [P, 512], F32)) for b in range(8)],
                      [sem(f"bank_full{b}") for b in range(8)], [sem(f"bank_free{b}") for b in range(8)])

        raw_in = [sem(f"raw_in{n}") for n in range(RAW)]
        hi_made = sem("hi_made")
        lo_made = sem("lo_made")
        slab_used = sem("slab_used")
        consts_in_sem = sem("consts_loaded")
        cols_loaded = sem("cols_loaded")
        masks_in = sem("masks_loaded")
        gains_in = [sem("gains_in"), sem("gains_in_b")]
        GAINS = [["norm_mix_pre", "attn_out_gain", "norm_mix_post", "norm_ffn_post", "norm_mem_g_2", "norm_final_g_2"],
                 ["norm_ffn_pre", "norm_mix_g_2", "norm_xa_g_2", "norm_moe_g_2"]]
        dve_steps = sem("dve_steps")
        act_steps = sem("act_steps")
        pool_steps = sem("pool_steps")

        def view(t, n, k, cols_):
            return t[:, n, 0:k * cols_].rearrange("p (k n) -> p k n", k=k)

        def slab_shape(n):
            return slabs[n][1].shape[1], slabs[n][1].shape[2]

        def load_slabs(sp, state, upto):
            while state[0] < min(upto, len(slabs)):
                n = state[0]
                k, c = slab_shape(n)
                if n >= RAW:
                    sp.wait_ge(lo_made, n - RAW + 1)
                sp.dma_start(view(raw, n % RAW, k, c), slabs[n][1]).then_inc(raw_in[n % RAW], 16)
                state[0] += 1

        def make_hi(act, state, upto):
            while state[0] < min(upto, len(slabs)):
                n = state[0]
                k, c = slab_shape(n)
                act.wait_ge(raw_in[n % RAW], 16 * (n // RAW + 1))
                if n >= SPLIT:
                    act.wait_ge(*slab_end[n - SPLIT])
                nc.scalar.activation(whi[:, n % SPLIT, 0:k * c], raw[:, n % RAW, 0:k * c], ACT.Copy).then_inc(hi_made, 1)
                state[0] += 1

        def make_lo(pool, state, upto):
            while state[0] < min(upto, len(slabs)):
                n = state[0]
                k, c = slab_shape(n)
                pool.wait_ge(hi_made, n + 1)
                nc.gpsimd.tensor_tensor(wlo[:, n % SPLIT, 0:k * c], raw[:, n % RAW, 0:k * c],
                                        whi[:, n % SPLIT, 0:k * c].bitcast(F32), ALU.subtract).then_inc(lo_made, 1)
                state[0] += 1

        sp_slab, act_slab, pool_slab = [0], [0], [0]

        def gain_place(name):
            r = name in GAINS[1]
            width = H if name == "attn_out_gain" else D
            return (gain_row, gain_row_b)[r][:, 0:width], gains_in[r], 16 * (GAINS[r].index(name) + 1)

        def load_gain(sp, name):
            row, loaded, _ = gain_place(name)
            src = w[name][0:1, :] if len(w[name].shape) == 2 else w[name].rearrange("(o d) -> o d", o=1)
            sp.dma_start(row, src.broadcast_to([P, row.shape[1]])).then_inc(loaded, 16)

        def gain(eng, name):
            row, loaded, n = gain_place(name)
            eng.wait_ge(loaded, n)
            return row

        slab_end = {}
        inner_slabs = [0]

        def wide_units(name, units, read=None):
            for j in range(units):
                banks.plan(f"{name}/{j}", read(j) if read else None)
                if j == units - 1:
                    slab_end[slab_no[name]] = banks.full_at(f"{name}/{j}")
                yield from range(WIDE_STEPS)

        def plan_wide(name, units, read=None):
            in_turn(wide_units(name, units, read))

        def plan_deep(names, unit, tiles=NT, read=None):
            for t in range(tiles):
                banks.plan(f"{unit}/{t}", read(t) if read else None)
            for name in names[:-1]:
                inner_slabs[0] += 1
                slab_end[slab_no[name]] = (slab_used, inner_slabs[0])
            slab_end[slab_no[names[-1]]] = banks.full_at(f"{unit}/{tiles - 1}")

        def three_passes(acc, pairs, first, last):
            ins = None
            for i, ((sh, sl), (mh, ml)) in enumerate(pairs):
                end = i == len(pairs) - 1
                nc.tensor.matmul(acc, sh, ml, start=first and i == 0, stop=False)
                nc.tensor.matmul(acc, sh, mh, start=False, stop=False)
                ins = nc.tensor.matmul(acc, sl, mh, start=False, stop=last and end)
            return ins

        def pe_wide(pe, name, **how):
            in_turn(pe_wide_steps(pe, name, **how))

        def pe_wide_steps(pe, name, k0=0, tokens=T, acts=None, parts=None):
            n = slab_no[name]
            k, c = slab_shape(n)
            xh, xl = acts or (ahi, alo)
            pe.wait_ge(lo_made, n + 1)
            wh, wl = view(whi, n % SPLIT, k, c), view(wlo, n % SPLIT, k, c)
            parts = parts or [(i, i + P) for i in range(0, c, P)]
            for j, (c0, c1) in enumerate(parts):
                unit = f"{name}/{j}"
                acc = banks.open(pe, unit)
                for step in range(WIDE_STEPS):
                    ks = range(step * k // WIDE_STEPS, (step + 1) * k // WIDE_STEPS)
                    ins = three_passes(acc[0:c1 - c0, 0:tokens],
                                       [((wh[:, i, c0:c1], wl[:, i, c0:c1]), (xh[:, k0 + i, 0:tokens], xl[:, k0 + i, 0:tokens]))
                                        for i in ks], step == 0, step == WIDE_STEPS - 1)
                    if step == WIDE_STEPS - 1:
                        banks.filled(ins, unit)
                    yield

        def pe_deep(pe, names, unit, k0=0, tiles=NT, acts=None):
            xh, xl = acts or (ahi, alo)
            accs = [banks.open(pe, f"{unit}/{t}") for t in range(tiles)]
            at = k0
            for s, name in enumerate(names):
                n = slab_no[name]
                k, c = slab_shape(n)
                pe.wait_ge(lo_made, n + 1)
                wh, wl = view(whi, n % SPLIT, k, c), view(wlo, n % SPLIT, k, c)
                for t in range(tiles):
                    ts = slice(t * P, (t + 1) * P)
                    ins = three_passes(accs[t][:, :], [((xh[:, at + i, ts], xl[:, at + i, ts]), (wh[:, i, :], wl[:, i, :]))
                                                       for i in range(k)], s == 0, s == len(names) - 1)
                    if s == len(names) - 1:
                        banks.filled(ins, f"{unit}/{t}")
                if s < len(names) - 1:
                    ins.then_inc(slab_used, 1)
                at += k


        squares_made = sem("squares_made")
        roots_made = sem("roots_made")
        scales_made = sem("scales_made")
        rows_normed = sem("rows_normed")
        cols_hi = sem("cols_hi")
        cols_lo = sem("cols_lo")
        cols_plain = sem("cols_plain")
        turns = {}
        turn_count = {"tile": 0, "split": 0, "plain": 0}

        def turn_units(name, tiles, depth, normalise=True, split=True):
            halves = (depth + 3) // 4
            st = dict(tiles=tiles, depth=depth, halves=halves, normalise=normalise, **turn_count)
            turns[name] = st
            if normalise:
                turn_count["tile"] += tiles
            kind, read = ("split", cols_lo) if split else ("plain", cols_plain)
            turn_count[kind] += tiles * halves
            for t in range(tiles):
                for h in range(halves):
                    banks.plan(f"{name}/{t}.{h}", (read, st[kind] + t * halves + h + 1))
                yield

        def plan_turn(*args, **how):
            in_turn(turn_units(*args, **how))

        def act_norm(act, name, rows, ready, scratch, sums):
            st = turns[name]
            for t in range(st["tiles"]):
                n = st["tile"] + t
                ready(act, t)
                if t >= 2:
                    act.wait_ge(squares_made, n - 1)
                nc.scalar.activation(scratch[:, t % 2, 0:st["depth"] * P], rows(t), ACT.Square,
                                     accum_out=sums[:, t:t + 1]).then_inc(squares_made, 1)
                act.wait_ge(squares_made, n + 1)
                nc.scalar.activation(sums[:, 4 + t:5 + t], sums[:, t:t + 1], ACT.Sqrt, scale=1.0 / (st["depth"] * P),
                                     bias=const("eps")[:, 0:1]).then_inc(roots_made, 1)
                yield

        def dve_norm(dve, name, rows, sums, normal, gain_name, buffers=2):
            st = turns[name]
            for t in range(st["tiles"]):
                n = st["tile"] + t + 1
                dve.wait_ge(roots_made, n)
                nc.vector.reciprocal(sums[:, 8 + t:9 + t], sums[:, 4 + t:5 + t]).then_inc(scales_made, 1)
                dve.wait_ge(scales_made, n)
                if t >= buffers:
                    banks.take(dve, f"{name}/{t - buffers}.{st['halves'] - 1}")
                nc.vector.scalar_tensor_tensor(out=normal(t), in0=rows(t), scalar=sums[:, 8 + t:9 + t], in1=gain(dve, gain_name),
                                               op0=ALU.mult, op1=ALU.mult).then_inc(rows_normed, 1)
                yield

        def pe_turn(pe, name, normal, ready=None):
            st = turns[name]
            for t in range(st["tiles"]):
                if st["normalise"]:
                    pe.wait_ge(rows_normed, st["tile"] + t + 1)
                else:
                    ready(pe, t)
                for h in range(st["halves"]):
                    acc = banks.open(pe, f"{name}/{t}.{h}")
                    for j in range(4):
                        c = (4 * h + j) * P
                        ins = nc.tensor.transpose(acc[:, j * P:(j + 1) * P], normal(t)[:, c:c + P], ident)
                    banks.filled(ins, f"{name}/{t}.{h}")
                yield

        def four(bank):
            return bank[:, :].rearrange("p (j n) -> p j n", j=4)

        def act_split(act, name, hi):
            st = turns[name]
            for t in range(st["tiles"]):
                for h in range(st["halves"]):
                    acc = banks.take(act, f"{name}/{t}.{h}")
                    nc.scalar.activation(hi[:, 4 * h:4 * h + 4, t * P:(t + 1) * P], four(acc), ACT.Copy).then_inc(cols_hi, 1)
                yield

        def dve_split(dve, name, hi, lo):
            st = turns[name]
            for t in range(st["tiles"]):
                for h in range(st["halves"]):
                    acc = banks.take(dve, f"{name}/{t}.{h}")
                    dve.wait_ge(cols_hi, st["split"] + t * st["halves"] + h + 1)
                    ks, ts = slice(4 * h, 4 * h + 4), slice(t * P, (t + 1) * P)
                    nc.vector.tensor_tensor(lo[:, ks, ts], four(acc), hi[:, ks, ts].bitcast(F32), ALU.subtract).then_inc(cols_lo, 1)
                yield

        def act_plain(act, name, to):
            st = turns[name]
            for t in range(st["tiles"]):
                for h in range(st["halves"]):
                    acc = banks.take(act, f"{name}/{t}.{h}")
                    nc.scalar.activation(to[:, 4 * h:4 * h + 4, t * P:(t + 1) * P], four(acc), ACT.Copy).then_inc(cols_plain, 1)
                yield

        def columns_ready(pe, name):
            st = turns[name]
            pe.wait_ge(cols_lo, st["split"] + st["tiles"] * st["halves"])

        scores_in = sem("scores_in_sbuf")
        peak_made = sem("score_peaks")
        probs_made = sem("probs_made")
        probs_turned = sem("probs_turned")
        heads_out = sem("heads_out")
        attns = {}
        attn_count = [0]

        def attn_units(name, heads, keys, by_tile=False):
            items = [(h, t, keys(t)) for h in range(heads) for t in range(NT)]
            if by_tile:
                items.sort(key=lambda item: item[1])
            base = attn_count[0]
            attns[name] = dict(items=items, base=base)
            attn_count[0] += len(items)
            for i in range(len(items) + 2):
                n = base + i
                if i < len(items):
                    banks.plan(f"{name}/s{i}", (scores_in, n + 1))
                if 1 <= i <= len(items):
                    banks.plan(f"{name}/t{i - 1}", (probs_turned, n))
                if i >= 2:
                    banks.plan(f"{name}/o{i - 2}", (heads_out, n - 1))
                yield

        def pe_attn(pe, name, q, k, v, probs, probs_t, bias=None):
            items, base = attns[name]["items"], attns[name]["base"]
            for i in range(len(items) + 2):
                if i < len(items):
                    h, t, keys = items[i]
                    acc = banks.open(pe, f"{name}/s{i}")
                    ins = nc.tensor.matmul(acc[:, 0:keys], q(h, t), k(h, keys), start=True, stop=bias is None)
                    if bias is not None:
                        ins = nc.tensor.matmul(acc[:, 0:keys], bias[0](h), bias[1](keys), start=False, stop=True)
                    banks.filled(ins, f"{name}/s{i}")
                if 1 <= i <= len(items):
                    h, t, keys = items[i - 1]
                    pe.wait_ge(probs_made, base + i)
                    acc = banks.open(pe, f"{name}/t{i - 1}")
                    for b in range(0, keys, P):
                        ins = nc.tensor.transpose(acc[:, b:b + P], probs[:, (i - 1) % 2, b:b + P], ident)
                    banks.filled(ins, f"{name}/t{i - 1}")
                if i >= 2:
                    h, t, keys = items[i - 2]
                    pe.wait_ge(probs_turned, base + i - 1)
                    acc = banks.open(pe, f"{name}/o{i - 2}")
                    n = v(h, 0).shape[1]
                    for b in range(keys // P):
                        ins = nc.tensor.matmul(acc[:, 0:n], probs_t[:, (i - 2) % 2, b * P:(b + 1) * P], v(h, b),
                                               start=b == 0, stop=b == keys // P - 1)
                    banks.filled(ins, f"{name}/o{i - 2}")
                yield

        def dve_attn(dve, steps, name, scale, band, masked, peaks, sums, heads):
            items, base = attns[name]["items"], attns[name]["base"]
            for i in range(len(items) + 2):
                if i < len(items):
                    h, t, keys = items[i]
                    n = base + i
                    acc = banks.take(dve, f"{name}/s{i}")
                    if i >= 2:
                        dve.wait_ge(probs_made, n - 1)
                    if band is None:
                        ins = nc.vector.tensor_scalar(masked[:, i % 2, 0:keys], acc[:, 0:keys], scale, None, ALU.mult)
                    else:
                        off = (NT - 1 - t) * P
                        ins = nc.vector.scalar_tensor_tensor(out=masked[:, i % 2, 0:keys], in0=acc[:, 0:keys], scalar=scale,
                                                             in1=band[:, off:off + keys], op0=ALU.mult, op1=ALU.add)
                    ins.then_inc(scores_in, 1)
                    dve.wait_ge(scores_in, n + 1)
                    nc.vector.tensor_reduce(peaks[:, i:i + 1], masked[:, i % 2, 0:keys], AX_X, ALU.max, negate=True).then_inc(peak_made, 1)
                if i >= 2:
                    h, t, keys = items[i - 2]
                    acc = banks.take(dve, f"{name}/o{i - 2}")
                    steps.link(nc.vector.reciprocal(peaks[:, 32 + i - 2:33 + i - 2], sums[:, i - 2:i - 1]))
                    to = heads(h, t)
                    nc.vector.tensor_scalar(to, acc[:, 0:to.shape[1]], peaks[:, 32 + i - 2:33 + i - 2], None,
                                            ALU.mult).then_inc(heads_out, 1)
                yield

        def act_attn(act, name, masked, peaks, sums, probs, probs_t):
            items, base = attns[name]["items"], attns[name]["base"]
            for i in range(len(items) + 2):
                if i < len(items):
                    h, t, keys = items[i]
                    act.wait_ge(peak_made, base + i + 1)
                    if i >= 2:
                        banks.take(act, f"{name}/t{i - 2}")
                    nc.scalar.activation(probs[:, i % 2, 0:keys], masked[:, i % 2, 0:keys], ACT.Exp, bias=peaks[:, i:i + 1],
                                         accum_out=sums[:, i:i + 1]).then_inc(probs_made, 1)
                if 1 <= i <= len(items):
                    h, t, keys = items[i - 1]
                    acc = banks.take(act, f"{name}/t{i - 1}")
                    if i >= 3:
                        banks.take(act, f"{name}/o{i - 3}")
                    nc.scalar.activation(probs_t[:, (i - 1) % 2, 0:keys], acc[:, 0:keys], ACT.Copy).then_inc(probs_turned, 1)
                yield

        put = phase(region)
        x_rows = put("x_rows", [P, NT, D])
        normal1 = put("normal1", [P, 2, D])
        scratch1 = put("scratch1", [P, 2, D])
        sums1 = put("sums1", [P, 16])
        put = phase(region)
        zr, zk, zv = (put(n, [P, KH, T]) for n in ("zr", "zk", "zv"))
        lora_wa = put("lora_wa", [P, T])
        lora_g = put("lora_g", [P, T])
        lora_w = put("lora_w", [2 * W_LORA, H])
        gate_w = put("gate_w", [R_GATE, H])
        rw_region = put.at[0]
        qt, kt = (put(n, [P, KH, T]) for n in ("qt", "kt"))
        vt = put("vt", [P, NT, H])
        masked1 = put("masked1", [P, 2, T])
        probs1 = put("probs1", [P, 2, T])
        probst1 = put("probst1", [P, 2, T])
        heads1 = put("heads1", [P, NT, H])
        peaks1 = put("peaks1", [P, 64])
        esum1 = put("esum1", [P, 32])
        ascratch = put("attn_scratch", [P, 2, 512])
        anormal = put("attn_normal", [P, 2, 512])
        asums = put("attn_sums", [P, 16])
        put = phase(rw_region)

        class Pair:
            pass

        def pair_buffers(s):
            b = Pair()
            work = put(f"rw_work{s}", [P, 12, T])

            def wk(n, m=1):
                return work[:, n:n + m, :].rearrange("p a n -> p (a n)")

            def units(n):
                return wk(n, 4).rearrange("p (u n) -> p u n", u=8)

            b.cum, b.cumx, b.e_in, b.e_inv, b.e_ex, b.aaa, b.knorm, b.kk, b.kmod, b.ka, b.rk, b.sig = (wk(n) for n in range(12))
            b.kr = put(f"rw_kr{s}", [P, NCH, 2, CHUNK])
            b.beta = put(f"rw_beta{s}", [P, T])
            b.khat = put(f"rw_khat{s}", [P, T])
            b.mids, b.fin, b.fout = (put(f"rw_{n}{s}", [P, 4]) for n in ("mids", "fin", "fout"))
            b.ab, b.bd = units(0), units(4)
            b.xinv = wk(8, 2).rearrange("p (u n) -> p u n", u=8)
            b.xinv_t = b.bd[:, :, 0:CHUNK]
            b.ktok, b.btok = (wk(n).rearrange("p (c n) -> p c n", c=NCH) for n in (10, 11))
            b.norms, b.sds = (put(f"rw_{n}{s}", [P, NCH, 2]) for n in ("norms", "sds"))
            b.vtok = put(f"rw_vtok{s}", [P, NCH, P])
            b.kb = put(f"rw_kb{s}", [P, 2, NCH, P])
            b.tm = b.beta[:, :].rearrange("p (u n) -> p u n", u=8)
            b.neg_w = b.xinv
            b.qq = b.khat[:, :]
            kb_flat = b.kb[:, :, :, :].rearrange("p h c n -> p (h c n)")
            b.gt = kb_flat[:, 0:256].rearrange("p (c n) -> p c n", c=4)
            b.state = kb_flat[:, 256:384].rearrange("p (b n) -> p b n", b=2)
            b.ysb, b.dev, b.dev2, b.over_sd, b.norm_y, b.with_bonus, b.rw = (wk(n) for n in (0, 1, 2, 3, 0, 2, 1))
            return b

        pairs = [pair_buffers(0), pair_buffers(1)]

        x_in = [sem(f"x_in{t}") for t in range(NT)]
        qkv_out = sem("qkv_out")
        z_less = sem("z_less")
        z_shifted = sem("z_shifted")
        lora_acts = sem("lora_acts")
        less_made = sem("less_made")
        small_in = sem("small_in")
        LEVEL_NAMES = [str(n) for n in range(LEVELS)]
        PAIR_STEPS = {
            "act": ["sig", "aaa", "sq", "norm", "e_in", "e_inv", "e_ex", "fout", "ktok", "vtok", "btok", "kktok", "bv"]
                   + [f"xt{n}.{i}" for n in LEVEL_NAMES for i in range(2)] + ["w0", "w1", "y", "dev2", "sd", "hi"],
            "dve": ["scan", "mids", "cum", "cumx", "fin", "kmod_a", "kmod", "rk", "nmax", "nrec", "over_norm", "kk", "khat", "beta", "kappa", "bonus"]
                   + [f"mask{i}" for i in range(8)] + [f"{x}{n}" for n in LEVEL_NAMES for x in ("tm", "x")]
                   + ["qq", "gt", "state0", "state1", "state2", "dev", "rstd", "over_sd", "norm_y", "with_bonus", "rw"],
            "pool": ["ka", "r", "init_x", "init_xt", "lo"],
        }
        pair_done = {e: [sem(f"pair_{e}_steps{s}") for s in range(2)] for e in PAIR_STEPS}
        states_summed = [sem(f"states_summed{s}") for s in range(2)]

        def step_of(engine, p, name):
            names = PAIR_STEPS[engine]
            return pair_done[engine][p % 2], len(names) * (p // 2) + names.index(name) + 1

        class PairSteps:

            def __init__(self, eng, engine, p):
                self.eng, self.engine, self.p, self.names = eng, engine, p, list(PAIR_STEPS.get(engine, []))

            def done(self, ins, name):
                assert name == self.names.pop(0), name
                ins.then_inc(pair_done[self.engine][self.p % 2], 1)

            def after(self, engine, name):
                self.eng.wait_ge(*step_of(engine, self.p, name))

        QKV = ["q0", "q1", "k0", "k1"]
        SHIFT = ["rr0", "rr1", "rk0", "rk1", "rv0", "rv1"]
        shift_units = [(f"{n}/{j}", z, 2 * (s % 2) + j, mu) for s, n in enumerate(SHIFT) for j in range(2)
                       for z, mu in [((zr, "mu_r"), (zk, "mu_k"), (zv, "mu_v"))[s // 2]]]

        plan_turn("mix1", NT, KD)
        for s, n in enumerate(QKV):
            plan_wide(n, 2, lambda j, s=s: (qkv_out, 2 * s + j + 1))
        plan_deep(["v0", "v1"], "v", read=lambda t: (qkv_out, 9 + t))
        def shift_plan():
            for s, n in enumerate(SHIFT):
                yield from wide_units(n, 2, lambda j, s=s: (z_shifted, 2 * s + j + 1))
            yield from wide_units("lora0", 2, lambda j: (z_shifted, 13 + j))

        in_turn(attn_units("dil", NHEAD, lambda t: (t + 1) * P), shift_plan())
        plan_turn("attn1", NT, KH)
        RW_STAGES = 20 + 3 * LEVELS

        def in_two_rows(program):
            def row(first):
                for p in (first, first + 2):
                    n = 0
                    for _ in program(p):
                        n += 1
                        yield
                    assert n == RW_STAGES, (program, n)

            in_turn(row(0), row(1))

        def rwkv_units(p):
            u = f"rw{p}/"

            def plan(name, engine, step):
                banks.plan(u + name, step_of(engine, p, step))

            plan("decay", "act", "sig")
            plan("aaa", "act", "aaa")
            yield
            plan("ss", "act", "norm")
            yield
            plan("over_norm", "dve", "kk")
            plan("bonus", "dve", "bonus")
            yield
            yield
            for two_names in (("ktok", "vtok"), ("btok", "kktok")):
                for name in two_names:
                    plan(name, "act", name)
                yield
            for i in range(8):
                plan(f"mask{i}", "dve", f"mask{i}")
                if i % 2:
                    yield
            plan("bv", "act", "bv")
            yield
            for n in range(LEVELS):
                plan(f"t{n}", "dve", f"tm{n}")
                yield
                if n:
                    plan(f"x{n}", "dve", f"x{n}")
                yield
                for i in range(2):
                    plan(f"xt{n}.{i}", "act", f"xt{n}.{i}")
                yield
            for i in range(2):
                plan(f"w{i}", "act", f"w{i}")
            yield
            plan("q", "dve", "qq")
            plan("g", "dve", "gt")
            yield
            banks.plan(u + "h", step_of("dve", p, "state2"), full=False)
            plan("y", "act", "y")
            yield
            for c in range(1, NCH):
                yield
            plan("mean", "dve", "dev")
            yield
            plan("var", "act", "sd")
            yield
            plan("over_sd", "dve", "norm_y")
            plan("gate", "dve", "rw")
            yield

        in_two_rows(rwkv_units)

        def x_ready(eng, t):
            eng.wait_ge(x_in[t], 16)

        def heads1_ready(eng, t):
            eng.wait_ge(heads_out, attns["dil"]["base"] + len(attns["dil"]["items"]))

        def normal1_of(t):
            return normal1[:, t % 2, :]

        def anormal_of(t):
            return anormal[:, t % 2, :]

        def half(h):
            return slice(h * HD, (h + 1) * HD)

        def pe_phase1(pe):
            pe.wait_ge(consts_in_sem, 16)
            in_turn(pe_turn(pe, "mix1", normal1_of))
            columns_ready(pe, "mix1")
            for n in QKV:
                pe_wide(pe, n)
            pe_deep(pe, ["v0", "v1"], "v")
            pe.wait_ge(masks_in, 16)
            pe.wait_ge(qkv_out, 12)
            in_turn(pe_attn(pe, "dil",
                            lambda h, t: qt[half(h % 2), h // 2, t * P:(t + 1) * P], lambda h, n: kt[half(h % 2), h // 2, 0:n],
                            lambda h, b: vt[:, b, half(h)], probs1, probst1),
                    pe_shift(pe))
            in_turn(pe_turn(pe, "attn1", anormal_of))
            pe.wait_ge(small_in, 48)
            pe.wait_ge(lora_acts, 2)
            in_two_rows(lambda p: pe_rwkv(pe, p))

        def pe_shift(pe):
            for n in SHIFT:
                yield from pe_wide_steps(pe, n)
            yield from pe_wide_steps(pe, "lora0", parts=[(0, P), (2 * W_LORA, 2 * W_LORA + R_GATE)])

        def pe_rwkv(pe, p):
            u = f"rw{p}/"
            b = pairs[p % 2]
            st = PairSteps(pe, "pe", p)
            fc = slice(p * P, (p + 1) * P)
            units = [(h, c) for h in range(2) for c in range(NCH)]

            def single(name, lhs, rhs):
                acc = banks.open(pe, u + name)
                banks.filled(nc.tensor.matmul(acc[:, :], lhs, rhs, start=True, stop=True), u + name)

            def head_sums(name, squares, heads):
                acc = banks.open(pe, u + name)
                for c in range(NCH):
                    ins = nc.tensor.matmul(acc[:, 2 * c:2 * c + 2], squares[:, c * CHUNK:(c + 1) * CHUNK], heads[:, 0:P:HD],
                                           start=True, stop=True)
                banks.filled(ins, u + name)

            def to_columns(name, rows):
                acc = banks.open(pe, u + name)
                for c in range(NCH):
                    ins = nc.tensor.transpose(acc[:, c * CHUNK:(c + 1) * CHUNK], rows[:, c * P:(c + 1) * P], ident)
                banks.filled(ins, u + name)

            single("decay", lora_w[0:W_LORA, fc], lora_wa[0:W_LORA, :])
            single("aaa", lora_w[W_LORA:2 * W_LORA, fc], lora_wa[W_LORA:2 * W_LORA, :])
            yield
            st.after("act", "sq")
            head_sums("ss", b.knorm, const("head_sum"))
            yield
            st.after("dve", "over_norm")
            to_columns("over_norm", b.knorm)
            st.after("dve", "rk")
            single("bonus", const("head_sum"), b.rk)
            yield
            yield
            for name, src, made in (("ktok", b.khat[:, :], "khat"), ("vtok", zv[:, p, :], None), ("btok", b.beta[:, :], "beta"),
                                    ("kktok", b.kr[:, :, 0, :], "kappa")):
                if made:
                    st.after("dve", made)
                acc = banks.open(pe, u + name)
                for c in range(NCH):
                    tokens = src[:, c, :] if name == "kktok" else src[:, c * CHUNK:(c + 1) * CHUNK]
                    ins = nc.tensor.transpose(acc[:, c * P:(c + 1) * P], tokens, ident)
                banks.filled(ins, u + name)
                if name in ("vtok", "kktok"):
                    yield
            st.after("pool", "r")
            for i, (src, h, c) in enumerate((src, h, c) for src in (b.beta, b.khat) for h in range(2) for c in (0, 2)):
                acc = banks.open(pe, f"{u}mask{i}")
                for j in range(2):
                    ins = nc.tensor.matmul(acc[:, j * 256:(j + 1) * 256], src[half(h), (c + j) * CHUNK:(c + j + 1) * CHUNK],
                                           b.kr[half(h), c + j, :, :].rearrange("p a n -> p (a n)"), start=True, stop=True)
                banks.filled(ins, f"{u}mask{i}")
                if i % 2:
                    yield
            st.after("act", "vtok")
            st.after("dve", "mask7")
            acc = banks.open(pe, u + "bv")
            for n, (h, c) in enumerate(units):
                ins = nc.tensor.matmul(acc[:, n * HD:(n + 1) * HD], b.bd[:, n, 0:CHUNK], b.vtok[:, c, half(h)], start=True, stop=True)
            banks.filled(ins, u + "bv")
            yield
            for lv in range(LEVELS):
                size = 1 << lv
                if lv:
                    st.after("dve", f"x{lv - 1}")
                else:
                    st.after("pool", "init_x")
                acc = banks.open(pe, f"{u}t{lv}")
                left = b.xinv.rearrange("p u (n s b) -> p u n s b", s=2, b=size)
                for n in range(8):
                    ins = nc.tensor.matmul(acc[:, n * 64:(n + 1) * 64], b.ab[:, n, 0:CHUNK], left[:, n, :, 0, :], start=True, stop=True)
                banks.filled(ins, f"{u}t{lv}")
                yield
                if lv:
                    st.after("dve", f"tm{lv}")
                    st.after("act", f"xt{lv - 1}.1")
                    acc = banks.open(pe, f"{u}x{lv}")
                    for n in range(8):
                        ins = nc.tensor.matmul(acc[:, n * 64:(n + 1) * 64], b.xinv_t[:, n, :], b.tm[:, n, :], start=True, stop=True)
                    banks.filled(ins, f"{u}x{lv}")
                yield
                st.after("dve", f"x{lv}")
                for i in range(2):
                    acc = banks.open(pe, f"{u}xt{lv}.{i}")
                    for j in range(4):
                        ins = nc.tensor.transpose(acc[:, j * P:(j + 1) * P], b.xinv[:, 4 * i + j, :], ident)
                    banks.filled(ins, f"{u}xt{lv}.{i}")
                yield
            st.after("act", f"xt{LEVELS - 1}.1")
            for i in range(2):
                acc = banks.open(pe, f"{u}w{i}")
                for c in range(NCH):
                    ins = nc.tensor.matmul(acc[:, c * P:(c + 1) * P], b.xinv_t[:, 4 * i + c, :], b.kb[:, i, c, :], start=True, stop=True)
                banks.filled(ins, f"{u}w{i}")
            yield
            st.after("act", "w1")
            acc = banks.open(pe, u + "q")
            for n, (h, c) in enumerate(units):
                ins = nc.tensor.matmul(acc[half(h), c * CHUNK:(c + 1) * CHUNK], b.neg_w[:, n, HD:2 * HD], b.ab[:, n, CHUNK:2 * CHUNK],
                                       start=c == 0, stop=c == NCH - 1, skip_group_check=True)
            banks.filled(ins, u + "q")
            acc = banks.open(pe, u + "g")
            for n, (h, c) in enumerate(units):
                if 1 <= c < NCH - 1:
                    ins = nc.tensor.matmul(acc[half(h), c * HD:(c + 1) * HD], b.neg_w[:, n, HD:2 * HD], b.btok[:, c, half(h)],
                                           start=c == 1, stop=c == NCH - 2, skip_group_check=True)
            banks.filled(ins, u + "g")
            yield
            hacc = banks.open(pe, u + "h")
            for n, (h, c) in enumerate(units):
                if c < NCH - 1:
                    to = hacc[half(h), c * HD:(c + 1) * HD]
                    nc.tensor.matmul(to, b.ktok[:, c, half(h)], b.vtok[:, c, half(h)], start=c == 0, stop=False, skip_group_check=True)
                    ins = nc.tensor.matmul(to, b.btok[:, c, half(h)], b.neg_w[:, n, 0:HD], start=False, stop=True, skip_group_check=True)
            ins.then_inc(states_summed[p % 2], 1)
            yacc = banks.open(pe, u + "y")
            for n, (h, c) in enumerate(units):
                to = yacc[half(h), c * CHUNK:(c + 1) * CHUNK]
                nc.tensor.matmul(to, b.neg_w[:, n, 0:HD], b.ab[:, n, CHUNK:2 * CHUNK], start=c == 0, stop=False, skip_group_check=True)
                nc.tensor.matmul(to, b.vtok[:, c, half(h)], b.bd[:, n, CHUNK:2 * CHUNK], start=False, stop=True, skip_group_check=True)
            yield
            st.after("dve", "gt")
            for c in range(1, NCH):
                st.after("dve", f"state{c - 1}")
                state = b.state[:, (c - 1) % 2, :]
                if c < NCH - 1:
                    for h in range(2):
                        ins = nc.tensor.matmul(hacc[half(h), c * HD:(c + 1) * HD], b.gt[half(h), c, :], state[half(h), :],
                                               start=False, stop=True, skip_group_check=True)
                    ins.then_inc(states_summed[p % 2], 1)
                for h in range(2):
                    ins = nc.tensor.matmul(yacc[half(h), c * CHUNK:(c + 1) * CHUNK], state[half(h), :],
                                           b.qq[half(h), c * CHUNK:(c + 1) * CHUNK], start=False, stop=True, skip_group_check=True)
                if c == NCH - 1:
                    banks.filled(ins, u + "y")
                yield
            st.after("act", "y")
            single("mean", const("head_mean"), b.ysb)
            yield
            st.after("act", "dev2")
            head_sums("var", b.dev2, const("head_mean"))
            yield
            st.after("dve", "over_sd")
            to_columns("over_sd", b.over_sd)
            single("gate", gate_w[:, fc], lora_g[0:R_GATE, :])
            yield

        def act_phase1(act):
            act.wait_ge(consts_in_sem, 16)
            nc.scalar.activation(sums1[:, 12:13], const("eps")[:, 0:1], ACT.Sqrt)
            in_turn(act_norm(act, "mix1", lambda t: x_rows[:, t, :], x_ready, scratch1, sums1), later(1, act_split(act, "mix1", ahi)), later(2, act_first_slab(act)))
            make_hi(act, act_slab, SPLIT)
            act.wait_ge(less_made, 2)
            for n in QKV + ["v0", "v1"]:
                make_hi(act, act_slab, slab_no[n] + 1 + SPLIT)
            in_turn(act_attn(act, "dil", masked1, peaks1, esum1, probs1, probst1), act_shift(act))
            act.wait_ge(z_shifted, 14)
            nc.scalar.activation(lora_wa[0:W_LORA, :], lora_wa[0:W_LORA, :], ACT.Tanh).then_inc(lora_acts, 1)
            nc.scalar.activation(lora_g[0:R_GATE, :], lora_g[0:R_GATE, :], ACT.Sigmoid).then_inc(lora_acts, 1)
            in_turn(act_norm(act, "attn1", lambda t: heads1[:, t, :], heads1_ready, ascratch, asums),
                    later(2, act_split(act, "attn1", ahi)))
            act.wait_ge(cols_lo, turns["attn1"]["split"] + NT)
            in_two_rows(lambda p: act_rwkv(act, p))

        def act_first_slab(act):
            make_hi(act, act_slab, 1)
            yield

        def act_shift(act):
            for i, (unit, z, m, mu) in enumerate(shift_units):
                yield from range(WIDE_STEPS - 1)
                acc = banks.take(act, unit)
                nc.scalar.activation(z[:, m, :], acc[:, :], ACT.Copy, scale=one_less(mu, m)).then_inc(z_less, 1)
                if i % 2:
                    make_hi(act, act_slab, slab_no[unit.split("/")[0]] + 1 + SPLIT)
                yield
            for i, (to, mu) in enumerate(((lora_wa, "mu_wa"), (lora_g, "mu_g"))):
                yield from range(WIDE_STEPS - 1)
                acc = banks.take(act, f"lora0/{i}")
                r = slice(0, (2 * W_LORA, R_GATE)[i])
                nc.scalar.activation(to[r, :], acc[r, :], ACT.Copy, scale=one_less(mu)[r, :]).then_inc(z_less, 1)
                yield
            make_hi(act, act_slab, slab_no["lora0"] + 1 + SPLIT)

        def act_rwkv(act, p):
            u = f"rw{p}/"
            b = pairs[p % 2]
            st = PairSteps(act, "act", p)
            activate = nc.scalar.activation
            if p >= 2:
                act.wait_ge(*step_of("pool", p - 2, "lo"))
            acc = banks.take(act, u + "decay")
            st.done(activate(b.sig, acc[:, :], ACT.Sigmoid, bias=col("decay_w0", p)), "sig")
            acc = banks.take(act, u + "aaa")
            st.done(activate(b.aaa, acc[:, :], ACT.Sigmoid, bias=col("aaa_a0", p)), "aaa")
            st.done(activate(b.knorm, zk[:, p, :], ACT.Square, scale=col("k_k", p)), "sq")
            yield
            acc = banks.take(act, u + "ss")
            st.done(activate(b.norms[:, :, :], acc[:, 0:2 * NCH].rearrange("p (c h) -> p c h", h=2), ACT.Sqrt), "norm")
            yield
            st.after("dve", "fin")
            st.done(activate(b.e_in, b.cum, ACT.Exp, scale=-DECAY), "e_in")
            st.done(activate(b.e_inv, b.cum, ACT.Exp, scale=DECAY), "e_inv")
            st.done(activate(b.e_ex, b.cumx, ACT.Exp, scale=-DECAY), "e_ex")
            st.done(activate(b.fout[:, 0:3], b.fin[:, 0:3], ACT.Exp, scale=-DECAY), "fout")
            yield
            yield
            for name, to in (("ktok", b.ktok), ("vtok", b.vtok), ("btok", b.btok)):
                acc = banks.take(act, u + name)
                st.done(activate(to[:, :, :], acc[:, :].rearrange("p (c n) -> p c n", c=NCH), ACT.Copy), name)
                if name == "vtok":
                    yield
            acc = banks.take(act, u + "kktok")
            st.done(activate(b.kb[:, :, :, HD:2 * HD].rearrange("p h c n -> p c h n"),
                             acc[:, :].rearrange("p (c h n) -> p c h n", c=NCH, h=2), ACT.Copy), "kktok")
            yield
            yield from range(4)
            acc = banks.take(act, u + "bv")
            st.done(activate(b.kb[:, :, :, 0:HD].rearrange("p h c n -> p (h c) n"),
                             acc[:, :].rearrange("p (u n) -> p u n", u=8), ACT.Copy), "bv")
            yield
            for lv in range(LEVELS):
                yield from range(2)
                for i in range(2):
                    acc = banks.take(act, f"{u}xt{lv}.{i}")
                    st.after("pool", "init_xt")
                    st.done(activate(b.xinv_t[:, 4 * i:4 * i + 4, :], acc[:, :].rearrange("p (u n) -> p u n", u=4),
                                     ACT.Copy), f"xt{lv}.{i}")
                yield
            for i in range(2):
                acc = banks.take(act, f"{u}w{i}")
                st.done(activate(b.neg_w[:, 4 * i:4 * i + 4, :], acc[:, :].rearrange("p (u n) -> p u n", u=4),
                                 ACT.Copy, scale=-1.0), f"w{i}")
            yield
            yield from range(4)
            acc = banks.take(act, u + "y")
            st.done(activate(b.ysb, acc[:, :], ACT.Copy), "y")
            yield
            st.after("dve", "dev")
            st.done(activate(b.dev2, b.dev, ACT.Square), "dev2")
            yield
            acc = banks.take(act, u + "var")
            st.done(activate(b.sds[:, :, :], acc[:, 0:2 * NCH].rearrange("p (c h) -> p c h", h=2), ACT.Sqrt,
                             bias=const("eps")[:, 1:2]), "sd")
            yield
            st.after("dve", "rw")
            st.done(activate(ahi[:, KH + p, :], b.rw, ACT.Copy), "hi")
            yield

        def dve_phase1(dve, steps):
            in_turn(dve_norm(dve, "mix1", lambda t: x_rows[:, t, :], sums1, normal1_of, "norm_mix_pre"), later(1, dve_split(dve, "mix1", ahi, alo)))
            dve.wait_ge(cols_loaded, 16)
            at, _ = COL_AT["mu_r"]
            nc.vector.tensor_scalar(less[:, 0:14], cols[:, at:at + 14], -1.0, 1.0, ALU.mult, ALU.add).then_inc(less_made, 1)
            nc.vector.tensor_scalar(less[:, 14:18], col("k_a", 0, 4), -1.0, 1.0, ALU.mult, ALU.add).then_inc(less_made, 1)
            dve.wait_ge(masks_in, 16)
            for s, n in enumerate(QKV):
                for j in range(2):
                    acc = banks.take(dve, f"{n}/{j}")
                    nc.vector.tensor_copy((qt, kt)[s // 2][:, 2 * (s % 2) + j, :], acc[:, :]).then_inc(qkv_out, 1)
            for t in range(NT):
                acc = banks.take(dve, f"v/{t}")
                nc.vector.tensor_copy(vt[:, t, :], acc[:, :]).then_inc(qkv_out, 1)
            in_turn(dve_attn(dve, steps, "dil", HD ** -0.5, const("band_dilated"), masked1, peaks1, esum1,
                             lambda h, t: heads1[:, t, half(h)]),
                    dve_shift(dve))
            in_turn(dve_norm(dve, "attn1", lambda t: heads1[:, t, :], asums, anormal_of, "attn_out_gain"), later(2, dve_split(dve, "attn1", ahi, alo)))
            in_two_rows(lambda p: dve_rwkv(dve, p))

        def dve_shift(dve):
            for i, (unit, z, m, mu) in enumerate(shift_units):
                yield from range(WIDE_STEPS - 1)
                acc = banks.take(dve, unit)
                dve.wait_ge(z_less, i + 1)
                nc.vector.scalar_tensor_tensor(out=z[:, m, 1:T], in0=acc[:, 0:T - 1], scalar=col(mu, m), in1=z[:, m, 1:T],
                                               op0=ALU.mult, op1=ALU.add).then_inc(z_shifted, 1)
                yield
            for i, (to, mu) in enumerate(((lora_wa, "mu_wa"), (lora_g, "mu_g"))):
                yield from range(WIDE_STEPS - 1)
                r = slice(0, (2 * W_LORA, R_GATE)[i])
                acc = banks.take(dve, f"lora0/{i}")
                dve.wait_ge(z_less, 13 + i)
                nc.vector.scalar_tensor_tensor(out=to[r, 1:T], in0=acc[r, 0:T - 1], scalar=col(mu)[r, :], in1=to[r, 1:T],
                                               op0=ALU.mult, op1=ALU.add).then_inc(z_shifted, 1)
                yield

        def dve_rwkv(dve, p):
            u = f"rw{p}/"
            b = pairs[p % 2]
            st = PairSteps(dve, "dve", p)
            chunks = lambda a: a.rearrange("p (c n) -> p c n", c=NCH)
            tt, stt, tsc = nc.vector.tensor_tensor, nc.vector.scalar_tensor_tensor, nc.vector.tensor_scalar

            def to_channels(to, factors):
                return nc.vector.tensor_copy(to.rearrange("p (c h n) -> p c h n", c=NCH, h=2),
                                             factors.unsqueeze(3).broadcast_to([P, NCH, 2, HD]))

            def link(ins, name):
                st.done(ins, name)
                st.after("dve", name)

            st.after("act", "sig")
            link(nc.vector.tensor_tensor_scan(b.cum, const("restart"), b.sig, 0.0, ALU.mult, ALU.add), "scan")
            link(nc.vector.tensor_copy(b.mids[:, :], chunks(b.cum)[:, :, CHUNK // 2 - 1]), "mids")
            link(tt(chunks(b.cum), chunks(b.cum), b.mids[:, :].unsqueeze(2).broadcast_to([P, NCH, CHUNK]), ALU.subtract), "cum")
            st.done(tt(b.cumx, b.cum, b.sig, ALU.subtract), "cumx")
            st.done(tt(b.fin[:, 0:3], chunks(b.cum)[:, 0:3, CHUNK - 1], b.mids[:, 1:4], ALU.add), "fin")
            yield
            st.after("act", "aaa")
            link(tsc(b.kmod, b.aaa, col("k_a", p), one_less("k_a", p), ALU.mult, ALU.add), "kmod_a")
            link(tt(b.kmod, b.kmod, zk[:, p, :], ALU.mult), "kmod")
            st.done(stt(out=b.rk, in0=zr[:, p, :], scalar=col("r_k", p), in1=b.kmod, op0=ALU.mult, op1=ALU.mult), "rk")
            st.after("act", "norm")
            link(tsc(b.norms[:, :, :], b.norms[:, :, :], 1e-12, None, ALU.max), "nmax")
            link(nc.vector.reciprocal(b.norms[:, :, :], b.norms[:, :, :]), "nrec")
            st.done(to_channels(b.knorm, b.norms[:, :, :]), "over_norm")
            yield
            acc = banks.take(dve, u + "over_norm")
            st.done(stt(out=b.kk, in0=zk[:, p, :], scalar=col("k_k", p), in1=acc[:, :], op0=ALU.mult, op1=ALU.mult), "kk")
            yield
            st.after("act", "e_inv")
            st.done(tt(b.khat[:, :], b.kmod, b.e_inv, ALU.mult), "khat")
            st.after("pool", "ka")
            st.done(tt(b.beta[:, :], b.ka, b.e_inv, ALU.mult), "beta")
            st.after("dve", "kk")
            st.after("act", "e_ex")
            st.done(tt(b.kr[:, :, 0, :], chunks(b.kk), chunks(b.e_ex), ALU.mult), "kappa")
            yield
            acc = banks.take(dve, u + "bonus")
            banks.take(dve, u + "vtok")
            st.done(tt(zv[:, p, :], acc[:, :], zv[:, p, :], ALU.mult), "bonus")
            yield
            yield
            tri = const("tri").unsqueeze(1).broadcast_to([P, 2, 256])
            for i in range(8):
                acc = banks.take(dve, f"{u}mask{i}")
                to = (b.ab, b.bd)[i // 4][:, 2 * (i % 4):2 * (i % 4) + 2, :]
                st.done(tt(to, acc[:, :].rearrange("p (c n) -> p c n", c=2), tri, ALU.mult), f"mask{i}")
                if i % 2:
                    yield
            yield
            for lv in range(LEVELS):
                size = 1 << lv
                between = const("levels")[:, lv * 64:(lv + 1) * 64].unsqueeze(1).broadcast_to([P, 8, 64])
                acc = banks.take(dve, f"{u}t{lv}")
                st.done(tt(b.tm, acc[:, :].rearrange("p (u n) -> p u n", u=8), between, ALU.mult), f"tm{lv}")
                yield
                left = b.xinv.rearrange("p u (n s b) -> p (u n) s b", s=2, b=size)[:, :, 0, :]
                if lv:
                    minus = banks.take(dve, f"{u}x{lv}")[:, :]
                else:
                    st.after("dve", "tm0")
                    minus = b.tm.rearrange("p u n -> p (u n)")
                st.done(tt(left, left, minus.rearrange("p (n b) -> p n b", b=size), ALU.subtract), f"x{lv}")
                yield
                yield
            yield
            acc = banks.take(dve, u + "q")
            st.done(tt(chunks(b.qq), chunks(acc[:, :]), b.kr[:, :, 1, :], ALU.add), "qq")
            acc = banks.take(dve, u + "g")
            st.done(tt(b.gt[:, 1:3, :], acc[:, HD:3 * HD].rearrange("p (c n) -> p c n", c=2),
                       const("ident64").unsqueeze(1).broadcast_to([P, 2, HD]), ALU.add), "gt")
            yield
            yield
            acc = banks.banks[banks.at[u + "h"][0]]
            for c in range(NCH - 1):
                dve.wait_ge(states_summed[p % 2], (NCH - 1) * (p // 2) + c + 1)
                st.done(tsc(b.state[:, c % 2, :], acc[:, c * HD:(c + 1) * HD], b.fout[:, c:c + 1], None, ALU.mult), f"state{c}")
                yield
            acc = banks.take(dve, u + "mean")
            st.done(tt(b.dev, b.ysb, acc[:, :], ALU.subtract), "dev")
            yield
            st.after("act", "sd")
            link(nc.vector.reciprocal(b.sds[:, :, :], b.sds[:, :, :]), "rstd")
            st.done(to_channels(b.over_sd, b.sds[:, :, :]), "over_sd")
            yield
            acc = banks.take(dve, u + "over_sd")
            link(stt(out=b.norm_y, in0=b.dev, scalar=col("gn_w", p), in1=acc[:, :], op0=ALU.mult, op1=ALU.mult), "norm_y")
            link(stt(out=b.with_bonus, in0=zv[:, p, :], scalar=col("gn_b", p), in1=b.norm_y, op0=ALU.add, op1=ALU.add), "with_bonus")
            acc = banks.take(dve, u + "gate")
            st.done(tt(b.rw, b.with_bonus, acc[:, :], ALU.mult), "rw")
            yield

        def pool_phase1(pool, steps):
            pool.wait_ge(consts_in_sem, 16)
            make_lo(pool, pool_slab, slab_no["lora0"] + 1 + SPLIT)
            pool.wait_ge(rows_normed, turns["attn1"]["tile"] + NT)
            nc.gpsimd.memset(gain_row[:, :], 0.0).then_inc(zeros_made, 1)
            in_two_rows(lambda p: pool_rwkv(pool, p))

        def pool_rwkv(pool, p):
            b = pairs[p % 2]
            st = PairSteps(pool, "pool", p)
            tt, copy = nc.gpsimd.tensor_tensor, nc.gpsimd.tensor_copy
            yield from range(2)
            st.after("dve", "kk")
            st.done(tt(b.ka, b.kk, b.aaa, ALU.mult), "ka")
            st.after("act", "e_in")
            st.done(tt(b.kr[:, :, 1, :], zr[:, p, :].rearrange("p (c n) -> p c n", c=NCH),
                       b.e_in.rearrange("p (c n) -> p c n", c=NCH), ALU.mult), "r")
            yield
            st.after("dve", "beta")
            st.after("pool", "ka")
            st.done(copy(b.xinv, ident.unsqueeze(1).broadcast_to([P, 8, P])), "init_x")
            yield
            yield from range(6)
            banks.take(pool, f"rw{p}/bv")
            st.done(copy(b.xinv_t, ident.unsqueeze(1).broadcast_to([P, 8, P])), "init_xt")
            yield
            yield from range(3 * LEVELS + 8)
            st.after("act", "hi")
            st.done(tt(alo[:, KH + p, :], b.rw, ahi[:, KH + p, :].bitcast(F32), ALU.subtract), "lo")
            yield

        def sp_phase1(sp):
            first = sum(n for _, n in CONSTS[0:2])
            sp.dma_start(consts[:, 0:first], consts_in[:, 0:first]).then_inc(consts_in_sem, 16)
            x_view = w["x"][0].rearrange("(t p) d -> p t d", p=P)
            for t in range(NT):
                sp.dma_start(x_rows[:, t, :], x_view[:, t, :]).then_inc(x_in[t], 16)
                if t == 0:
                    load_gain(sp, "norm_mix_pre")
            load_slabs(sp, sp_slab, RAW)
            sp.dma_start(cols[:, :], cols_in).then_inc(cols_loaded, 16)
            sp.dma_start(consts[:, first:], consts_in[:, first:]).then_inc(masks_in, 16)
            load_slabs(sp, sp_slab, RAW + 2)
            sp.wait_ge(rows_normed, NT)
            load_gain(sp, "attn_out_gain")
            sp.wait_ge(cols_lo, 2 * NT)
            sp.dma_start(lora_w[0:W_LORA, :], w["decay_up"][0]).then_inc(small_in, 16)
            sp.dma_start(lora_w[W_LORA:2 * W_LORA, :], w["aaa_up"][0]).then_inc(small_in, 16)
            sp.dma_start(gate_w[:, :], w["gate_up"][0]).then_inc(small_in, 16)
            load_slabs(sp, sp_slab, slab_no["lora0"] + 1 + RAW)
            sp.wait_ge(zeros_made, 1)
            sp.dma_start(slots_dram.rearrange("(t p) d -> p t d", p=P),
                         gain_row[:, :].unsqueeze(1).broadcast_to([P, MOE_TILES, D])).then_inc(slots_zeroed, 16)
            sp.dma_start(y_dram[NE * P:, :].rearrange("(t p) d -> p t d", p=P),
                         gain_row[:, :].unsqueeze(1).broadcast_to([P, EXTRA, D])).then_inc(slots_zeroed, 16)

        put = phase(region)
        x = put("x_res", [P, NT, D])
        after_x = put.at[0]
        fsb = put("f_rows", [P, NT, D])
        normal2 = put("normal2", [P, 2, D])
        scratch2 = put("scratch2", [P, 2, D])
        put.at[0] -= 4 * 4096
        fhi = put("ffn_hi", [P, 2, KD, T], F32R)
        flo = put("ffn_lo", [P, 2, KD, T], F32R)
        relu = put("ffn_relu", [P, 2, T])
        relu2 = put("ffn_relu2", [P, 2, T])
        gained = sb("post_gained_rows", [P, NT, D], at=after_x + 16384 + 2 * 16384)
        post_scratch = sb("post_scratch", [P, 2, D], at=put.at[0] - 8192)
        sums2 = put("sums2", [P, 16])
        psums = put("post_sums", [P, 16])

        mix_out = sem("mix_out")
        post_sq = sem("post_sq")
        post_root = sem("post_root")
        post_scale = sem("post_scale")
        post_gained = sem("post_gained")
        x_added = sem("x_added")
        up_relu = sem("up_relu")
        up_sq = sem("up_sq")
        up_hi = sem("up_hi")
        up_lo = sem("up_lo")

        for hf in range(2):
            plan_deep([f"out.{hf}.0", f"out.{hf}.1"], f"mix.{hf}", read=lambda t, hf=hf: (mix_out, 4 * hf + t + 1))
        plan_turn("ffn", NT, KD)
        for up, down in FFN_ORDER:
            if up is not None:
                for s in range(4):
                    plan_wide(f"up.{up}.{s}", 2, lambda j, up=up, s=s: (up_relu, 8 * up + 2 * s + j + 1))
            else:
                for hf in range(2):
                    plan_deep([f"down.{down}.{hf}.0", f"down.{down}.{hf}.1"], f"down.{down}.{hf}",
                              read=lambda t, hf=hf, down=down: (mix_out, 8 + 8 * down + 4 * hf + t + 1))

        def normal2_of(t):
            return normal2[:, t % 2, :]

        def x_ready_after(n):
            return lambda eng, t: eng.wait_ge(x_added, NT * (n - 1) + t + 1)

        def sp_phase2(sp):
            sp.wait_ge(slots_zeroed, 32)
            load_gain(sp, "norm_mix_post")
            wait_pairs(sp)
            load_gain(sp, "norm_ffn_pre")
            x_view = w["x"][0].rearrange("(t p) d -> p t d", p=P)
            for t in range(NT):
                sp.dma_start(x[:, t, :], x_view[:, t, :]).then_inc(x_in[t], 16)
            load_slabs(sp, sp_slab, slab_no["up.0.0"] + RAW)
            sp.wait_ge(x_added, NT)
            load_gain(sp, "norm_ffn_post")
            load_slabs(sp, sp_slab, slab_no["down.0.0.0"] + RAW)
            sp.wait_ge(rows_normed, turns["ffn"]["tile"] + NT)
            load_gain(sp, "norm_mix_g_2")
            load_slabs(sp, sp_slab, slab_no["glu_gate0"] + RAW)

        def wait_pairs(eng):
            for p in (2, 3):
                eng.wait_ge(*step_of("pool", p, "lo"))

        def pe_phase2(pe):
            columns_ready(pe, "attn1")
            wait_pairs(pe)
            for hf in range(2):
                pe_deep(pe, [f"out.{hf}.0", f"out.{hf}.1"], f"mix.{hf}")
            in_turn(pe_turn(pe, "ffn", normal2_of))
            columns_ready(pe, "ffn")
            for up, down in FFN_ORDER:
                if up is not None:
                    for s in range(4):
                        pe_wide(pe, f"up.{up}.{s}")
                else:
                    pe.wait_ge(up_lo, 8 * down + 8)
                    b = down % 2
                    for hf in range(2):
                        pe_deep(pe, [f"down.{down}.{hf}.0", f"down.{down}.{hf}.1"], f"down.{down}.{hf}",
                                acts=(fhi[:, b, :, :], flo[:, b, :, :]))

        def act_post(act, stage, rows_after):
            for t in range(NT):
                act.wait_ge(mix_out, rows_after + t + 1)
                n = NT * stage + t
                if t >= 2:
                    act.wait_ge(post_sq, n - 1)
                nc.scalar.activation(post_scratch[:, t % 2, :], fsb[:, t, :], ACT.Square, accum_out=psums[:, t:t + 1]).then_inc(post_sq, 1)
                act.wait_ge(post_sq, n + 1)
                nc.scalar.activation(psums[:, 4 + t:5 + t], psums[:, t:t + 1], ACT.Sqrt, scale=1.0 / D,
                                     bias=const("eps")[:, 0:1]).then_inc(post_root, 1)
                yield

        def dve_post(dve, stage):
            for t in range(NT):
                n = NT * stage + t + 1
                dve.wait_ge(post_root, n)
                nc.vector.reciprocal(psums[:, 8 + t:9 + t], psums[:, 4 + t:5 + t]).then_inc(post_scale, 1)
                dve.wait_ge(post_scale, n)
                dve.wait_ge(x_in[t], 2 * 16)
                dve.wait_ge(post_gained, n)
                nc.vector.scalar_tensor_tensor(out=x[:, t, :], in0=gained[:, t, :], scalar=psums[:, 8 + t:9 + t], in1=x[:, t, :],
                                               op0=ALU.mult, op1=ALU.add).then_inc(x_added, 1)
                yield

        def pool_post(pool, stage, rows_after, gain_name):
            for t in range(NT):
                pool.wait_ge(mix_out, rows_after + t + 1)
                nc.gpsimd.tensor_tensor(gained[:, t, :], fsb[:, t, :], gain(pool, gain_name), ALU.mult).then_inc(post_gained, 1)

        def act_phase2(act):
            make_hi(act, act_slab, slab_no["up.0.0"] + 1)
            in_turn(act_post(act, 0, 4), later(2, act_norm(act, "ffn", lambda t: x[:, t, :], x_ready_after(1), scratch2, sums2)),
                    later(4, act_split(act, "ffn", ahi)))
            for up, down in FFN_ORDER:
                if up is not None:
                    for s in range(4):
                        name = f"up.{up}.{s}"
                        make_hi(act, act_slab, slab_no[name] + 1 + SPLIT)
                        for j in range(2):
                            m = 2 * s + j
                            n = 8 * up + m
                            acc = banks.take(act, f"{name}/{j}")
                            if n >= 2:
                                act.wait_ge(up_sq, n - 1)
                            nc.scalar.activation(relu[:, n % 2, :], acc[:, :], ACT.Relu).then_inc(up_relu, 1)
                            act.wait_ge(up_sq, n + 1)
                            nc.scalar.activation(fhi[:, up % 2, m, :], relu2[:, n % 2, :], ACT.Copy).then_inc(up_hi, 1)
                else:
                    make_hi(act, act_slab, slab_no[f"down.{down}.1.1"] + 1 + SPLIT - (down == 3))
            in_turn(act_post(act, 1, 8 + 24 + 4),
                    later(2, act_norm(act, "mix2", lambda t: x[:, t, :], x_ready_after(2), scratch3, sums3)),
                    later(4, act_split(act, "mix2", ahi)))

        def dve_phase2(dve, steps):
            in_turn(dve_out(dve, 0))
            in_turn(dve_out(dve, 1), later(2, dve_post(dve, 0)),
                    later(3, dve_norm(dve, "ffn", lambda t: x[:, t, :], sums2, normal2_of, "norm_ffn_pre")),
                    later(5, dve_split(dve, "ffn", ahi, alo)))
            for up, down in FFN_ORDER:
                if up is not None:
                    for m in range(8):
                        n = 8 * up + m
                        dve.wait_ge(up_relu, n + 1)
                        if n >= 2:
                            dve.wait_ge(up_lo, n - 1)
                        nc.vector.tensor_tensor(relu2[:, n % 2, :], relu[:, n % 2, :], relu[:, n % 2, :], ALU.mult).then_inc(up_sq, 1)
                else:
                    in_turn(dve_down(dve, down, 0))
                    if down < 3:
                        in_turn(dve_down(dve, down, 1))
            in_turn(dve_down(dve, 3, 1), later(2, dve_post(dve, 1)),
                    later(3, dve_norm(dve, "mix2", lambda t: x[:, t, :], sums3, normal3_of, "norm_mix_g_2")),
                    later(5, dve_split(dve, "mix2", ahi, alo)))

        def dve_out(dve, hf):
            for t in range(NT):
                acc = banks.take(dve, f"mix.{hf}/{t}")
                nc.vector.tensor_copy(fsb[:, t, hf * 512:(hf + 1) * 512], acc[:, :]).then_inc(mix_out, 1)
                yield

        def dve_down(dve, down, hf):
            for t in range(NT):
                acc = banks.take(dve, f"down.{down}.{hf}/{t}")
                to = fsb[:, t, hf * 512:(hf + 1) * 512]
                if down == 0:
                    ins = nc.vector.tensor_copy(to, acc[:, :])
                else:
                    dve.wait_ge(mix_out, 8 + 8 * (down - 1) + 4 * hf + t + 1)
                    ins = nc.vector.tensor_tensor(to, to, acc[:, :], ALU.add)
                ins.then_inc(mix_out, 1)
                yield

        def pool_phase2(pool, steps):
            make_lo(pool, pool_slab, slab_no["up.0.0"] + 1)
            pool_post(pool, 0, 4, "norm_mix_post")
            for up, down in FFN_ORDER:
                if up is not None:
                    for s in range(4):
                        make_lo(pool, pool_slab, slab_no[f"up.{up}.{s}"] + 1 + SPLIT)
                        for j in range(2):
                            m = 2 * s + j
                            n = 8 * up + m
                            pool.wait_ge(up_hi, n + 1)
                            nc.gpsimd.tensor_tensor(flo[:, up % 2, m, :], relu2[:, n % 2, :],
                                                    fhi[:, up % 2, m, :].bitcast(F32), ALU.subtract).then_inc(up_lo, 1)
                else:
                    make_lo(pool, pool_slab, slab_no[f"down.{down}.1.1"] + 1 + SPLIT - (down == 3))
            pool_post(pool, 1, 8 + 24 + 4, "norm_ffn_post")

        put = phase(after_x)
        at_glu = put.at[0]
        u_glu = put("u_glu", [P, KH, PAD + T])
        masked3 = sb("masked3", [P, 2, T], at=at_glu)
        probs3 = sb("probs3", [P, 2, T], at=at_glu + 4096)
        peaks3 = sb("peaks3", [P, 64], at=at_glu + 8192)
        esum3 = sb("esum3", [P, 32], at=at_glu + 8448)
        conv = put("conv", [P, KH, T])
        probst3 = sb("probst3", [P, 2, T], at=put.at[0] - 8192)
        gated = sb("gated", [P, 2, T], at=put.at[0] - 4096)
        sig_glu = put("sig_glu", [P, KH, T])
        conv_sq = sb("conv_sq", [P, KH, T], at=put.at[0] - 8192)
        heads3 = sb("heads3", [P, NT, H], at=put.at[0] - 8192)
        uhi = put("u_hi", [P, KH, T], F32R)
        ulo = put("u_lo", [P, KH, T], F32R)
        normal3 = sb("normal3", [P, 2, D], at=after_x + 16384)
        scratch3 = sb("scratch3", [P, 2, D], at=after_x + 24576)
        sig_ga = sb("sig_ga", [P, KD, T], at=put.at[0] - 16384)
        fq, fk = (put(n, [P, KH, T]) for n in ("fq_t", "fk_t"))
        ohi = sb("o_hi", [P, KH, T], F32R, at=put.at[0] - 16384)
        olo = sb("o_lo", [P, KH, T], F32R, at=put.at[0] - 8192)
        fv = put("fv_rows", [P, NT, H])
        merged = put("merged", [P, KD, T])
        crstd = put("conv_rstd", [P, T])
        forget = put("forget", [NHEAD, 3, T])
        minus8 = put("minus8", [NHEAD, NHEAD, P])
        sums3 = put("sums3", [P, 16])

        glu_gate = sem("glu_gate")
        glu_u = sem("glu_u")
        pads = sem("glu_pads")
        fox_in = sem("fox_in")
        forget_in = sem("forget_in")
        forget_dve = sem("forget_dve")
        forget_act = sem("forget_act")
        conv_made = sem("conv_made")
        conv_dev = sem("conv_dev")
        conv_dev2 = sem("conv_dev2")
        conv_sd = sem("conv_sd")
        conv_norm = sem("conv_norm")
        conv_silu = sem("conv_silu_made")
        conv_hi = sem("conv_hi")
        conv_lo = sem("conv_lo")
        gate_sig = sem("gate_sig")
        ga_in = sem("ga_in")
        ga_sig = sem("ga_sig")
        merged_made = sem("merged_made")
        gated_made = sem("gated_made")
        merged_hi = sem("merged_hi")
        merged_lo = sem("merged_lo")

        plan_turn("mix2", NT, KD)
        for s in range(2):
            plan_wide(f"glu_gate{s}", 2, lambda j, s=s: (glu_gate, 2 * s + j + 1))
        for s in range(2):
            plan_wide(f"glu_a{s}", 2, lambda j, s=s: (glu_u, 2 * s + j + 1))
        for s in range(4):
            plan_wide(("fq0", "fq1", "fk0", "fk1")[s], 2, lambda j, s=s: (fox_in, 2 * s + j + 1))
        plan_deep(["fv0", "fv1"], "fv", read=lambda t: (fox_in, 9 + t))
        plan_wide("ff0", 1, lambda j: (forget_in, 1))
        GATE_C = [f"gc.{hf}.{s}" for hf in range(2) for s in range(2)]
        GATE_A = [f"ga.{hf}.{s}" for hf in range(2) for s in range(2)]
        for i, n in enumerate(GATE_C):
            plan_wide(n, 2, lambda j, i=i: (gate_sig, 2 * i + j + 1))
            if i == 1:
                banks.plan("conv_mean", (conv_dev, KH))
            if i == 2:
                banks.plan("conv_var", (conv_sd, 1))

        def beside_fox_units():
            for hf in range(2):
                yield from wide_units(f"pw.{hf}.0", 4, lambda j, hf=hf: (merged_made, 4 * hf + j + 1))
            for i, n in enumerate(GATE_A[0:2]):
                yield from wide_units(n, 2, lambda j, i=i: (ga_in, 2 * i + j + 1))

        in_turn(attn_units("fox", NHEAD, lambda t: (t + 1) * P), beside_fox_units())
        plan_turn("foxo", NT, KH, normalise=False)
        for i, n in enumerate(GATE_A[2:4]):
            plan_wide(n, 2, lambda j, i=i: (ga_sig, 4 + 2 * i + j + 1))
        for hf in range(2):
            plan_wide(f"ab.{hf}.0", 4, lambda j, hf=hf: (gated_made, 4 * hf + j + 1))
        plan_deep(["out2.0.0", "out2.0.1"], "mix2.0", read=lambda t: (x_added, 8 + t + 1))
        plan_turn("mem", NMT, KD)
        plan_deep(["out2.1.0", "out2.1.1"], "mix2.1", read=lambda t: (x_added, 12 + t + 1))

        def normal3_of(t):
            return normal3[:, t % 2, :]

        def sp_phase3(sp):
            load_slabs(sp, sp_slab, slab_no["gc.0.0"])

        def pe_phase3(pe):
            in_turn(pe_turn(pe, "mix2", normal3_of))
            columns_ready(pe, "mix2")
            for n in ("glu_gate0", "glu_gate1", "glu_a0", "glu_a1", "fq0", "fq1", "fk0", "fk1"):
                pe_wide(pe, n)
            pe_deep(pe, ["fv0", "fv1"], "fv")
            pe_wide(pe, "ff0")
            for i, n in enumerate(GATE_C):
                pe_wide(pe, n)
                for at, name, made, src in ((1, "conv_mean", conv_made, conv), (2, "conv_var", conv_dev2, conv_sq)):
                    if i == at:
                        pe.wait_ge(made, KH)
                        acc = banks.open(pe, name)
                        for m in range(KH):
                            ins = nc.tensor.matmul(acc[:, :], const("chan_mean"), src[:, m, :], start=m == 0, stop=m == KH - 1)
                        banks.filled(ins, name)
            pe.wait_ge(fox_in, 12)
            pe.wait_ge(forget_dve, 5)
            in_turn(pe_attn(pe, "fox",
                            lambda h, t: fq[half(h % 2), h // 2, t * P:(t + 1) * P], lambda h, n: fk[half(h % 2), h // 2, 0:n],
                            lambda h, b: fv[:, b, half(h)], probs3, probst3,
                            bias=(lambda h: minus8[:, h, :], lambda n: forget[:, 0, 0:n])),
                    pe_beside_fox(pe))
            in_turn(pe_turn(pe, "foxo", lambda t: heads3[:, t, :], fox_heads_ready))
            for n in GATE_A[2:4]:
                pe_wide(pe, n)
            columns_ready(pe, "foxo")
            for hf in range(2):
                pe_wide(pe, f"ab.{hf}.0", acts=(ohi, olo))
            pe.wait_ge(merged_lo, KD)
            pe_deep(pe, ["out2.0.0", "out2.0.1"], "mix2.0")
            in_turn(pe_turn(pe, "mem", lambda t: normal4m[:, t, :]))
            pe_deep(pe, ["out2.1.0", "out2.1.1"], "mix2.1")

        def pe_beside_fox(pe):
            pe.wait_ge(conv_lo, KH)
            for hf in range(2):
                yield from pe_wide_steps(pe, f"pw.{hf}.0", acts=(uhi, ulo))
            for n in GATE_A[0:2]:
                yield from pe_wide_steps(pe, n)

        def fox_heads_ready(eng, t):
            eng.wait_ge(heads_out, attns["fox"]["base"] + len(attns["fox"]["items"]))

        def act_phase3(act):
            make_hi(act, act_slab, slab_no["glu_gate1"] + 1)
            for s in range(2):
                make_hi(act, act_slab, slab_no[f"glu_gate{s}"] + 1 + SPLIT)
                for j in range(2):
                    acc = banks.take(act, f"glu_gate{s}/{j}")
                    nc.scalar.activation(sig_glu[:, 2 * s + j, :], acc[:, :], ACT.Sigmoid).then_inc(glu_gate, 1)
            for s in range(2):
                make_hi(act, act_slab, slab_no[f"glu_a{s}"] + 1 + SPLIT)
            for s, n in enumerate(("fq0", "fq1", "fk0", "fk1")):
                make_hi(act, act_slab, slab_no[n] + 1 + SPLIT)
                for j in range(2):
                    acc = banks.take(act, f"{n}/{j}")
                    nc.scalar.activation((fq, fk)[s // 2][:, 2 * (s % 2) + j, :], acc[:, :], ACT.Copy).then_inc(fox_in, 1)
            make_hi(act, act_slab, slab_no["fv1"] + 1 + SPLIT)
            for t in range(NT):
                acc = banks.take(act, f"fv/{t}")
                nc.scalar.activation(fv[:, t, :], acc[:, :], ACT.Copy).then_inc(fox_in, 1)
            make_hi(act, act_slab, slab_no["ff0"] + 1 + SPLIT)
            acc = banks.take(act, "ff0/0")
            nc.scalar.activation(forget[:, 0, :], acc[0:NHEAD, :], ACT.Identity, bias=col("fox_bf_2")[0:NHEAD, :]).then_inc(forget_in, 1)
            for i, n in enumerate(GATE_C):
                if i == 2:
                    for m in range(KH):
                        act.wait_ge(conv_dev, m + 1)
                        nc.scalar.activation(conv_sq[:, m, :], conv[:, m, :], ACT.Square).then_inc(conv_dev2, 1)
                if i == 3:
                    acc = banks.take(act, "conv_var")
                    nc.scalar.activation(crstd[:, :], acc[:, :], ACT.Sqrt, bias=const("eps")[:, 0:1]).then_inc(conv_sd, 1)
                    act.wait_ge(forget_dve, 3)
                    nc.scalar.activation(forget[:, 2, :], forget[:, 2, :], ACT.Exp, scale=-1.0).then_inc(forget_act, 1)
                    act.wait_ge(forget_act, 1)
                    nc.scalar.activation(forget[:, 2, :], forget[:, 2, :], ACT.Ln, bias=const("ones")[0:NHEAD, 0:1]).then_inc(forget_act, 1)
                    for m in range(KH):
                        act.wait_ge(conv_norm, m + 1)
                        nc.scalar.activation(conv[:, m, :], conv[:, m, :], ACT.Silu, bias=col("conv_ln_b_2", m)).then_inc(conv_silu, 1)
                        act.wait_ge(conv_silu, m + 1)
                        nc.scalar.activation(uhi[:, m, :], conv[:, m, :], ACT.Copy).then_inc(conv_hi, 1)
                for j in range(2):
                    acc = banks.take(act, f"{n}/{j}")
                    nc.scalar.activation(merged[:, 2 * i + j, :], acc[:, :], ACT.Sigmoid).then_inc(gate_sig, 1)
                make_hi(act, act_slab, slab_no[n] + 1 + SPLIT)
            act.wait_ge(conv_lo, 2)
            in_turn(act_attn(act, "fox", masked3, peaks3, esum3, probs3, probst3), act_beside_fox(act))
            for m in range(4):
                act.wait_ge(ga_in, m + 1)
                nc.scalar.activation(sig_ga[:, m, :], sig_ga[:, m, :], ACT.Sigmoid).then_inc(ga_sig, 1)
            in_turn(act_split(act, "foxo", ohi))
            for i, n in enumerate(GATE_A[2:4]):
                for j in range(2):
                    acc = banks.take(act, f"{n}/{j}")
                    nc.scalar.activation(sig_ga[:, 4 + 2 * i + j, :], acc[:, :], ACT.Sigmoid).then_inc(ga_sig, 1)
                make_hi(act, act_slab, slab_no[n] + 1 + SPLIT)
            for m in range(KD):
                act.wait_ge(merged_made, 9 + m)
                nc.scalar.activation(ahi[:, m, :], merged[:, m, :], ACT.Copy).then_inc(merged_hi, 1)
                if m % 4 == 3:
                    make_hi(act, act_slab, slab_no[f"ab.{m // 4}.0"] + 1 + SPLIT)

        def act_beside_fox(act):
            for hf in range(2):
                yield from range(4 * WIDE_STEPS - 1)
                make_hi(act, act_slab, slab_no[f"pw.{hf}.0"] + 1 + SPLIT)
                yield
            for i, n in enumerate(GATE_A[0:2]):
                for j in range(2):
                    yield from range(WIDE_STEPS - 1)
                    acc = banks.take(act, f"{n}/{j}")
                    nc.scalar.activation(sig_ga[:, 2 * i + j, :], acc[:, :], ACT.Copy).then_inc(ga_in, 1)
                    if j:
                        make_hi(act, act_slab, slab_no[n] + 1 + SPLIT)
                    yield

        def dve_beside_fox(dve):
            for m in range(KD):
                yield from range(WIDE_STEPS - 1)
                acc = banks.take(dve, f"pw.{m // 4}.0/{m % 4}")
                dve.wait_ge(gate_sig, m + 1)
                nc.vector.tensor_tensor(merged[:, m, :], acc[:, :], merged[:, m, :], ALU.mult).then_inc(merged_made, 1)
                yield

        def dve_phase3(dve, steps):
            for m in range(KH):
                acc = banks.take(dve, f"glu_a{m // 2}/{m % 2}")
                dve.wait_ge(glu_gate, m + 1)
                nc.vector.tensor_tensor(u_glu[:, m, PAD:PAD + T], acc[:, :], sig_glu[:, m, :], ALU.mult).then_inc(glu_u, 1)
            dve.wait_ge(pads, 1)
            dve.wait_ge(glu_u, KH)
            before = [0] * KH
            for m in range(KH):
                before[m] = steps.mark(nc.vector.tensor_scalar(conv[:, m, :], u_glu[:, m, 0:T], col("conv_dw_w_2", m),
                                                               col("conv_dw_b_2", m), ALU.mult, ALU.add))
            for j in range(1, TAPS):
                for m in range(KH):
                    steps.after(before[m])
                    ins = nc.vector.scalar_tensor_tensor(out=conv[:, m, :], in0=u_glu[:, m, j:j + T],
                                                         scalar=col("conv_dw_w_2", KH * j + m), in1=conv[:, m, :],
                                                         op0=ALU.mult, op1=ALU.add)
                    if j < TAPS - 1:
                        before[m] = steps.mark(ins)
                    else:
                        ins.then_inc(conv_made, 1)
            nc.vector.tensor_scalar(minus8[:, :, :], ident[0:NHEAD, 0:NHEAD].unsqueeze(2).broadcast_to([NHEAD, NHEAD, P]),
                                    -float(HD) ** 0.5, None, ALU.mult).then_inc(forget_dve, 1)
            dve.wait_ge(forget_in, 1)
            nc.vector.tensor_scalar(forget[:, 1, :], forget[:, 0, :], 0.0, None, ALU.min).then_inc(forget_dve, 1)
            dve.wait_ge(forget_dve, 2)
            nc.vector.scalar_tensor_tensor(out=forget[:, 2, :], in0=forget[:, 1, :], scalar=-2.0, in1=forget[:, 0, :],
                                           op0=ALU.mult, op1=ALU.add).then_inc(forget_dve, 1)
            acc = banks.take(dve, "conv_mean")
            for m in range(KH):
                nc.vector.tensor_tensor(conv[:, m, :], conv[:, m, :], acc[:, :], ALU.subtract).then_inc(conv_dev, 1)
            dve.wait_ge(conv_sd, 1)
            steps.link(nc.vector.reciprocal(crstd[:, :], crstd[:, :]))
            dve.wait_ge(conv_dev, KH)
            for m in range(KH):
                nc.vector.scalar_tensor_tensor(out=conv[:, m, :], in0=conv[:, m, :], scalar=col("conv_ln_g_2", m), in1=crstd[:, :],
                                               op0=ALU.mult, op1=ALU.mult).then_inc(conv_norm, 1)
            dve.wait_ge(forget_act, 2)
            nc.vector.tensor_tensor(forget[:, 1, :], forget[:, 1, :], forget[:, 2, :], ALU.subtract).then_inc(forget_dve, 1)
            dve.wait_ge(forget_dve, 4)
            nc.vector.tensor_tensor_scan(forget[:, 0, :], const("ones")[0:NHEAD, 0:1].broadcast_to([NHEAD, T]), forget[:, 1, :],
                                         0.0, ALU.mult, ALU.add).then_inc(forget_dve, 1)
            in_turn(dve_attn(dve, steps, "fox", HD ** -0.5, const("band_causal"), masked3, peaks3, esum3,
                             lambda h, t: heads3[:, t, half(h)]),
                    dve_beside_fox(dve))
            in_turn(dve_split(dve, "foxo", ohi, olo))
            for m in range(KD):
                acc = banks.take(dve, f"ab.{m // 4}.0/{m % 4}")
                dve.wait_ge(ga_sig, m + 1)
                if m >= 2:
                    dve.wait_ge(merged_made, KD + m - 1)
                nc.vector.tensor_tensor(gated[:, m % 2, :], acc[:, :], sig_ga[:, m, :], ALU.mult).then_inc(gated_made, 1)
                dve.wait_ge(gated_made, m + 1)
                dve.wait_ge(merged_made, m + 1)
                nc.vector.tensor_tensor(merged[:, m, :], merged[:, m, :], gated[:, m % 2, :], ALU.add).then_inc(merged_made, 1)
                if m:
                    dve_merged_lo(dve, m - 1)
            dve_merged_lo(dve, KD - 1)
            in_turn(dve_norm(dve, "mem", lambda t: mem_rows[:, t, :], sums4m, lambda t: normal4m[:, t, :], "norm_mem_g_2"))
            in_turn(dve_add(dve, "mix2", 0))
            in_turn(dve_split(dve, "mem", mhi, mlo))
            in_turn(dve_add(dve, "mix2", 1), later(1, dve_norm(dve, "xa", lambda t: x[:, t, :], sums4, normal4_of, "norm_xa_g_2", buffers=NT)))

        def dve_merged_lo(dve, m):
            dve.wait_ge(merged_hi, m + 1)
            nc.vector.tensor_tensor(alo[:, m, :], merged[:, m, :], ahi[:, m, :].bitcast(F32), ALU.subtract).then_inc(merged_lo, 1)

        def dve_add(dve, unit, hf):
            for t in range(NT):
                acc = banks.take(dve, f"{unit}.{hf}/{t}")
                to = x[:, t, hf * 512:(hf + 1) * 512]
                nc.vector.tensor_tensor(to, to, acc[:, :], ALU.add).then_inc(x_added, 1)
                yield

        def pool_phase3(pool, steps):
            pool.wait_ge(cols_lo, turns["mix2"]["split"] + 2 * NT)
            nc.gpsimd.memset(u_glu[:, :, 0:PAD], 0.0).then_inc(pads, 1)
            make_lo(pool, pool_slab, slab_no[GATE_C[2]] + 1 + SPLIT)
            for m in range(KH):
                pool.wait_ge(conv_hi, m + 1)
                nc.gpsimd.tensor_tensor(ulo[:, m, :], conv[:, m, :], uhi[:, m, :].bitcast(F32), ALU.subtract).then_inc(conv_lo, 1)
            make_lo(pool, pool_slab, slab_no["ga.0.1"] + 1 + SPLIT)
            make_lo(pool, pool_slab, slab_no["ab.1.0"] + 1 + SPLIT)

        put = phase(after_x)
        mem_rows = put("mem_rows", [P, NMT, D])
        scratch4 = put("scratch4", [P, 2, D])
        normal4 = put("normal4", [P, NT, D])
        normal4m = put("normal4m", [P, NMT, D])
        mhi = put("mem_hi", [P, KD, MEM], F32R)
        mlo = put("mem_lo", [P, KD, MEM], F32R)
        kx = put("kx_t", [P, XH, MEM])
        vx = put("vx_rows", [P, NMT, H])
        qx = put("qx_t", [P, XH, T])
        masked4 = put("masked4", [P, 2, MEM])
        probs4 = put("probs4", [P, 2, MEM])
        probst4 = put("probst4", [P, 2, MEM])
        sums4m = put("sums4m", [P, 16])
        sums4 = put("sums4", [P, 16])
        peaks4 = put("peaks4", [P, 64])
        esum4 = put("esum4", [P, 32])
        heads4 = sb("heads4", [P, NT, H], at=act_at)
        xohi = sb("xo_hi", [P, KH, T], F32R, at=act_at + 8192)
        xolo = sb("xo_lo", [P, KH, T], F32R, at=act_at + 16384)

        mem_in = sem("mem_in")
        cross_in = sem("cross_in")

        for s in range(2):
            plan_wide(f"xk{s}", 2, lambda j, s=s: (cross_in, 2 * s + j + 1))
        plan_turn("xa", NT, KD)
        plan_deep(["xv0", "xv1"], "xv", NMT, lambda t: (cross_in, 5 + t))
        for s in range(2):
            plan_wide(f"xq{s}", 2, lambda j, s=s: (cross_in, 7 + 2 * s + j))
        XO_AFTER = XH + 2

        def cross_out_units():
            yield from range(XO_AFTER)
            turning = turn_units("xao", NT, KH, normalise=False)
            for t in range(NT):
                next(turning)
                yield from range(2)
                for hf in range(2):
                    banks.plan(f"xo.{hf}/{t}", (x_added, 16 + 2 * t + hf + 1))
                    yield
            in_turn(turning)

        MOE_AFTER = XO_AFTER + XH + 3

        def router_units():
            yield from range(MOE_AFTER)
            turning = turn_units("moe", NT, KD, split=False)
            for t in range(NT):
                next(turning)
                yield from range(2)
                banks.plan(f"logits/{t}", (logits_made, t + 1))
                yield from range(2)
            in_turn(turning)

        logits_made = sem("logits_made")
        in_turn(attn_units("xa", XH, lambda t: MEM, by_tile=True), cross_out_units(), router_units())

        def mem_ready(eng, t):
            eng.wait_ge(mem_in, 16 * NMT)

        def normal4_of(t):
            return normal4[:, t, :]

        def cross_heads_ready(eng, t):
            eng.wait_ge(heads_out, attns["xa"]["base"] + XH * (t + 1))

        def sp_phase4(sp):
            sp.wait_ge(x_added, 2 * NT)
            load_gain(sp, "norm_mem_g_2")
            sp.wait_ge(rows_normed, turns["mix2"]["tile"] + NT)
            load_gain(sp, "norm_xa_g_2")
            load_slabs(sp, sp_slab, slab_no["out2.1.1"] + 1)
            sp.wait_ge(merged_lo, KD)
            mem_view = w["mem_2"][0].rearrange("(t p) d -> p t d", p=P)
            for t in range(NMT):
                sp.dma_start(mem_rows[:, t, :], mem_view[:, t, :]).then_inc(mem_in, 16)
            load_slabs(sp, sp_slab, len(slabs))

        def pe_phase4(pe):
            columns_ready(pe, "mem")
            for s in range(2):
                pe_wide(pe, f"xk{s}", tokens=MEM, acts=(mhi, mlo))
            in_turn(pe_turn(pe, "xa", normal4_of))
            pe_deep(pe, ["xv0", "xv1"], "xv", tiles=NMT, acts=(mhi, mlo))
            columns_ready(pe, "xa")
            for s in range(2):
                pe_wide(pe, f"xq{s}")
            pe.wait_ge(cross_in, 10)
            in_turn(pe_attn(pe, "xa", lambda h, t: qx[:, h, t * P:(t + 1) * P], lambda h, n: kx[:, h, 0:n],
                            lambda h, b: vx[:, b, h * XHD:(h + 1) * XHD], probs4, probst4),
                    pe_cross_out(pe), pe_router(pe))

        def pe_cross_out(pe):
            yield from range(XO_AFTER)
            turning = pe_turn(pe, "xao", lambda t: heads4[:, t, :], cross_heads_ready)
            for t in range(NT):
                next(turning)
                yield from range(2)
                for hf in range(2):
                    n = slab_no[f"xo.{hf}.0"]
                    k, c = slab_shape(n)
                    pe.wait_ge(lo_made, n + 1)
                    pe.wait_ge(cols_lo, turns["xao"]["split"] + t + 1)
                    wh, wl = view(whi, n % SPLIT, k, c), view(wlo, n % SPLIT, k, c)
                    ts = slice(t * P, (t + 1) * P)
                    acc = banks.open(pe, f"xo.{hf}/{t}")
                    ins = three_passes(acc[:, :], [((xohi[:, i, ts], xolo[:, i, ts]), (wh[:, i, :], wl[:, i, :])) for i in range(k)],
                                       True, True)
                    banks.filled(ins, f"xo.{hf}/{t}")
                    yield

        def pe_router(pe):
            yield from range(MOE_AFTER)
            turning = pe_turn(pe, "moe", hn_of)
            for t in range(NT):
                next(turning)
                yield from range(2)
                if t == 0:
                    pe.wait_ge(router_in, 64)
                pe.wait_ge(cols_plain, 2 * (t + 1))
                acc = banks.open(pe, f"logits/{t}")
                for k in range(KD):
                    ins = nc.tensor.matmul(acc[:, 0:NG + NE], h_t[:, k, t * P:(t + 1) * P], router_w[:, k, :],
                                           start=k == 0, stop=k == KD - 1)
                banks.filled(ins, f"logits/{t}")
                yield from range(2)

        def act_phase4(act):
            in_turn(act_norm(act, "mem", lambda t: mem_rows[:, t, :], mem_ready, scratch4, sums4m))
            make_hi(act, act_slab, slab_no["out2.1.1"] + 1)
            in_turn(act_split(act, "mem", mhi))
            make_hi(act, act_slab, slab_no["xk0"] + 1)
            in_turn(act_norm(act, "xa", lambda t: x[:, t, :], x_ready_after(4), scratch4, sums4))
            for s in range(2):
                make_hi(act, act_slab, slab_no[f"xk{s}"] + 1 + SPLIT)
                for j in range(2):
                    acc = banks.take(act, f"xk{s}/{j}")
                    nc.scalar.activation(kx[:, 2 * s + j, :], acc[:, 0:MEM], ACT.Copy).then_inc(cross_in, 1)
            in_turn(act_split(act, "xa", ahi))
            make_hi(act, act_slab, slab_no["xv1"] + 1 + SPLIT)
            for t in range(NMT):
                acc = banks.take(act, f"xv/{t}")
                nc.scalar.activation(vx[:, t, :], acc[:, :], ACT.Copy).then_inc(cross_in, 1)
            for s in range(2):
                make_hi(act, act_slab, slab_no[f"xq{s}"] + 1 + SPLIT)
                for j in range(2):
                    acc = banks.take(act, f"xq{s}/{j}")
                    nc.scalar.activation(qx[:, 2 * s + j, :], acc[:, :], ACT.Copy).then_inc(cross_in, 1)
            in_turn(act_attn(act, "xa", masked4, peaks4, esum4, probs4, probst4), act_cross_out(act), act_router(act))

        def act_router(act):
            yield from range(MOE_AFTER)
            for _ in act_plain(act, "moe", h_t):
                yield from range(XH)

        def act_cross_out(act):
            yield from range(XO_AFTER)
            splitting = act_split(act, "xao", xohi)
            norm = act_norm(act, "moe", lambda t: x[:, t, :], cross_added, scratch5, sums5)
            for t in range(NT):
                next(splitting)
                yield
                if t:
                    next(norm)
                yield from range(3)
            next(norm)

        def cross_added(eng, t):
            eng.wait_ge(x_added, 4 * NT + 2 * t + 2)

        def dve_phase4(dve, steps):
            in_turn(dve_split(dve, "xa", ahi, alo))
            in_turn(dve_attn(dve, steps, "xa", XHD ** -0.5, None, masked4, peaks4, esum4,
                             lambda h, t: heads4[:, t, h * XHD:(h + 1) * XHD]),
                    dve_cross_out(dve), dve_router(dve))

        def dve_router(dve):
            yield from range(MOE_AFTER)
            for t in range(NT):
                yield from range(2)
                acc = banks.take(dve, f"logits/{t}")
                if t == 0:
                    dve.wait_ge(router_in, 64)
                nc.vector.tensor_tensor(logits[:, t, :], acc[:, 0:NG + NE], router_b[:, :], ALU.add).then_inc(logits_made, 1)
                yield from range(2)

        def dve_cross_out(dve):
            yield from range(XO_AFTER)
            splitting = dve_split(dve, "xao", xohi, xolo)
            norm = dve_norm(dve, "moe", lambda t: x[:, t, :], sums5, hn_of, "norm_moe_g_2", buffers=NT)
            for t in range(NT):
                next(splitting)
                yield from range(2)
                for hf in range(2):
                    acc = banks.take(dve, f"xo.{hf}/{t}")
                    to = x[:, t, hf * 512:(hf + 1) * 512]
                    nc.vector.tensor_tensor(to, to, acc[:, :], ALU.add).then_inc(x_added, 1)
                    if hf == 0 and t:
                        next(norm)
                    yield
            next(norm)

        def pool_phase4(pool, steps):
            make_lo(pool, pool_slab, len(slabs))

        put = phase(after_x)
        hn = put("hn_rows", [P, NT, D])
        scratch5 = put("scratch5", [P, 2, D])
        h_t = put("h_cols", [P, KD, T])
        sums5 = put("sums5", [P, 16])
        router_w = put("router_w", [P, KD, NG + NE])
        router_b = put("router_b", [P, NG + NE])
        logits = put("logits", [P, NT, NG + NE])
        small4 = put("small4", [P, 12, NT])
        group16 = put("group16", [P, 8, NT, EPG])
        by_expert = put("by_expert", [P, 4, NT, NG, EPG])
        picks_upto = put("picks_upto", [P, NT, NE])
        edges = put("edges", [P, NE, 3])
        expert16 = put("expert16", [P, 5, NE])
        later_tiles = put("later_tiles", [P, EXTRA, NE])
        later_sum = put("later_sum", [P, 8])
        later_expert = put("later_expert", [P, 8], I32)
        slot_f = put("slot_f", [P, TOPK, NT])
        slot = put("slot", [P, TOPK, NT], I32)
        weight = put("weight", [P, TOPK, NT])
        rows = put("expert_rows", [P, 2, D])
        silu5 = put("expert_silu", [P, 2, EF])
        hidden = put("expert_hidden", [P, 2, EF])
        hidden_t = put("expert_hidden_t", [P, 2, EF])
        down_w = sb("expert_down", [P, 2, EF // P, D], at=ring_at)
        x_t = sb("expert_x_t", [P, 2, KD, P], at=ring_at + 16384)
        y_rows = sb("expert_y", [P, 2, D], at=ring_at + 24576)
        gate_up = sb("expert_gate_up", [P, 2, KD, 2 * EF], at=act_at)
        y_pair = sb("y_pair", [P, NT, TOPK, D], at=after_x)
        final_sq = sb("final_sq", [P, 2, D], at=act_at)
        out_rows = sb("out_rows", [P, NT, D], at=act_at + 8192)

        slots_dram = nc.dram_tensor("expert_rows_dram", (SLOTS, D), F32, kind="Internal").ap()
        y_dram = nc.dram_tensor("expert_y_dram", (SLOTS, D), F32, kind="Internal").ap()

        router_in = sem("router_in")
        slots_zeroed = sem("slots_zeroed")
        zeros_made = sem("zeros_made")
        route_exp_in = sem("route_exp_in")
        route_exps = sem("route_exps")
        picks_made = sem("picks_made")
        slots_made = sem("slots_made")
        weights_made = sem("weights_made")
        rows_placed = sem("rows_placed")
        y_gathered = [sem(f"y_gathered{t}") for t in range(NT)]
        y_sums = sem("y_sums")
        final_squares = sem("final_squares")
        final_root = sem("final_root")
        final_rows = sem("final_rows")
        out_stored = sem("out_stored")

        def two(name):
            return [sem(f"{name}{s}") for s in range(2)]

        gate_up_in, down_in, rows_in = two("gate_up_in"), two("down_in"), two("rows_in")
        rows_turned = two("rows_turned")
        x_t_made = two("x_t_made")
        gate_up_made = two("gate_up_made")
        silu_made = two("silu_made")
        hidden_made = two("hidden_made")
        hidden_turned = two("hidden_turned")
        hidden_t_made = two("hidden_t_made")
        y_made = two("y_made")
        y_left = two("y_left")
        y_right = two("y_right")
        y_stored = two("y_stored")

        banks.plan("ranks", (slots_made, 1))
        TURN_BANKS, GATE_UP_BANKS, HIDDEN_BANKS, Y_BANKS = ([banks.banks[2 * i], banks.banks[2 * i + 1]] for i in range(4))

        def hn_of(t):
            return hn[:, t, :]

        def unless_first(eng, sem_, n):
            if not isinstance(n, int) or n > 0:
                eng.wait_ge(sem_, n)

        def later_tiles_used(eng):
            eng.wait_ge(slots_made, 2)
            return eng.value_load(later_expert[0:1, EXTRA:EXTRA + 1], min_val=0, max_val=EXTRA)

        def turn_rows(pe, r, s):
            pe.wait_ge(rows_in[s], 16 * (r + 1))
            unless_first(pe, x_t_made[1 - s], 2 * (r + s))
            for h in range(2):
                for j in range(4):
                    c = (4 * h + j) * P
                    ins = nc.tensor.transpose(TURN_BANKS[h][:, j * P:(j + 1) * P], rows[:, s, c:c + P], ident)
            ins.then_inc(rows_turned[s], 1)

        def pe_gate_up(pe, r, s):
            pe.wait_ge(x_t_made[s], 2 * (r + 1))
            pe.wait_ge(gate_up_in[s], 32 * (r + 1))
            unless_first(pe, hidden_made[s], r)
            for k in range(KD):
                ins = nc.tensor.matmul(GATE_UP_BANKS[s][:, :], x_t[:, s, k, :], gate_up[:, s, k, :], start=k == 0, stop=k == KD - 1)
            ins.then_inc(gate_up_made[s], 1)

        def turn_hidden(pe, r, s):
            pe.wait_ge(hidden_made[s], r + 1)
            unless_first(pe, hidden_t_made[s], r)
            for j in range(EF // P):
                ins = nc.tensor.transpose(HIDDEN_BANKS[s][:, j * P:(j + 1) * P], hidden[:, s, j * P:(j + 1) * P], ident)
            ins.then_inc(hidden_turned[s], 1)

        def pe_down(pe, r, s):
            pe.wait_ge(hidden_t_made[s], r + 1)
            pe.wait_ge(down_in[s], 16 * (r + 1))
            unless_first(pe, y_left[1 - s], r + s)
            unless_first(pe, y_right[1 - s], r + s)
            for k in range(EF // P):
                for h in range(2):
                    ins = nc.tensor.matmul(Y_BANKS[h][:, :], hidden_t[:, s, k * P:(k + 1) * P], down_w[:, s, k, h * 512:(h + 1) * 512],
                                           start=k == 0, stop=k == EF // P - 1)
            ins.then_inc(y_made[s], 1)

        def pe_step(pe, r, s, last=False):
            before, after = (r - 1 + s, 1 - s), (r + s, 1 - s)
            pe_gate_up(pe, r, s)
            turn_hidden(pe, *before)
            if not last:
                turn_rows(pe, *after)
            pe_down(pe, *before)

        def pe_tile(pe, r, s):
            turn_rows(pe, r, s)
            pe_gate_up(pe, r, s)
            turn_hidden(pe, r, s)
            pe_down(pe, r, s)

        def pe_phase5(pe):
            pe.wait_ge(picks_made, 3)
            acc = banks.open(pe, "ranks")
            nc.tensor.matmul(acc[:, 0:NT * NE], const("before"), by_expert[:, 2, :, :, :].rearrange("p t g e -> p (t g e)"),
                             start=True, stop=False, skip_group_check=True)
            pe.wait_ge(picks_made, 3 + NT)
            upto = picks_upto[:, :, :].rearrange("p t n -> p (t n)")
            for to, of in ((slice(NE, NT * NE), slice(0, (NT - 1) * NE)), (slice(NT * NE, (NT + 1) * NE), slice((NT - 1) * NE, NT * NE))):
                ins = nc.tensor.matmul(acc[:, to], const("ones"), upto[:, of], start=False, stop=True, skip_group_check=True)
            banks.filled(ins, "ranks")
            turn_rows(pe, 0, 0)
            pe_gate_up(pe, 0, 0)
            turn_rows(pe, 0, 1)
            pe_step(pe, 0, 1)
            pe_step(pe, 1, 0)
            used = later_tiles_used(pe)
            with pe.Fori(1, FIRST_PAIRS - 1) as r:
                pe_step(pe, r, 1)
                pe_step(pe, r + 1, 0)
            pe_step(pe, FIRST_PAIRS - 1, 1, last=True)
            turn_hidden(pe, FIRST_PAIRS - 1, 1)
            pe_down(pe, FIRST_PAIRS - 1, 1)
            with pe.Fori(FIRST_PAIRS, PAIRS) as r:
                for s in range(2):
                    with pe.If(used > 2 * r + (s - NE)):
                        pe_tile(pe, r, s)
            with pe.If(used > EXTRA - 1):
                pe_tile(pe, PAIRS, 0)

        def act_tile(act, r, s):
            act.wait_ge(gate_up_made[s], r + 1)
            unless_first(act, hidden_made[s], r)
            nc.scalar.activation(silu5[:, s, :], GATE_UP_BANKS[s][:, 0:EF], ACT.Silu).then_inc(silu_made[s], 1)
            act.wait_ge(hidden_turned[s], r + 1)
            unless_first(act, y_made[s], r)
            nc.scalar.activation(hidden_t[:, s, :], HIDDEN_BANKS[s][:, 0:EF], ACT.Copy).then_inc(hidden_t_made[s], 1)
            act.wait_ge(y_made[s], r + 1)
            unless_first(act, y_stored[s], 16 * r)
            nc.scalar.activation(y_rows[:, s, 512:1024], Y_BANKS[1][:, :], ACT.Copy).then_inc(y_right[s], 1)

        def act_phase5(act):
            act.wait_ge(route_exp_in, 1)
            nc.scalar.activation(group16[:, 1, :, :], group16[:, 0, :, :], ACT.Exp).then_inc(route_exps, 1)
            act.wait_ge(route_exp_in, 2)
            nc.scalar.activation(small4[:, 4, :], small4[:, 3, :], ACT.Exp).then_inc(route_exps, 1)
            act_tile(act, 0, 0)
            act_tile(act, 0, 1)
            used = later_tiles_used(act)
            with act.Fori(1, FIRST_PAIRS) as r:
                act_tile(act, r, 0)
                act_tile(act, r, 1)
            with act.Fori(FIRST_PAIRS, PAIRS) as r:
                for s in range(2):
                    with act.If(used > 2 * r + (s - NE)):
                        act_tile(act, r, s)
            with act.If(used > EXTRA - 1):
                act_tile(act, PAIRS, 0)
            for t in range(NT):
                act.wait_ge(y_sums, 2 * t + 2)
                if t >= 2:
                    act.wait_ge(final_squares, t - 1)
                nc.scalar.activation(final_sq[:, t % 2, :], x[:, t, :], ACT.Square, accum_out=sums5[:, t:t + 1]).then_inc(final_squares, 1)
                act.wait_ge(final_squares, t + 1)
                nc.scalar.activation(sums5[:, 4 + t:5 + t], sums5[:, t:t + 1], ACT.Sqrt, scale=1.0 / D,
                                     bias=const("eps")[:, 0:1]).then_inc(final_root, 1)

        def dve_first_max(steps, values, peak, one):
            tt = nc.vector.tensor_tensor
            steps.link(nc.vector.tensor_reduce(peak, values, AX_X, ALU.max))
            steps.link(tt(one, values, peak.unsqueeze(2).broadcast_to([P, NT, 4]), ALU.is_equal))
            steps.link(tt(one, one, const("first4").unsqueeze(1).broadcast_to([P, NT, 4]), ALU.mult))
            top = small4[:, 11, :]
            steps.link(nc.vector.tensor_reduce(top, one, AX_X, ALU.max))
            steps.link(tt(one, one, top.unsqueeze(2).broadcast_to([P, NT, 4]), ALU.is_equal))

        def dve_route(dve, steps):
            tt, stt, tsc, reduce = (nc.vector.tensor_tensor, nc.vector.scalar_tensor_tensor, nc.vector.tensor_scalar,
                                    nc.vector.tensor_reduce)
            dve.wait_ge(logits_made, NT)
            g = logits[:, :, 0:NG]
            e = logits[:, :, NG:NG + NE].rearrange("p t (g e) -> p t g e", g=NG)
            g_peak, peak1, peak2, gap, gap_exp, g_sum, den, pw = (small4[:, i, :] for i in range(8))
            g_gap, g_exp, g_one, one1, one2, e_of, e_rest = (group16[:, i, :, :] for i in range(7))
            dve_first_max(steps, g, g_peak, g_one)
            tt(g_gap, g, g_peak.unsqueeze(2).broadcast_to([P, NT, NG]), ALU.subtract).then_inc(route_exp_in, 1)
            over = g_one.unsqueeze(3).broadcast_to([P, NT, NG, EPG])
            steps.link(tt(by_expert[:, 3], e, over, ALU.mult))
            steps.link(reduce(e_of, by_expert[:, 3].rearrange("p t g e -> p t e g"), AX_X, ALU.add))
            dve_first_max(steps, e_of, peak1, one1)
            steps.link(stt(out=e_rest, in0=one1, scalar=NEG, in1=e_of, op0=ALU.mult, op1=ALU.add))
            dve_first_max(steps, e_rest, peak2, one2)
            tt(gap, peak2, peak1, ALU.subtract).then_inc(route_exp_in, 1)
            for k, one in enumerate((one1, one2)):
                tt(by_expert[:, k], over, one.unsqueeze(2).broadcast_to([P, NT, NG, EPG]), ALU.mult).then_inc(picks_made, 1)
            dve.wait_ge(picks_made, 2)
            tt(by_expert[:, 2], by_expert[:, 0], by_expert[:, 1], ALU.add).then_inc(picks_made, 1)
            dve.wait_ge(picks_made, 3)
            picks = by_expert[:, 2, :, :, :].rearrange("p t g e -> p t (g e)")
            nc.vector.tensor_copy(picks_upto[:, 0, :], picks[:, 0, :]).then_inc(picks_made, 1)
            for t in range(1, NT):
                dve.wait_ge(picks_made, 3 + t)
                tt(picks_upto[:, t, :], picks_upto[:, t - 1, :], picks[:, t, :], ALU.add).then_inc(picks_made, 1)
            dve.wait_ge(route_exps, 2)
            steps.link(reduce(g_sum, g_exp, AX_X, ALU.add))
            steps.link(tsc(den, gap_exp, 1.0, None, ALU.add))
            steps.link(tt(den, den, g_sum, ALU.mult))
            steps.link(nc.vector.reciprocal(weight[:, 0, :], den))
            tt(weight[:, 1, :], weight[:, 0, :], gap_exp, ALU.mult).then_inc(weights_made, 1)
            extra, to, start, shift = (expert16[:, i, :] for i in range(4))
            numbers = const("tile_no")
            acc = banks.take(dve, "ranks")
            count = acc[:, NT * NE:(NT + 1) * NE]
            rank = acc[:, 0:NT * NE].rearrange("p (t n) -> p t n", t=NT)
            steps.link(tt(edges[:, :, :], count.unsqueeze(2).broadcast_to([P, NE, 3]),
                          const("tile_edges")[:, 1:4].unsqueeze(1).broadcast_to([P, NE, 3]), ALU.is_gt))
            steps.link(reduce(extra, edges[:, :, :], AX_X, ALU.add))
            steps.link(nc.vector.tensor_tensor_scan(to, const("ones")[:, 0:NE], extra, 0.0, ALU.mult, ALU.add))
            steps.link(tt(start, to, extra, ALU.subtract))
            steps.link(tt(start, start, numbers[:, 0:NE], ALU.subtract))
            steps.link(tsc(shift, start, float(NE - 1), float(P), ALU.add, ALU.mult))
            by = [by_expert[:, i].rearrange("p t g e -> p t (g e)") for i in range(4)]
            steps.link(tsc(by[3], rank, float(P), None, ALU.is_ge))
            steps.link(tt(by[3], by[3], shift.unsqueeze(1).broadcast_to([P, NT, NE]), ALU.mult))
            steps.link(tt(by[3], by[3], rank, ALU.add))
            steps.link(stt(out=by[3], in0=numbers[:, 0:NE].unsqueeze(1).broadcast_to([P, NT, NE]), scalar=float(P), in1=by[3],
                           op0=ALU.mult, op1=ALU.add))
            for k in range(TOPK):
                steps.link(tt(by[k], by[k], by[3], ALU.mult))
                steps.link(reduce(slot_f[:, k, :], by[k], AX_X, ALU.add))
            nc.vector.tensor_copy(slot[:, :, :], slot_f[:, :, :]).then_inc(slots_made, 1)
            steps.link(tt(later_tiles[:, :, :], to.unsqueeze(1).broadcast_to([P, EXTRA, NE]),
                          numbers[:, 0:EXTRA].unsqueeze(2).broadcast_to([P, EXTRA, NE]), ALU.is_le))
            steps.link(reduce(later_sum[:, 0:EXTRA], later_tiles[:, :, :], AX_X, ALU.add))
            steps.link(tsc(later_sum[:, 0:EXTRA], later_sum[:, 0:EXTRA], float(NE - 1), None, ALU.min))
            steps.link(nc.vector.tensor_copy(later_sum[:, EXTRA:EXTRA + 1], to[:, NE - 1:NE]))
            nc.vector.tensor_copy(later_expert[:, 0:EXTRA + 1], later_sum[:, 0:EXTRA + 1]).then_inc(slots_made, 1)

        def dve_x_t(dve, r, s):
            dve.wait_ge(rows_turned[s], r + 1)
            unless_first(dve, gate_up_made[s], r)
            for h in range(2):
                nc.vector.tensor_copy(x_t[:, s, 4 * h:4 * h + 4, :], four(TURN_BANKS[h])).then_inc(x_t_made[s], 1)

        def dve_hidden(dve, r, s):
            dve.wait_ge(silu_made[s], r + 1)
            unless_first(dve, hidden_turned[s], r)
            nc.vector.tensor_tensor(hidden[:, s, :], silu5[:, s, :], GATE_UP_BANKS[s][:, EF:2 * EF], ALU.mult).then_inc(hidden_made[s], 1)

        def dve_y(dve, r, s):
            dve.wait_ge(y_made[s], r + 1)
            unless_first(dve, y_stored[s], 16 * r)
            nc.vector.tensor_copy(y_rows[:, s, 0:512], Y_BANKS[0][:, :]).then_inc(y_left[s], 1)

        def dve_step(dve, r, s, last=False):
            dve_hidden(dve, r, s)
            if not last:
                dve_x_t(dve, r + 1, s)
            dve_y(dve, r, s)

        def dve_phase5(dve, steps):
            dve_route(dve, steps)
            dve_x_t(dve, 0, 0)
            dve_x_t(dve, 0, 1)
            dve_step(dve, 0, 0)
            dve_step(dve, 0, 1)
            used = later_tiles_used(dve)
            with dve.Fori(1, FIRST_PAIRS - 1) as r:
                dve_step(dve, r, 0)
                dve_step(dve, r, 1)
            dve_step(dve, FIRST_PAIRS - 1, 0, last=True)
            dve_step(dve, FIRST_PAIRS - 1, 1, last=True)
            with dve.Fori(FIRST_PAIRS, PAIRS) as r:
                for s in range(2):
                    with dve.If(used > 2 * r + (s - NE)):
                        dve_x_t(dve, r, s)
                        dve_step(dve, r, s, last=True)
            with dve.If(used > EXTRA - 1):
                dve_x_t(dve, PAIRS, 0)
                dve_step(dve, PAIRS, 0, last=True)
            in_turn(dve_sum(dve), later(2, dve_final(dve, steps)))

        def dve_sum(dve):
            for t in range(NT):
                dve.wait_ge(y_gathered[t], 16 * TOPK)
                for k in range(TOPK):
                    if k:
                        dve.wait_ge(y_sums, 2 * t + 1)
                    nc.vector.scalar_tensor_tensor(out=x[:, t, :], in0=y_pair[:, t, k, :], scalar=weight[:, k, t:t + 1], in1=x[:, t, :],
                                                   op0=ALU.mult, op1=ALU.add).then_inc(y_sums, 1)
                yield

        def dve_final(dve, steps):
            g = gain(dve, "norm_final_g_2")
            for t in range(NT):
                dve.wait_ge(final_root, t + 1)
                steps.link(nc.vector.reciprocal(sums5[:, 8 + t:9 + t], sums5[:, 4 + t:5 + t]))
                nc.vector.scalar_tensor_tensor(out=out_rows[:, t, :], in0=x[:, t, :], scalar=sums5[:, 8 + t:9 + t], in1=g,
                                               op0=ALU.mult, op1=ALU.mult).then_inc(final_rows, 1)
                yield

        def pool_tile_in(pool, r, s):
            unless_first(pool, rows_turned[s], r)
            i = 2 * r + s
            pool.dma_start(rows[:, s, :], slots_dram[bass.ds(i * P, P), :]).then_inc(rows_in[s], 16)

        def pool_tile_out(pool, r, s):
            pool.wait_ge(y_left[s], r + 1)
            pool.wait_ge(y_right[s], r + 1)
            i = 2 * r + s
            pool.dma_start(y_dram[bass.ds(i * P, P), :], y_rows[:, s, :]).then_inc(y_stored[s], 16)

        def pool_phase5(pool, steps):
            pool.wait_ge(slots_zeroed, 32)
            pool.wait_ge(slots_made, 1)
            for t in range(NT):
                for k in range(TOPK):
                    pool.indirect_dma_start(slots_dram, bass.IndirectOffsetOnAxis(ap=slot[:, k, t:t + 1], axis=0),
                                            hn[:, t, :], None).then_inc(rows_placed, 16)
            pool.wait_ge(rows_placed, 16 * NT * TOPK)
            for r in range(2):
                pool_tile_in(pool, r, 0)
                pool_tile_in(pool, r, 1)
            used = later_tiles_used(pool)
            with pool.Fori(2, FIRST_PAIRS) as r:
                for s in range(2):
                    pool_tile_in(pool, r, s)
                    pool_tile_out(pool, r - 2, s)
            pool_tile_in(pool, FIRST_PAIRS, 0)
            for r in (FIRST_PAIRS - 2, FIRST_PAIRS - 1):
                pool_tile_out(pool, r, 0)
                pool_tile_out(pool, r, 1)
            with pool.Fori(FIRST_PAIRS, PAIRS) as r:
                for s in range(2):
                    with pool.If(used > 2 * r + (s - NE)):
                        pool_tile_in(pool, r + s, 1 - s)
                        pool_tile_out(pool, r, s)
                        pool.wait_ge(y_stored[s], 16 * (r + 1))
            with pool.If(used > EXTRA - 1):
                pool_tile_out(pool, PAIRS, 0)
                pool.wait_ge(y_stored[0], 16 * (PAIRS + 1))
            pool.wait_ge(y_stored[0], 16 * FIRST_PAIRS)
            pool.wait_ge(y_stored[1], 16 * FIRST_PAIRS)
            for t in range(NT):
                for k in range(TOPK):
                    pool.indirect_dma_start(y_pair[:, t, k, :], None, y_dram,
                                            bass.IndirectOffsetOnAxis(ap=slot[:, k, t:t + 1], axis=0)).then_inc(y_gathered[t], 16)

        def sp_expert(sp, r, s, e):
            view3 = lambda a: a[0, bass.ds(e, 1), :, :].rearrange("o (k p) n -> p (o k) n", p=P)
            unless_first(sp, gate_up_made[s], r)
            sp.dma_start(gate_up[:, s, :, 0:EF], view3(w["expert_w_gate_2"])).then_inc(gate_up_in[s], 16)
            sp.dma_start(gate_up[:, s, :, EF:2 * EF], view3(w["expert_w_up_2"])).then_inc(gate_up_in[s], 16)
            unless_first(sp, y_made[s], r)
            sp.dma_start(down_w[:, s, :, :], view3(w["expert_w_down_2"])).then_inc(down_in[s], 16)

        def sp_phase5(sp):
            sp.wait_ge(rows_normed, turns["xa"]["tile"] + NT)
            load_gain(sp, "norm_moe_g_2")
            load_gain(sp, "norm_final_g_2")
            sp.wait_ge(cross_in, 6)
            k3 = lambda a: a[0].rearrange("(k p) n -> p k n", p=P)
            sp.dma_start(router_w[:, :, 0:NG], k3(w["router_group_w_2"])).then_inc(router_in, 16)
            sp.dma_start(router_w[:, :, NG:NG + NE], k3(w["router_expert_w_2"])).then_inc(router_in, 16)
            sp.dma_start(router_b[:, 0:NG], w["router_group_b_2"][0:1, :].broadcast_to([P, NG])).then_inc(router_in, 16)
            sp.dma_start(router_b[:, NG:NG + NE], w["router_expert_b_2"][0:1, :].broadcast_to([P, NE])).then_inc(router_in, 16)
            sp.wait_ge(x_added, 6 * NT)
            for s in range(2):
                sp_expert(sp, 0, s, s)
            with sp.Fori(1, FIRST_PAIRS) as r:
                for s in range(2):
                    sp_expert(sp, r, s, 2 * r + s)
            used = later_tiles_used(sp)
            with sp.Fori(FIRST_PAIRS, PAIRS) as r:
                for s in range(2):
                    at = 2 * r + (s - NE)
                    with sp.If(used > at):
                        sp_expert(sp, r, s, sp.value_load(later_expert[0:1, bass.ds(at, 1)], min_val=0, max_val=NE - 1))
            with sp.If(used > EXTRA - 1):
                sp_expert(sp, PAIRS, 0, sp.value_load(later_expert[0:1, EXTRA - 1:EXTRA], min_val=0, max_val=NE - 1))
            out_view = out[0].rearrange("(t p) d -> p t d", p=P)
            for t in range(NT):
                sp.wait_ge(final_rows, t + 1)
                sp.dma_start(out_view[:, t, :], out_rows[:, t, :]).then_inc(out_stored, 16)
            sp.wait_ge(out_stored, 16 * NT)

        block = ctx.enter_context(nc.Block())

        @block.sync
        def _(sp):
            sp_phase1(sp)
            sp_phase2(sp)
            sp_phase3(sp)
            sp_phase4(sp)
            sp_phase5(sp)

        @block.tensor
        def _(pe):
            pe_phase1(pe)
            pe_phase2(pe)
            pe_phase3(pe)
            pe_phase4(pe)
            pe_phase5(pe)

        @block.scalar
        def _(act):
            act_phase1(act)
            act_phase2(act)
            act_phase3(act)
            act_phase4(act)
            act_phase5(act)

        @block.vector
        def _(dve):
            steps = Steps(dve, dve_steps)
            dve_phase1(dve, steps)
            dve_phase2(dve, steps)
            dve_phase3(dve, steps)
            dve_phase4(dve, steps)
            dve_phase5(dve, steps)

        @block.gpsimd
        def _(pool):
            steps = Steps(pool, pool_steps)
            pool_phase1(pool, steps)
            pool_phase2(pool, steps)
            pool_phase3(pool, steps)
            pool_phase4(pool, steps)
            pool_phase5(pool, steps)


_BIG = ["x", "w_in_first", "decay_up", "aaa_up", "gate_up", "w_out", "w_ffn_up", "w_ffn_down", "norm_mix_post",
        "norm_ffn_post", "mem_2", "w_in_2", "conv_pw_w_2", "attn_branch_w_2", "w_out_2", "xa_wq_2", "xa_wk_2",
        "xa_wv_2", "xa_wo_2", "router_group_w_2", "router_group_b_2", "router_expert_w_2", "router_expert_b_2",
        "expert_w_gate_2", "expert_w_up_2", "expert_w_down_2", "norm_final_g_2", "norm_mix_pre", "norm_ffn_pre",
        "attn_out_gain", "norm_mix_g_2", "norm_xa_g_2", "norm_mem_g_2", "norm_moe_g_2"]


def _packed_cols(inputs):
    v = {name: np.asarray(inputs[name]).reshape(-1) for name in
         ("decay_w0", "aaa_a0", "k_k", "k_a", "r_k", "gn_w", "gn_b",
          "conv_dw_b_2", "conv_ln_g_2", "conv_ln_b_2",
          "fox_bf_2", "conv_dw_w_2")}
    mu = np.asarray(inputs["mu_shift"]).reshape(-1)
    v["mu_r"], v["mu_k"], v["mu_v"] = mu[0:H], mu[H:2 * H], mu[2 * H:3 * H]
    v["mu_wa"], v["mu_g"] = mu[3 * H:3 * H + 2 * W_LORA], mu[3 * H + 2 * W_LORA:NSHIFT]
    packed = np.zeros((P, NCOLS), np.float32)
    for name, (at, n) in COL_AT.items():
        a = v[name]
        if a.size == n * P:
            packed[:, at:at + n] = a.reshape(n, P).T
        else:
            packed[0:a.size, at] = a
    return packed


def kernel(**inputs):
    import concourse.bacc as _bacc
    from concourse.bass_utils import run_bass_kernel_spmd as _run

    nc = _bacc.Bacc("TRN2", target_bir_lowering=False, num_devices=1)
    arrays = {f"in_{n}_dram": np.ascontiguousarray(inputs[n]) for n in _BIG}
    arrays["in_cols_dram"] = _packed_cols(inputs)
    arrays["in_consts_dram"] = shape_constants()
    aps = {n: nc.dram_tensor(n, a.shape, mybir.dt.from_np(a.dtype), kind="ExternalInput").ap() for n, a in arrays.items()}
    out = nc.dram_tensor("out_0_dram", (1, T, D), F32, kind="ExternalOutput").ap()
    two_blocks(nc, {n: aps[f"in_{n}_dram"] for n in _BIG}, aps["in_cols_dram"], aps["in_consts_dram"], out)
    r = _run(nc, [arrays], core_ids=[0])
    return r.results[0]["out_0_dram"]
```
